# Optimizing a Trainium2 kernel written in Bass

```python
import jax, jax.numpy as jnp
from jax import lax
import numpy as np
import math

D_MODEL = 1024
BATCH = 1
SEQ = 256
DEPTH = 2

N_MIXERS = 2
N_A = (DEPTH + 1) // 2
N_B = DEPTH // 2
D_FF = 2816
LRU_WIDTH = D_MODEL
LRU_HEADS = 16
LRU_HEAD_DIM = LRU_WIDTH // LRU_HEADS
LRU_C = 8.0
CONV_WIDTH = 4
SG_WIDTH = D_MODEL
SG_HEADS = 8
SG_HEAD_DIM = SG_WIDTH // SG_HEADS
CHUNK = 128
NORM_EPS = 1e-6


def rms_norm(x, g):
    xf = x.astype(jnp.float32)
    y = xf * lax.rsqrt(jnp.mean(xf * xf, axis=-1, keepdims=True) + NORM_EPS)
    return (y * g.astype(jnp.float32)).astype(x.dtype)

def swiglu(x, w_in, w_out):
    g, u = jnp.split(x @ w_in, 2, axis=-1)
    return (jax.nn.silu(g) * u) @ w_out

def causal_depthwise_conv(x, w, b):
    k_width = w.shape[0]
    s = x.shape[1]
    xp = jnp.pad(x, ((0, 0), (k_width - 1, 0), (0, 0)))
    out = b + xp[:, 0:s] * w[0]
    for k in range(1, k_width):
        out = out + xp[:, k:k + s] * w[k]
    return out

def block_diag_linear(x, w, b):
    bsz, s, _ = x.shape
    h, dh, _ = w.shape
    xh = x.reshape(bsz, s, h, dh)
    return (jnp.einsum('bshi,hij->bshj', xh, w) + b).reshape(bsz, s, h * dh)

def rg_lru(x, w_a, b_a, w_x, b_x, lam):
    f32 = jnp.float32
    xf = x.astype(f32)
    gate_a = jax.nn.sigmoid(block_diag_linear(xf, w_a.astype(f32), b_a.astype(f32)))
    gate_x = jax.nn.sigmoid(block_diag_linear(xf, w_x.astype(f32), b_x.astype(f32)))
    log_a = -LRU_C * gate_a * jax.nn.softplus(-lam.astype(f32))
    a = jnp.exp(log_a)
    mult = jnp.sqrt(-jnp.expm1(2.0 * log_a))
    bx = xf * gate_x * mult

    def combine(left, right):
        a_l, b_l = left
        a_r, b_r = right
        return a_l * a_r, a_r * b_l + b_r

    _, h = lax.associative_scan(combine, (a, bx), axis=1)
    return h.astype(x.dtype)

def recurrent_mixer(x, w_in, conv_w, conv_b, gate_a_w, gate_a_b, gate_x_w, gate_x_b, lam, w_out):
    y, r = jnp.split(x @ w_in, 2, axis=-1)
    y = jax.nn.gelu(y)
    r = causal_depthwise_conv(r, conv_w, conv_b)
    h = rg_lru(r, gate_a_w, gate_a_b, gate_x_w, gate_x_b, lam)
    return (y * h) @ w_out

def spatial_gating_mixer(x, w_in, v_norm, w_s, b_s, w_out):
    bsz, s, _ = x.shape
    u, v = jnp.split(jax.nn.gelu(x @ w_in), 2, axis=-1)
    v = rms_norm(v, v_norm)
    h, p, _ = w_s.shape
    c = v.shape[-1] // h
    vc = v.reshape(bsz, s // p, p, h, c)
    causal = jnp.tril(jnp.ones((p, p), dtype=bool))
    ws = jnp.where(causal[None], w_s, jnp.zeros_like(w_s))
    sg = jnp.einsum('hpq,bnqhc->bnphc', ws, vc) + b_s.T[:, :, None]
    sg = sg.reshape(bsz, s, h * c)
    return (u * sg) @ w_out

def first_inputs(seed: int = 0) -> dict:
    key = jax.random.key(seed)
    ks = jax.random.split(key, 32)
    f32 = jnp.float32

    def nrm(k, shape, fan_in):
        return jax.random.normal(k, shape, f32) * (fan_in ** -0.5)

    def gain(k, shape):
        return 1.0 + 0.05 * jax.random.normal(k, shape, f32)

    def small(k, shape):
        return 0.01 * jax.random.normal(k, shape, f32)

    x = jax.random.normal(ks[0], (BATCH, SEQ, D_MODEL), f32)

    a0 = jax.random.uniform(ks[14], (N_A, LRU_WIDTH), f32, 0.9, 0.999)
    p0 = a0 ** (1.0 / LRU_C)
    rec_lambda = jnp.log(p0) - jnp.log1p(-p0)

    return {
        "x": x,
        "ffn1_norm": gain(ks[1], (DEPTH, D_MODEL)),
        "ffn1_w_in": nrm(ks[2], (DEPTH, D_MODEL, 2 * D_FF), D_MODEL),
        "ffn1_w_out": nrm(ks[3], (DEPTH, D_FF, D_MODEL), D_FF),
        "mix_norm": gain(ks[4], (DEPTH, D_MODEL)),
        "ffn2_norm": gain(ks[5], (DEPTH, D_MODEL)),
        "ffn2_w_in": nrm(ks[6], (DEPTH, D_MODEL, 2 * D_FF), D_MODEL),
        "ffn2_w_out": nrm(ks[7], (DEPTH, D_FF, D_MODEL), D_FF),
        "rec_w_in": nrm(ks[8], (N_A, D_MODEL, 2 * LRU_WIDTH), D_MODEL),
        "rec_conv_w": nrm(ks[9], (N_A, CONV_WIDTH, LRU_WIDTH), CONV_WIDTH),
        "rec_conv_b": small(ks[10], (N_A, LRU_WIDTH)),
        "rec_gate_a_w": nrm(ks[11], (N_A, LRU_HEADS, LRU_HEAD_DIM, LRU_HEAD_DIM), LRU_HEAD_DIM),
        "rec_gate_a_b": small(ks[12], (N_A, LRU_HEADS, LRU_HEAD_DIM)),
        "rec_gate_x_w": nrm(ks[13], (N_A, LRU_HEADS, LRU_HEAD_DIM, LRU_HEAD_DIM), LRU_HEAD_DIM),
        "rec_gate_x_b": small(ks[15], (N_A, LRU_HEADS, LRU_HEAD_DIM)),
        "rec_lambda": rec_lambda,
        "rec_w_out": nrm(ks[16], (N_A, LRU_WIDTH, D_MODEL), LRU_WIDTH),
        "sg_w_in": nrm(ks[17], (N_B, D_MODEL, 2 * SG_WIDTH), D_MODEL),
        "sg_v_norm": gain(ks[18], (N_B, SG_WIDTH)),
        "sg_w_s": nrm(ks[19], (N_B, SG_HEADS, CHUNK, CHUNK), CHUNK),
        "sg_b_s": 1.0 + 0.1 * jax.random.normal(ks[20], (N_B, SG_HEADS, CHUNK), f32),
        "sg_w_out": nrm(ks[21], (N_B, SG_WIDTH, D_MODEL), SG_WIDTH),
        "final_norm": gain(ks[22], (D_MODEL,)),
    }

def first_block(x, ffn1_norm, ffn1_w_in, ffn1_w_out, mix_norm, ffn2_norm, ffn2_w_in, ffn2_w_out,
              rec_w_in, rec_conv_w, rec_conv_b, rec_gate_a_w, rec_gate_a_b, rec_gate_x_w, rec_gate_x_b,
              rec_lambda, rec_w_out, sg_w_in, sg_v_norm, sg_w_s, sg_b_s, sg_w_out, final_norm):
    h = x
    for i in range(DEPTH):
        h = h + 0.5 * swiglu(rms_norm(h, ffn1_norm[i]), ffn1_w_in[i], ffn1_w_out[i])
        hn = rms_norm(h, mix_norm[i])
        j = i // N_MIXERS
        if i % N_MIXERS == 0:
            m = recurrent_mixer(hn, rec_w_in[j], rec_conv_w[j], rec_conv_b[j], rec_gate_a_w[j], rec_gate_a_b[j],
                                rec_gate_x_w[j], rec_gate_x_b[j], rec_lambda[j], rec_w_out[j])
        else:
            m = spatial_gating_mixer(hn, sg_w_in[j], sg_v_norm[j], sg_w_s[j], sg_b_s[j], sg_w_out[j])
        h = h + m
        h = h + 0.5 * swiglu(rms_norm(h, ffn2_norm[i]), ffn2_w_in[i], ffn2_w_out[i])
    return rms_norm(h, final_norm)


N_META = 16
ATT_HEAD_DIM = 64
ATT_HEADS = D_MODEL // ATT_HEAD_DIM
ATT_KV_HEADS = ATT_HEADS // 8
ATT_WIDTH = ATT_HEADS * ATT_HEAD_DIM
ATT_KV_WIDTH = ATT_KV_HEADS * ATT_HEAD_DIM
WINDOW = 128
ATT_BLOCK = 128
ROT_DIM = ATT_HEAD_DIM // 4
ROPE_THETA = 500000.0
M_HEADS = 4
M_V_DIM = D_MODEL // M_HEADS
M_QK_DIM = M_V_DIM // 2
M_WIDTH = M_HEADS * M_V_DIM
M_QK_WIDTH = M_HEADS * M_QK_DIM
CHUNK_2 = 64
CONV_K = 4
MIX_WIDTH = ATT_WIDTH + M_WIDTH
SPLIT_SIZES = (ATT_WIDTH, ATT_KV_WIDTH, ATT_KV_WIDTH, ATT_WIDTH,
               M_QK_WIDTH, M_QK_WIDTH, M_WIDTH, M_HEADS, M_HEADS, M_WIDTH, M_WIDTH)
IN_WIDTH = sum(SPLIT_SIZES)
EPS = 1e-6
NEG = -1e30


def split_points():
    pts, acc = [], 0
    for s in SPLIT_SIZES[:-1]:
        acc += s
        pts.append(acc)
    return pts

def rms_norm_2(x, g):
    xf = x.astype(jnp.float32)
    y = xf * lax.rsqrt(jnp.mean(xf * xf, axis=-1, keepdims=True) + EPS)
    return (y * g.astype(jnp.float32)).astype(x.dtype)

def rope_tables(length):
    pos = jnp.arange(length, dtype=jnp.float32)
    inv_freq = ROPE_THETA ** (-jnp.arange(0, ROT_DIM, 2, dtype=jnp.float32) / ROT_DIM)
    ang = pos[:, None] * inv_freq[None, :]
    return jnp.cos(ang), jnp.sin(ang)

def apply_partial_rope(x, cos, sin):
    half = ROT_DIM // 2
    x1, x2, rest = x[..., :half], x[..., half:ROT_DIM], x[..., ROT_DIM:]
    c = cos[None, :, None, :]
    s = sin[None, :, None, :]
    out = jnp.concatenate([x1 * c - x2 * s, x2 * c + x1 * s, rest.astype(jnp.float32)], axis=-1)
    return out.astype(x.dtype)

def sliding_window_sink_attention(q, k, v, sink):
    B, L, H, Dh = q.shape
    KV = k.shape[2]
    G = H // KV
    pad = ATT_BLOCK - N_META
    Lp = L + pad
    nb = Lp // ATT_BLOCK
    padf = lambda a: jnp.pad(a, ((0, 0), (pad, 0), (0, 0), (0, 0)))
    qb = padf(q).reshape(B, nb, ATT_BLOCK, KV, G, Dh)

    def band_keys(a):
        ab = padf(a).reshape(B, nb, ATT_BLOCK, KV, Dh)
        prev = jnp.concatenate([jnp.zeros_like(ab[:, :1]), ab[:, :-1]], axis=1)
        meta = jnp.broadcast_to(a[:, None, :N_META], (B, nb, N_META, KV, Dh))
        return jnp.concatenate([meta, prev, ab], axis=2)

    kb = band_keys(k)
    vb = band_keys(v)

    blk = jnp.arange(nb)
    qpos = blk[:, None] * ATT_BLOCK + jnp.arange(ATT_BLOCK)[None, :] - pad
    kpos = blk[:, None] * ATT_BLOCK - ATT_BLOCK + jnp.arange(2 * ATT_BLOCK)[None, :] - pad
    mpos = jnp.arange(N_META)
    valid_meta = mpos[None, None, :] <= qpos[:, :, None]
    dist = qpos[:, :, None] - kpos[:, None, :]
    valid_band = (kpos[:, None, :] >= N_META) & (dist >= 0) & (dist < WINDOW)
    mask = jnp.concatenate([valid_meta, valid_band], axis=-1)

    scale = 1.0 / math.sqrt(Dh)
    scores = jnp.einsum('bnqkgd,bnskd->bnkgqs', qb, kb).astype(jnp.float32) * scale
    scores = jnp.where(mask[None, :, None, None], scores, NEG)
    sink_b = sink.astype(jnp.float32).reshape(KV, G)[None, None, :, :, None, None]
    m = jnp.maximum(scores.max(axis=-1, keepdims=True), sink_b)
    e = jnp.exp(scores - m)
    probs = e / (e.sum(axis=-1, keepdims=True) + jnp.exp(sink_b - m))
    out = jnp.einsum('bnkgqs,bnskd->bnqkgd', probs.astype(vb.dtype), vb)
    return out.reshape(B, Lp, H, Dh)[:, pad:]

def causal_depthwise_conv_2(x, w, b):
    C = x.shape[-1]
    y = lax.conv_general_dilated(x, w[:, None, :].astype(x.dtype), (1,), [(CONV_K - 1, 0)],
                                 dimension_numbers=('NWC', 'WIO', 'NWC'), feature_group_count=C)
    return y + b.astype(x.dtype)

def mlstm_chunkwise(q, k, v, log_i, log_f):
    B, L, NH, DQK = q.shape
    DV = v.shape[-1]
    pad = CHUNK_2 - N_META
    Lp = L + pad
    NC = Lp // CHUNK_2
    f32 = jnp.float32

    def prep(a):
        a = jnp.pad(a.astype(f32), ((0, 0), (pad, 0), (0, 0), (0, 0)))
        return a.reshape(B, NC, CHUNK_2, NH, a.shape[-1]).transpose(0, 3, 1, 2, 4)

    q, k, v = prep(q), prep(k), prep(v)
    log_i = jnp.pad(log_i, ((0, 0), (pad, 0), (0, 0)), constant_values=NEG)
    log_f = jnp.pad(log_f, ((0, 0), (pad, 0), (0, 0)), constant_values=0.0)
    log_i = log_i.reshape(B, NC, CHUNK_2, NH).transpose(0, 3, 1, 2)
    log_f = log_f.reshape(B, NC, CHUNK_2, NH).transpose(0, 3, 1, 2)

    b = jnp.cumsum(log_f, axis=-1)
    bT = b[..., -1]
    causal = jnp.tril(jnp.ones((CHUNK_2, CHUNK_2), dtype=bool))
    D = jnp.where(causal, b[..., :, None] - b[..., None, :] + log_i[..., None, :], NEG)

    g = bT[..., None] - b + log_i
    mg = g.max(axis=-1)
    wg = jnp.exp(g - mg[..., None])
    kv_chunk = jnp.einsum('bhcsk,bhcsv->bhckv', wg[..., None] * k, v)
    n_chunk = jnp.einsum('bhcs,bhcsk->bhck', wg, k)

    def step(carry, inp):
        C, n, m = carry
        kv_c, n_c, bT_c, mg_c = inp
        m_new = jnp.maximum(bT_c + m, mg_c)
        a = jnp.exp(bT_c + m - m_new)
        w = jnp.exp(mg_c - m_new)
        C_new = a[..., None, None] * C + w[..., None, None] * kv_c
        n_new = a[..., None] * n + w[..., None] * n_c
        return (C_new, n_new, m_new), (C, n, m)

    init = (jnp.zeros((B, NH, DQK, DV), f32), jnp.zeros((B, NH, DQK), f32), jnp.zeros((B, NH), f32))
    xs = (jnp.moveaxis(kv_chunk, 2, 0), jnp.moveaxis(n_chunk, 2, 0),
          jnp.moveaxis(bT, 2, 0), jnp.moveaxis(mg, 2, 0))
    _, (C_in, n_in, m_in) = lax.scan(step, init, xs)
    C_in = jnp.moveaxis(C_in, 0, 2)
    n_in = jnp.moveaxis(n_in, 0, 2)
    m_in = jnp.moveaxis(m_in, 0, 2)

    a_t = b + m_in[..., None]
    m_t = jnp.maximum(a_t, D.max(axis=-1))
    S = jnp.einsum('bhctd,bhcsd->bhcts', q, k) * jnp.exp(D - m_t[..., None])
    inter = jnp.exp(a_t - m_t)
    num = inter[..., None] * jnp.einsum('bhctk,bhckv->bhctv', q, C_in) \
        + jnp.einsum('bhcts,bhcsv->bhctv', S, v)
    den = inter * jnp.einsum('bhctk,bhck->bhct', q, n_in) + S.sum(axis=-1)
    h = num / jnp.maximum(jnp.abs(den), jnp.exp(-m_t))[..., None]
    h = h.transpose(0, 2, 3, 1, 4).reshape(B, Lp, NH, DV)
    return h[:, pad:]

def hybrid_layer(x, cos, sin, norm_g, w_in, q_norm_g, k_norm_g, sink,
                 conv_w, conv_b, b_i, b_f, out_norm_g, w_out):
    B, L, _ = x.shape
    h = rms_norm_2(x, norm_g)
    z = h @ w_in.astype(x.dtype)
    aq, ak, av, ag, mq, mk, mv, mi, mf, mo, mgate = jnp.split(z, split_points(), axis=-1)

    q = rms_norm_2(aq.reshape(B, L, ATT_HEADS, ATT_HEAD_DIM), q_norm_g)
    k = rms_norm_2(ak.reshape(B, L, ATT_KV_HEADS, ATT_HEAD_DIM), k_norm_g)
    q = apply_partial_rope(q, cos, sin)
    k = apply_partial_rope(k, cos, sin)
    v = av.reshape(B, L, ATT_KV_HEADS, ATT_HEAD_DIM)
    ya = sliding_window_sink_attention(q, k, v, sink).reshape(B, L, ATT_WIDTH)
    ya = ya * jax.nn.silu(ag)

    qk = jax.nn.silu(causal_depthwise_conv_2(jnp.concatenate([mq, mk], axis=-1), conv_w, conv_b))
    mq, mk = jnp.split(qk, [M_QK_WIDTH], axis=-1)
    mq = mq.reshape(B, L, M_HEADS, M_QK_DIM)
    mk = mk.reshape(B, L, M_HEADS, M_QK_DIM) * (M_QK_DIM ** -0.5)
    mv = mv.reshape(B, L, M_HEADS, M_V_DIM)
    log_i = (mi + b_i).astype(jnp.float32)
    log_f = jax.nn.log_sigmoid((mf + b_f).astype(jnp.float32))
    hm = mlstm_chunkwise(mq, mk, mv, log_i, log_f)
    hm = rms_norm_2(hm, out_norm_g.reshape(M_HEADS, M_V_DIM)).reshape(B, L, M_WIDTH).astype(x.dtype)
    ym = hm * jax.nn.sigmoid(mo) * jax.nn.silu(mgate)

    y = jnp.concatenate([ya, ym], axis=-1) @ w_out.astype(x.dtype)
    return x + y

def second_inputs(seed: int = 0) -> dict:
    key = jax.random.key(seed)
    ks = jax.random.split(key, 13)
    f32 = jnp.float32
    n = lambda k, shape, s: jax.random.normal(k, shape, f32) * s
    return {
        "x": n(ks[0], (BATCH, SEQ, D_MODEL), 1.0),
        "meta": n(ks[1], (N_META, D_MODEL), 1.0),
        "norm_g": 1.0 + n(ks[2], (DEPTH, D_MODEL), 0.02),
        "w_in": n(ks[3], (DEPTH, D_MODEL, IN_WIDTH), D_MODEL ** -0.5),
        "attn_q_norm_g": 1.0 + n(ks[4], (DEPTH, ATT_HEAD_DIM), 0.02),
        "attn_k_norm_g": 1.0 + n(ks[5], (DEPTH, ATT_HEAD_DIM), 0.02),
        "attn_sink": n(ks[6], (DEPTH, ATT_HEADS), 0.5),
        "mlstm_conv_w": n(ks[7], (DEPTH, CONV_K, 2 * M_QK_WIDTH), CONV_K ** -0.5),
        "mlstm_conv_b": n(ks[8], (DEPTH, 2 * M_QK_WIDTH), 0.02),
        "mlstm_b_i": n(ks[9], (DEPTH, M_HEADS), 0.1),
        "mlstm_b_f": jnp.linspace(3.0, 6.0, M_HEADS, dtype=f32)[None, :] + n(ks[10], (DEPTH, M_HEADS), 0.1),
        "mlstm_out_norm_g": 1.0 + n(ks[11], (DEPTH, M_WIDTH), 0.02),
        "w_out": n(ks[12], (DEPTH, MIX_WIDTH, D_MODEL), 0.5 * MIX_WIDTH ** -0.5),
    }

def second_block(x, meta, norm_g, w_in, attn_q_norm_g, attn_k_norm_g, attn_sink,
              mlstm_conv_w, mlstm_conv_b, mlstm_b_i, mlstm_b_f, mlstm_out_norm_g, w_out):
    B = x.shape[0]
    h = jnp.concatenate([jnp.broadcast_to(meta.astype(x.dtype)[None], (B, N_META, x.shape[-1])), x], axis=1)
    L = h.shape[1]
    cos, sin = rope_tables(L)
    for l in range(DEPTH):
        h = hybrid_layer(h, cos, sin, norm_g[l], w_in[l], attn_q_norm_g[l], attn_k_norm_g[l],
                         attn_sink[l], mlstm_conv_w[l], mlstm_conv_b[l], mlstm_b_i[l],
                         mlstm_b_f[l], mlstm_out_norm_g[l], w_out[l])
    return h[:, N_META:]


def setup_inputs(seed=0):
    out = dict(first_inputs(seed))
    for name, value in second_inputs(seed + 1).items():
        if name != "x":
            out[name + "_2"] = value
    return out


def reference(
    x, ffn1_norm, ffn1_w_in, ffn1_w_out, mix_norm, ffn2_norm, ffn2_w_in, ffn2_w_out, rec_w_in,
    rec_conv_w, rec_conv_b, rec_gate_a_w, rec_gate_a_b, rec_gate_x_w, rec_gate_x_b, rec_lambda,
    rec_w_out, sg_w_in, sg_v_norm, sg_w_s, sg_b_s, sg_w_out, final_norm, meta_2, norm_g_2,
    w_in_2, attn_q_norm_g_2, attn_k_norm_g_2, attn_sink_2, mlstm_conv_w_2, mlstm_conv_b_2,
    mlstm_b_i_2, mlstm_b_f_2, mlstm_out_norm_g_2, w_out_2,
):
    x = first_block(
        x, ffn1_norm, ffn1_w_in, ffn1_w_out, mix_norm, ffn2_norm, ffn2_w_in, ffn2_w_out,
        rec_w_in, rec_conv_w, rec_conv_b, rec_gate_a_w, rec_gate_a_b, rec_gate_x_w,
        rec_gate_x_b, rec_lambda, rec_w_out, sg_w_in, sg_v_norm, sg_w_s, sg_b_s, sg_w_out,
        final_norm,
    )
    return second_block(
        x, meta_2, norm_g_2, w_in_2, attn_q_norm_g_2, attn_k_norm_g_2, attn_sink_2,
        mlstm_conv_w_2, mlstm_conv_b_2, mlstm_b_i_2, mlstm_b_f_2, mlstm_out_norm_g_2, w_out_2,
    )


_drawn_inputs = setup_inputs


def setup_inputs(seed=0):
    import zlib

    import numpy as np

    out = dict(_drawn_inputs(seed))
    spreads = {}
    factors = {'rec_gate_a_b': 8.0,
     'rec_gate_x_b': 8.0,
     'sg_v_norm': 3.509,
     'norm_g_2': 8.0,
     'attn_q_norm_g_2': 8.0,
     'attn_k_norm_g_2': 8.0,
     'attn_sink_2': 8.0,
     'mlstm_conv_b_2': 46.096,
     'mlstm_b_i_2': 64.0,
     'mlstm_out_norm_g_2': 8.0}
    for name, (base, spread) in spreads.items():
        noise = np.random.default_rng([zlib.crc32(name.encode()), seed]).standard_normal(out[name].shape)
        drawn = base * np.exp(spread * noise) if base else spread * noise
        out[name] = __import__('jax').numpy.asarray(drawn.astype(out[name].dtype))
    for name, factor in factors.items():
        out[name] = (out[name] * factor).astype(out[name].dtype)
    return out
```

```python
import numpy as np
import concourse.bass as bass
from concourse import mybir
from contextlib import ExitStack

P = 128
D = 1024
NC8 = D // P
SEQ = 256
META = 16
L = META + SEQ
FF = 2816
NF = FF // P
DEPTH = 2
KU = 4
CU = 256
RING = 4
LEAD = 3
EPS = 1e-6
NEG = -1e30
BIG = 1e30
ATT_H, DH, M_H, QK_D = 16, 64, 4, 128
ROT = 16
IN2 = 6408
C_AQ, C_KV, C_AG, C_MQK, C_MV, C_MIF, C_MO, C_MG = 0, 1024, 1280, 2304, 3328, 4352, 4360, 5384
KEYS1 = META + P
WORK_SLOTS = 66
SW = KEYS1 + L
LT = [(0, 128), (128, 256), (256, 272)]
QT = [(0, 16), (16, 144), (144, 272)]
MOFF = [0, L, L + (L - 128)]
MW = MOFF[2] + 16

CONST_W = dict(ident=P, tri=P, amask=SW + META, mmask=MW, rot=P, swap=P, head_mean=P, cos=L, sin=L, sel=4 * P)
CONST_AT = {}
_at = 0
for _n, _w in CONST_W.items():
    CONST_AT[_n] = _at
    _at += _w
CONST_ALL = _at


def constants():
    c = {n: np.zeros((P, w), np.float32) for n, w in CONST_W.items()}
    i = np.arange(P)
    c["ident"][i, i] = 1
    c["tri"][:] = i[:, None] <= i[None, :]

    def hidden(q, k):
        return ~((k <= q) & ((k < META) | (q - k < P)))

    c["amask"][:, :KEYS1] = NEG * hidden(META + i[:, None], np.arange(KEYS1)[None])
    c["amask"][:, KEYS1:SW] = NEG * hidden(META + P + i[:, None], np.arange(L)[None])
    c["amask"][:META, SW:] = NEG * (np.arange(META)[None] > np.arange(META)[:, None])
    for n, (a, b) in enumerate(LT):
        t = np.arange(a, L)
        c["mmask"][:b - a, MOFF[n]:MOFF[n] + L - a] = BIG * (t[None] < np.arange(a, b)[:, None])
    half = ROT // 2
    for h0 in (0, DH):
        for d in range(half):
            c["rot"][h0 + half + d, h0 + d] = -1
            c["rot"][h0 + d, h0 + half + d] = 1
    c["swap"][i, (i + DH) % P] = 1
    c["head_mean"][:] = (i[:, None] // DH == i[None, :] // DH) / DH
    inv = (500000.0 ** (-np.arange(0, ROT, 2, dtype=np.float32) / ROT)).astype(np.float32)
    ang = np.arange(L, dtype=np.float32)[None] * inv[:, None]
    c["cos"][:] = 1
    for h0 in (0, DH):
        for k in (0, half):
            c["cos"][h0 + k:h0 + k + half] = np.cos(ang)
            c["sin"][h0 + k:h0 + k + half] = np.sin(ang)
    for h in range(4):
        c["sel"][h, h * P:(h + 1) * P] = 1
    return np.concatenate([c[n] for n in CONST_W], 1)


PAR = {}
for _t, _rows in enumerate([
    [("ffn1_norm", 16), ("ffn2_norm", 16), ("mix_norm", 16), ("final_norm", 8), ("rec_conv_w", 32), ("rec_conv_b", 8),
     ("rec_gate_a_b", 8), ("rec_gate_x_b", 8), ("rec_lambda", 8), ("sg_v_norm", 8)],
    [("norm_g_2", 16), ("mlstm_conv_w_2", 64), ("mlstm_conv_b_2", 16), ("mlstm_out_norm_g_2", 16),
     ("attn_q_norm_g_2", 2), ("attn_k_norm_g_2", 2)],
]):
    _r = 0
    for _n, _k in _rows:
        PAR[_n] = (_t, _r, _k)
        _r += _k


def plan():
    units, pairs, phases = [], [], {}

    def phase(name, src, layer, rows, cols):
        ub, pb = len(units), len(pairs)
        for c0 in cols:
            ks = []
            k = 0
            while k < rows:
                n = min(KU, rows - k) if rows - k != 6 else 3
                ks.append((k, n))
                k += n
            pairs.append([(len(units) + j, k0, n) for j, (k0, n) in enumerate(ks)])
            units.extend((src, layer, k0, n, c0) for k0, n in ks)
        phases[name] = (ub, pb, len(cols))

    wide = range(0, D, CU)
    for l in range(DEPTH):
        for f in (1, 2):
            gate_up = [c + s * FF for c in range(0, FF, CU) for s in (0, 1)]
            phase(f"in{l}{f}", f"ffn{f}_w_in", l, NC8, gate_up)
            phase(f"out{l}{f}", f"ffn{f}_w_out", l, NF, wide)
            if f == 1:
                m = ("rec", "sg")[l]
                phase(m + "_b", m + "_w_in", 0, NC8, [D + c for c in wide])
                phase(m + "_a", m + "_w_in", 0, NC8, wide)
                phase(m + "_out", m + "_w_out", 0, NC8, wide)
    for l in range(DEPTH):
        for n, c in (("kv", [C_KV]), ("mif", [C_MIF]), ("aq", [C_AQ + c for c in wide]),
                     ("mqk", [C_MQK + c for c in wide]), ("mv", [C_MV + c for c in wide]),
                     ("ag", [C_AG + c for c in wide]), ("mo", [C_MO + c for c in wide]),
                     ("mg", [C_MG + c for c in wide])):
            phase(f"{n}{l}", "w_in_2", l, NC8, c)
        phase(f"proj{l}", "w_out_2", l, 2 * NC8, wide)
    return units, pairs, phases


UNITS, PAIRS, PHASES = plan()


def build_stack(nc: bass.Bass, consts, x, ffn1_norm, ffn1_w_in, ffn1_w_out, mix_norm, ffn2_norm, ffn2_w_in, ffn2_w_out,
                rec_w_in, rec_conv_w, rec_conv_b, rec_gate_a_w, rec_gate_a_b, rec_gate_x_w, rec_gate_x_b, rec_lambda,
                rec_w_out, sg_w_in, sg_v_norm, sg_w_s, sg_b_s, sg_w_out, final_norm, meta_2, norm_g_2, w_in_2,
                attn_q_norm_g_2, attn_k_norm_g_2, attn_sink_2, mlstm_conv_w_2, mlstm_conv_b_2, mlstm_b_i_2,
                mlstm_b_f_2, mlstm_out_norm_g_2, w_out_2, out):
    fp32, fp32r = mybir.dt.float32, mybir.dt.float32r
    ALU, ACT = mybir.AluOpType, mybir.ActivationFunctionType
    MUL, ADD, SUB, MAX, MIN = ALU.mult, ALU.add, ALU.subtract, ALU.max, ALU.min
    dram = dict(ffn1_w_in=ffn1_w_in, ffn1_w_out=ffn1_w_out, ffn2_w_in=ffn2_w_in, ffn2_w_out=ffn2_w_out,
                rec_w_in=rec_w_in, rec_w_out=rec_w_out, sg_w_in=sg_w_in, sg_w_out=sg_w_out, w_in_2=w_in_2,
                w_out_2=w_out_2)
    NU = len(UNITS)

    with ExitStack() as ctx:
        def sb(name, shape, dt=fp32):
            return ctx.enter_context(nc.sbuf_tensor(name, shape, dt))

        def sem(name):
            return ctx.enter_context(nc.semaphore(name))

        ctx.enter_context(nc.allow_non_contiguous_dma(reason="gate columns and biases of a few elements"))

        raw = sb("raw", [P, RING, KU, CU])
        w_hi = sb("w_hi", [P, RING, KU, CU], fp32r)
        w_lo = sb("w_lo", [P, RING, KU, CU], fp32r)
        h = sb("h", [P, NC8, L])
        x_hi = sb("x_hi", [P, NC8 * L], fp32r)
        x_lo = sb("x_lo", [P, NC8 * L], fp32r)
        y_hi = sb("y_hi", [P, NF * SEQ], fp32r)
        y_lo = sb("y_lo", [P, NF * SEQ], fp32r)
        con = sb("con", [P, CONST_ALL])
        ones = sb("ones", [P, P])
        par_rows = sb("par_rows", [P, 2, P])
        par = sb("par", [P, 2, P])
        rstd = sb("rstd", [P, L])
        rms = sb("rms", [P, L])
        sumsq = sb("sumsq", [P, L])
        sq = sb("sq", [P, L])
        epsc = sb("epsc", [P, 1])
        work = sb("work", [P, WORK_SLOTS * L])
        pre = sb("pre", [P, 2, L + 3])
        bank = [ctx.enter_context(nc.psum_tensor(f"bank{i}", [P, 512], fp32)) for i in range(8)]

        def cst(name, rows=P):
            return con[0:rows, CONST_AT[name]:CONST_AT[name] + CONST_W[name]]

        ident, tri = cst("ident"), cst("tri")

        def pcol(name, k, rows=P):
            t, r, _ = PAR[name]
            return par[0:rows, t, r + k:r + k + 1]

        at = [0]

        def region(slots, width=L):
            o = at[0]
            at[0] += slots * width
            assert at[0] <= WORK_SLOTS * L, at[0]
            return work[:, o:o + slots * width].rearrange("p (c n) -> p c n", n=width)

        ffn_t, ffn_s, ffn_r, ffn_h = (region(2, SEQ) for _ in range(4))
        mixer_at = at[0]
        rec_y, rec_x, rec_a, rec_g = (region(NC8, SEQ) for _ in range(4))
        rec_p = region(NC8, SEQ + 3)
        blocks_a, blocks_x = region(NC8, P), region(NC8, P)
        decay = region(12, NC8)
        ws_raw, ws_t, bs_all = region(NC8, P), region(NC8, P), region(NC8, P)
        at[0] = mixer_at
        sg_u, sg_v, sg_s = (region(NC8, SEQ) for _ in range(3))
        v_tok = region(2, D)
        sg_r = region(8, 2)
        at[0] = 0
        q = region(NC8)
        k_att, k_swap, v_att = region(1)[:, 0], region(1)[:, 0], region(1)[:, 0]
        qk = region(NC8)
        mv = region(NC8)
        mvt = region(3, D)
        hm = mv
        prob = region(2, SW + META)
        score = region(2, SW + META)
        pt_big = region(2, 384)
        pt_meta = region(2)
        va_t = region(3, P)
        cos_g = region(2)
        rot_g = region(2, P)
        qtmp, qtmp2 = prob[:, :, 0:L], region(2)
        att_s = region(16, 4)
        g_row = region(6)
        g_tok = region(3, 4)
        exp_b = region(1)[:, 0]
        m_b = region(1)[:, 0]
        m_arg, m_pt = score[:, 0, :], score[:, 1, :]
        sinks = sb("sinks", [P, DEPTH * ATT_H])
        gbias = sb("gbias", [4, 2 * DEPTH])
        xrow = work[:, 0:3 * D].rearrange("p (t n) -> p t n", n=D)
        orow = work[:, 0:2 * D].rearrange("p (t n) -> p t n", n=D)

        w_loaded = [sem(f"w_loaded{i}") for i in range(RING)]
        hi_made = sem("hi_made")
        lo_made = sem("lo_made")
        unit_done = sem("unit_done")
        first_done = sem("first_done")
        tile_read = sem("tile_read")
        act_hi = sem("act_hi")
        act_ready = sem("act_ready")
        act_new = sem("act_new")
        silu_done = sem("silu_done")
        gate_scaled = sem("gate_scaled")
        par_loaded, con_loaded, x_loaded, blk_loaded, sg_loaded = (
            sem(n) for n in ("par_loaded", "con_loaded", "x_loaded", "blk_loaded", "sg_loaded"))
        ones_set, zero_set = sem("ones_set"), sem("zero_set")
        par_t, par_ready = sem("par_t"), sem("par_ready")
        xt_done, xt_read = sem("xt_done"), sem("xt_read")
        sq_done, sum_done, rms_done, rstd_ready = (sem(n) for n in ("sq_done", "sum_done", "rms_done", "rstd_ready"))
        pool_ch = sem("pool_ch")
        dch = sem("dch")
        ach = sem("ach")
        final_new = sem("final_new")
        conv_new, gates_mm, gates_sig, ax_new, mult2, mult_new, rec_gelu, rec_bx = (
            sem(n) for n in ("conv_new", "gates_mm", "gates_sig", "ax_new", "mult2", "mult_new", "rec_gelu", "rec_bx"))
        decay_e = sem("decay_e")
        decay_v = sem("decay_v")
        sg_gelu, sg_sum, sg_rms, ws_tr, vt_tr, vt_read, sg_mm, sg_read, ws_read, sg_rs, sg_sqs = (
            sem(n) for n in ("sg_gelu", "sg_sum", "sg_rms", "ws_tr", "vt_tr", "vt_read", "sg_mm", "sg_read", "ws_read",
                             "sg_rs", "sg_sqs"))
        qsq_new, qn_mm, qn_read, qn_sqrt, q_ready = (sem(n) for n in ("qsq_new", "qn_mm", "qn_read", "qn_sqrt", "q_ready"))
        kx_mm, kx_read, k_swapped = sem("kx_mm"), sem("kx_read"), sem("k_swapped")
        s_mm, s_max, s_exp, s_prob, s_tr, s_ptb, s_ptm, s_pv, s_out = (
            sem(n) for n in ("s_mm", "s_max", "s_exp", "s_prob", "s_tr", "s_ptb", "s_ptm", "s_pv", "s_out"))
        g_nx, g_e, g_cm, g_exp, g_tr, g_tok_new = (sem(n) for n in ("g_nx", "g_e", "g_cm", "g_exp", "g_tr", "g_tok_new"))
        conv2_new, qk_new = sem("conv2_new"), sem("qk_new")
        mt_tr, mt_read = sem("mt_tr"), sem("mt_read")
        m_bc, m_mb, m_eb, m_arg_new, m_exp_new, m_pt_new, m_nd, m_hm = (
            sem(n) for n in ("m_bc", "m_mb", "m_eb", "m_arg_new", "m_exp_new", "m_pt_new", "m_nd", "m_hm"))
        n_sq, n_mm, n_sqrt, n_new = (sem(n) for n in ("n_sq", "n_mm", "n_sqrt", "n_new"))
        gate_act = sem("gate_act")
        ot_tr, ot_read, stored = sem("ot_tr"), sem("ot_read"), sem("stored")

        block = ctx.enter_context(nc.Block())

        NORMS = ["in01", "rec_b", "in02", "in11", "sg_b", "in12", "final", "kv0", "kv1"]
        def xview(t, k, n):
            return t[:, k * n:(k + 1) * n]

        SPLITS = {}
        cnt = 0
        for name, k in [("x_in01", 8), ("y_out01", NF), ("x_rec_b", 8), ("y_rec_out", 8), ("x_in02", 8), ("y_out02", NF),
                        ("x_in11", 8), ("y_out11", NF), ("x_sg_b", 8), ("y_sg_out", 8), ("x_in12", 8), ("y_out12", NF),
                        ("x_kv0", 8), ("y_proj0", 16), ("x_kv1", 8), ("y_proj1", 16)]:
            SPLITS[name] = cnt
            cnt += k

        def units_of(pair):
            return PAIRS[pair]

        @block.sync
        def _(sp):
            sp.dma_start(xrow[:, 0:2, :], x[0].rearrange("(t p) d -> p t d", p=P)).then_inc(x_loaded, 16)
            sp.dma_start(xrow[0:META, 2, :], meta_2).then_inc(x_loaded, 16)
            sp.dma_start(con[:, :], consts).then_inc(con_loaded, 16)
            rows = dict(ffn1_norm=ffn1_norm, ffn2_norm=ffn2_norm, mix_norm=mix_norm,
                        rec_conv_b=rec_conv_b, rec_lambda=rec_lambda, sg_v_norm=sg_v_norm, norm_g_2=norm_g_2,
                        mlstm_conv_b_2=mlstm_conv_b_2, mlstm_out_norm_g_2=mlstm_out_norm_g_2)
            srcs = {n: a.rearrange("l (c p) -> (l c) p", p=P) for n, a in rows.items()}
            srcs["final_norm"] = final_norm.rearrange("(c p) -> c p", p=P)
            srcs["rec_conv_w"] = rec_conv_w[0].rearrange("k (c p) -> (k c) p", p=P)
            srcs["mlstm_conv_w_2"] = mlstm_conv_w_2.rearrange("l k (c p) -> (l k c) p", p=P)
            for n, a in (("rec_gate_a_b", rec_gate_a_b), ("rec_gate_x_b", rec_gate_x_b)):
                srcs[n] = a[0].rearrange("(c e) d -> c (e d)", e=2)
            for n, src in srcs.items():
                t, r, k = PAR[n]
                sp.dma_start(par_rows[r:r + k, t, :], src).then_inc(par_loaded, 16)
            for n, src in (("attn_q_norm_g_2", attn_q_norm_g_2), ("attn_k_norm_g_2", attn_k_norm_g_2)):
                t, r, k = PAR[n]
                for e in range(2):
                    sp.dma_start(par_rows[r:r + k, t, e * DH:(e + 1) * DH], src).then_inc(par_loaded, 16)

            def load(U, src, wait):
                n = UNITS[U][3]
                if wait is not None:
                    sp.wait_ge(lo_made, wait)
                sp.dma_start(raw[:, U % RING, 0:n, :], src).then_inc(w_loaded[U % RING], 16)

            def straight(name, first=0):
                ub, pb, npairs = PHASES[name]
                for pr in range(pb + first, pb + npairs):
                    for U, _, n in PAIRS[pr]:
                        src, l, k0, n, c0 = UNITS[U]
                        a = dram[src][l]
                        if name.startswith("mif"):
                            sp.wait_ge(lo_made, U - RING + 1)
                            for g in range(2):
                                sp.dma_start(raw[:, U % RING, 0:n, 32 * g:32 * g + 4],
                                             a[k0 * P:(k0 + n) * P, c0 + 4 * g:c0 + 4 * g + 4].rearrange(
                                                 "(k p) n -> p k n", p=P)).then_inc(w_loaded[U % RING], 16)
                            continue
                        load(U, a[k0 * P:(k0 + n) * P, c0:c0 + CU].rearrange("(k p) n -> p k n", p=P),
                             U - RING + 1 if U >= RING else None)

            def gate_up(name):
                ub, pb, _ = PHASES[name]
                src, l, _, _, _ = UNITS[ub]
                cols = dram[src][l].rearrange("(s k p) (f j n) -> s f j p k n", k=KU, p=P, f=2, n=CU)
                first = 1 if ub == 0 else 0

                def turn(i):
                    for j in range(4):
                        U = ub + j
                        wait = U - RING + 1 + 4 * i
                        load(U, cols[j % 2, j // 2, i], None if isinstance(i, int) and wait <= 0 else wait)

                if first:
                    turn(0)
                with sp.Fori(first, FF // CU) as i:
                    turn(i)

            gate_up_first = True
            sp.wait_ge(zero_set, 1)
            for dst, src in ((blocks_a, rec_gate_a_w), (blocks_x, rec_gate_x_w)):
                for e in range(2):
                    sp.dma_start(dst[e * DH:(e + 1) * DH, :, e * DH:(e + 1) * DH],
                                 src[0].rearrange("(c e) i j -> e i c j", e=2)[e]).then_inc(blk_loaded, 16)
            gate_up("in01")
            sp.dma_start(ws_raw[:, :, :], sg_w_s[0].rearrange("h p q -> p h q")).then_inc(sg_loaded, 16)
            sp.dma_start(bs_all[:, :, :], sg_b_s[0].rearrange("(o h) p -> o h p", o=1).broadcast_to((P, NC8, P))).then_inc(sg_loaded, 16)
            sp.dma_start(sinks[:, :], attn_sink_2.rearrange("(o l) h -> o (l h)", o=1).broadcast_to((P, DEPTH * ATT_H))).then_inc(sg_loaded, 16)
            for g, src in enumerate((mlstm_b_i_2, mlstm_b_f_2)):
                sp.dma_start(gbias[:, g * DEPTH:(g + 1) * DEPTH], src.rearrange("l h -> h l")).then_inc(sg_loaded, 16)
            straight("out01")
            for n in ("rec_b", "rec_a", "rec_out"):
                straight(n)
            gate_up("in02")
            straight("out02")
            gate_up("in11")
            straight("out11")
            for n in ("sg_b", "sg_a", "sg_out"):
                straight(n)
            gate_up("in12")
            straight("out12")
            for l in range(DEPTH):
                for n in ("kv", "mif", "aq", "mqk", "mv", "ag", "mo", "mg", "proj"):
                    straight(f"{n}{l}")
            sp.wait_ge(ot_read, 4)
            sp.dma_start(out[0].rearrange("(t p) d -> p t d", p=P), orow[:, :, :]).then_inc(stored, 16)
            sp.wait_ge(stored, 16)

        MIF_UNITS = {U for l in range(DEPTH) for U, _, _ in PAIRS[PHASES[f"mif{l}"][1]]}
        LANDED = {}
        _c = [0] * RING
        for U in range(NU):
            _c[U % RING] += 32 if U in MIF_UNITS else 16
            LANDED[U] = _c[U % RING]
        LOOPED = {name: PHASES[name] for name in ("in01", "in02", "in11", "in12")}

        @block.tensor
        def _(pe):
            mm = nc.tensor.matmul

            def unit(U, k0, n, pair, npair_off, xs, N, first, last, ready, off, tiles=2):
                hi, lo = xs
                pe.wait_ge(lo_made, U + 1 + off)
                s = U % RING
                for m in range(tiles):
                    T = 2 * pair + m
                    acc = bank[T % 4][:, 0:N]
                    if first and not (isinstance(off, int) and T - 3 + off // 2 <= 0):
                        pe.wait_ge(tile_read, T - 3 + tile_off(off))
                    for j in range(n):
                        k = k0 + j
                        if m == 0 and ready is not None:
                            pe.wait_ge(act_ready, ready + k + 1)
                        wh, wl = (t[:, s, j, m * P:(m + 1) * P] for t in (w_hi, w_lo))
                        xh, xl = xview(hi, k, N), xview(lo, k, N)
                        mm(acc, wh, xh, start=first and j == 0, stop=False)
                        mm(acc, wh, xl, start=False, stop=False)
                        i_ = mm(acc, wl, xh, start=False, stop=last and j == n - 1)
                    if last and m == 0 and tiles == 2:
                        i_.then_inc(first_done, 1)
                i_.then_inc(unit_done, 1)

            def tile_off(off):
                return off // 2 if isinstance(off, int) else off_half[0]

            off_half = [0]

            def pair(pr, xs, N, ready=None, after=None, tiles=2):
                us = units_of(pr)
                for j, (U, k0, n) in enumerate(us):
                    unit(U, k0, n, pr, 0, xs, N, j == 0, j == len(us) - 1, ready, 0, tiles)
                    if after is not None:
                        after(j)

            xs, ys = (x_hi, x_lo), (y_hi, y_lo)

            def norm_sum(n, T0):
                pe.wait_ge(sq_done, n + 1)
                mm(bank[4][:, T0:L], ones[:, :], sumsq[:, T0:L], start=True, stop=True).then_inc(sum_done, 1)

            def in_phase(name, n, ready):
                ub, pb, _ = PHASES[name]
                for p in range(2):
                    pair(pb + p, xs, SEQ, ready=ready if p == 0 else None,
                         after=(lambda j: norm_sum(n, META) if j == 0 else None) if p == 0 else None)
                with pe.Fori(1, FF // CU) as i:
                    off_half[0] = 4 * i
                    for p in range(2):
                        us = units_of(pb + p)
                        for j, (U, k0, nk) in enumerate(us):
                            unit(U, k0, nk, pb + p, 0, xs, SEQ, j == 0, j == 1, None, 4 * i)

            def out_phase(name, ready, N=SEQ, after=None):
                ub, pb, npairs = PHASES[name]
                for p in range(npairs):
                    pair(pb + p, ys, N, ready=ready if p == 0 else None)

            pe.wait_ge(ones_set, 1)
            pe.wait_ge(con_loaded, 16)
            pe.wait_ge(par_loaded, 16 * 18)
            for t in range(2):
                rows = sum(k for (tt, _, k) in PAR.values() if tt == t)
                i_ = nc.tensor.transpose(bank[4][:, t * P:t * P + rows], par_rows[0:rows, t, :], ident[0:rows, 0:rows])
            i_.then_inc(par_t, 1)
            pe.wait_ge(x_loaded, 32)
            for c in range(NC8):
                b = bank[c % 4]
                if c >= 4:
                    pe.wait_ge(xt_read, c - 3)
                nc.tensor.transpose(b[:, 0:META], xrow[0:META, 2, c * P:(c + 1) * P], ident[0:META, 0:META])
                for t in range(2):
                    i_ = nc.tensor.transpose(b[:, META + t * P:META + (t + 1) * P], xrow[:, t, c * P:(c + 1) * P], ident)
                i_.then_inc(xt_done, 1)
            pe.wait_ge(xt_read, NC8)
            pe.wait_ge(par_ready, 1)

            in_phase("in01", 0, SPLITS["x_in01"])
            out_phase("out01", SPLITS["y_out01"])

            ub, pb, _ = PHASES["rec_b"]
            for p in range(4):
                pair(pb + p, xs, SEQ, ready=SPLITS["x_rec_b"] if p == 0 else None,
                     after=(lambda j: norm_sum(1, META) if j == 0 else None) if p == 0 else None)
            ub, pb, _ = PHASES["rec_a"]
            pair(pb, xs, SEQ)
            pe.wait_ge(blk_loaded, 64)
            for c in range(NC8):
                pe.wait_ge(conv_new, c + 1)
                if c >= 4:
                    pe.wait_ge(gates_sig, 2 * (c - 3))
                mm(bank[4 + c % 4][:, 0:SEQ], blocks_a[:, c, :], rec_x[:, c, :], start=True, stop=True)
                mm(bank[4 + c % 4][:, SEQ:2 * SEQ], blocks_x[:, c, :], rec_x[:, c, :], start=True,
                   stop=True).then_inc(gates_mm, 1)
            for p in range(1, 4):
                pair(pb + p, xs, SEQ)
            out_phase("rec_out", SPLITS["y_rec_out"])

            in_phase("in02", 2, SPLITS["x_in02"])
            out_phase("out02", SPLITS["y_out02"])
            in_phase("in11", 3, SPLITS["x_in11"])
            out_phase("out11", SPLITS["y_out11"])

            ub, pb, _ = PHASES["sg_b"]
            for p in range(4):
                pair(pb + p, xs, SEQ, ready=SPLITS["x_sg_b"] if p == 0 else None,
                     after=(lambda j: norm_sum(4, META) if j == 0 else None) if p == 0 else None)
                if p == 0:
                    pe.wait_ge(sg_loaded, 80)
                    for c in range(NC8):
                        i_ = nc.tensor.transpose(bank[5 + c // 4][:, (c % 4) * P:(c % 4 + 1) * P], ws_raw[:, c, :], ident)
                    i_.then_inc(ws_tr, 1)
            ub, pb, _ = PHASES["sg_a"]
            pair(pb, xs, SEQ)
            pe.wait_ge(sg_sqs, 1)
            pe.wait_ge(rms_done, 5)
            for t in range(2):
                i_ = mm(bank[4][:, t:t + 1], sumsq[:, META + t * P:META + (t + 1) * P], ones[:, 0:1], start=True, stop=True)
            i_.then_inc(sg_sum, 1)
            pe.wait_ge(ws_read, 2)
            for g in range(4):
                t, c0 = g // 2, 4 * (g % 2)
                if g == 3:
                    pe.wait_ge(vt_read, 1)
                for c in range(c0, c0 + 4):
                    i_ = nc.tensor.transpose(bank[5 + g % 3][:, (c % 4) * P:(c % 4 + 1) * P],
                                             sg_v[:, c, t * P:(t + 1) * P], ident)
                i_.then_inc(vt_tr, 1)
            pair(pb + 1, xs, SEQ)
            for c in range(NC8):
                if c == 0:
                    pe.wait_ge(vt_read, 4)
                if c >= 4:
                    pe.wait_ge(sg_read, c - 3)
                for t in range(2):
                    i_ = mm(bank[4 + c % 4][:, t * P:(t + 1) * P], v_tok[:, t, c * P:(c + 1) * P], ws_t[:, c, :],
                            start=True, stop=True)
                i_.then_inc(sg_mm, 1)
            for p in range(2, 4):
                pair(pb + p, xs, SEQ)
            out_phase("sg_out", SPLITS["y_sg_out"])

            in_phase("in12", 5, SPLITS["x_in12"])
            out_phase("out12", SPLITS["y_out12"])
            norm_sum(6, META)

            for l in range(DEPTH):
                pair(PHASES[f"kv{l}"][1], xs, L, ready=SPLITS[f"x_kv{l}"],
                     after=lambda j: norm_sum(7 + l, 0) if j == 0 else None)
                pair(PHASES[f"mif{l}"][1], xs, L, tiles=1)
                pb = PHASES[f"aq{l}"][1]
                for p in range(4):
                    pair(pb + p, xs, L)

                for c in range(9):
                    n = 9 * l + c
                    pe.wait_ge(qsq_new, n + 1)
                    if n >= 2:
                        pe.wait_ge(qn_read, n - 1)
                        pe.wait_ge(qn_sqrt, n - 1)
                    src = k_att if c == 0 else q[:, c - 1, :]
                    mm(bank[4 + 2 * (n % 2)][:, 0:L], cst("head_mean"), qtmp[:, n % 2, :], start=True, stop=True)
                    mm(bank[5 + 2 * (n % 2)][:, 0:L], rot_g[:, 0 if c else 1, :], src, start=True,
                       stop=True).then_inc(qn_mm, 1)
                pe.wait_ge(qn_read, 9 * (l + 1))
                pe.wait_ge(qn_sqrt, 9 * (l + 1))
                pe.wait_ge(q_ready, 9 * l + 1)
                mm(bank[4][:, 0:L], cst("swap"), k_att, start=True, stop=True)
                for t, (a, b) in enumerate(QT):
                    nc.tensor.transpose(bank[5][0:b - a, t * P:(t + 1) * P], v_att[:, a:b], ident)
                pe.wait_ge(g_cm, l + 1)
                for t, (a, b) in enumerate(LT):
                    i_ = nc.tensor.transpose(bank[6][0:b - a, 4 * t:4 * t + 4], g_row[0:4, 3, a:b], ident[0:4, 0:4])
                i_.then_inc(kx_mm, 1)

                def attention(n):
                    N0 = ATT_H * l
                    if n < ATT_H:
                        hd, kv = n, n // 8
                        e = hd % 2
                        rows = slice(e * DH, (e + 1) * DH)
                        kk = k_att if kv == e else k_swap
                        if n == 0:
                            pe.wait_ge(q_ready, 9 * (l + 1))
                            pe.wait_ge(kx_read, l + 1)
                            pe.wait_ge(k_swapped, l + 1)
                        else:
                            pe.wait_ge(s_max, N0 + n)
                        qh = q[rows, hd // 2, :]
                        mm(bank[4][:, 0:KEYS1], qh[:, 16:144], kk[rows, 0:KEYS1], start=True, stop=True)
                        mm(bank[4][:, KEYS1:SW], qh[:, 144:L], kk[rows, 0:L], start=True, stop=True)
                        mm(bank[4][0:META, SW:SW + META], qh[:, 0:META], kk[rows, 0:META], start=True,
                           stop=True).then_inc(s_mm, 1)
                    if 1 <= n <= ATT_H:
                        m = n - 1
                        pr = prob[:, m % 2, :]
                        pe.wait_ge(s_prob, N0 + m + 1)
                        if m >= 1:
                            pe.wait_ge(s_ptb, N0 + m)
                            pe.wait_ge(s_ptm, N0 + m)
                        tr = nc.tensor.transpose
                        tr(bank[5][:, 0:P], pr[:, META:KEYS1], ident)
                        tr(bank[5][:, P:2 * P], pr[:, KEYS1 + META:KEYS1 + KEYS1], ident)
                        tr(bank[5][:, 2 * P:3 * P], pr[:, KEYS1 + KEYS1:SW], ident)
                        tr(bank[6][0:META, 0:META], pr[0:META, SW:SW + META], ident[0:META, 0:META])
                        tr(bank[6][0:META, META:KEYS1], pr[:, 0:META], ident)
                        tr(bank[6][0:META, KEYS1:L], pr[:, KEYS1:KEYS1 + META], ident).then_inc(s_tr, 1)
                    if n >= 2:
                        m = n - 2
                        e, kv = m % 2, m // 8
                        vc = slice(kv * DH, (kv + 1) * DH)
                        if m >= 2 and e == 0:
                            pe.wait_ge(s_out, (N0 + m) // 2)
                        pe.wait_ge(s_ptb, N0 + m + 1)
                        pe.wait_ge(s_ptm, N0 + m + 1)
                        o = bank[7][e * DH:(e + 1) * DH, :]
                        pb_, pm = pt_big[:, m % 2, :], pt_meta[:, m % 2, :]
                        mm(o[:, 0:L], va_t[0:META, 0, vc], pm[0:META, :], start=True, stop=False)
                        mm(o[:, META:L], va_t[:, 1, vc], pb_[:, 0:2 * P], start=False, stop=False)
                        mm(o[:, KEYS1:L], va_t[:, 2, vc], pb_[:, 2 * P:3 * P], start=False, stop=True).then_inc(s_pv, 1)

                step = 0
                for ph in ("mqk", "mv"):
                    pb = PHASES[f"{ph}{l}"][1]
                    for p in range(4):
                        def after(j, base=[0]):
                            attention(steps[0])
                            steps[0] += 1
                        if ph == "mqk" and p == 0:
                            steps = [0]
                        pair(pb + p, xs, L, after=after)
                attention(16)
                attention(17)

                pe.wait_ge(s_out, 8 * (l + 1))
                for c in range(NC8):
                    if c >= 4:
                        pe.wait_ge(mt_read, NC8 * l + c - 3)
                    for t, (a, b) in enumerate(LT):
                        i_ = nc.tensor.transpose(bank[4 + c % 4][0:b - a, t * P:(t + 1) * P], mv[:, c, a:b], ident)
                    i_.then_inc(mt_tr, 1)
                pe.wait_ge(mt_read, NC8 * (l + 1))

                def mlstm(hd):
                    n = M_H * l + hd
                    if hd:
                        pe.wait_ge(m_hm, n)
                    pe.wait_ge(g_exp, l + 1)
                    sel = con[0:4, CONST_AT["sel"] + hd * P:CONST_AT["sel"] + (hd + 1) * P]
                    mm(bank[4][:, 0:L], sel, g_row[0:4, 4, :], start=True, stop=True)
                    mm(bank[5][:, 0:L], sel, g_row[0:4, 5, :], start=True, stop=True).then_inc(m_bc, 1)
                    if hd == 0:
                        pe.wait_ge(qk_new, 8 * (l + 1))
                    for t, (a, b) in enumerate(LT):
                        i_ = mm(bank[6][0:b - a, MOFF[t]:MOFF[t] + L - a], qk[:, 4 + hd, a:b], qk[:, hd, a:L],
                                start=True, stop=True)
                    i_.then_inc(m_bc, 1)
                    pe.wait_ge(m_pt_new, n + 1)
                    for o, w in ((7, 0), (4, 1), (5, None)):
                        for t, (a, b) in enumerate(LT):
                            lhs = ones[0:b - a, :] if w is None else mvt[0:b - a, t, (2 * hd + w) * P:(2 * hd + w + 1) * P]
                            i_ = mm(bank[o][:, a:L], lhs, m_pt[0:b - a, MOFF[t]:MOFF[t] + L - a],
                                    start=t == 0, stop=t == 2)
                    i_.then_inc(m_nd, 1)

                pb = PHASES[f"ag{l}"][1]
                for hd in range(M_H):
                    mlstm(hd)
                pe.wait_ge(m_hm, M_H * (l + 1))
                for hd in range(M_H):
                    n = M_H * l + hd
                    pe.wait_ge(n_sq, n + 1)
                    mm(bank[4 + hd][:, 0:L], ones[:, :], qtmp2[:, hd % 2, :], start=True, stop=True).then_inc(n_mm, 1)
                for ph in ("ag", "mo", "mg"):
                    pb = PHASES[f"{ph}{l}"][1]
                    for p in range(4):
                        pair(pb + p, xs, L)
                pb = PHASES[f"proj{l}"][1]
                for p in range(4):
                    pair(pb + p, ys, L, ready=SPLITS[f"y_proj{l}"] if p == 0 else None)

            last_tile = 2 * len(PAIRS)
            for g in range(4):
                t, c0 = g // 2, 4 * (g % 2)
                pe.wait_ge(tile_read, last_tile)
                for c in range(c0, c0 + 4):
                    i_ = nc.tensor.transpose(bank[4 + g][:, (c % 4) * P:(c % 4 + 1) * P],
                                             h[:, c, META + t * P:META + (t + 1) * P], ident)
                i_.then_inc(ot_tr, 1)

        @block.scalar
        def _(act):
            activation = nc.scalar.activation
            chain = [0]

            def split_w(U, off=0):
                if U >= NU:
                    return
                n, s = UNITS[U][3], U % RING
                act.wait_ge(w_loaded[s], LANDED[U] + (off * 4 if not isinstance(off, int) else 4 * off))
                if not (isinstance(off, int) and U - RING + 1 + off <= 0):
                    act.wait_ge(unit_done, U - RING + 1 + off)
                nc.scalar.copy(w_hi[:, s, 0:n, :], raw[:, s, 0:n, :]).then_inc(hi_made, 1)

            def split_x(dst, k, N, src, scale=None):
                if scale is None:
                    i_ = nc.scalar.copy(xview(dst, k, N), src)
                else:
                    i_ = activation(xview(dst, k, N), src, ACT.Copy, scale=scale)
                i_.then_inc(act_hi, 1)

            def ahead(pr):
                for U, _, _ in units_of(pr):
                    split_w(U + LEAD)

            def root(n, T0):
                act.wait_ge(sum_done, n + 1)
                activation(rms[:, T0:L], bank[4][:, T0:L], ACT.Sqrt, scale=1.0 / D, bias=epsc[:, 0:1]).then_inc(rms_done, 1)

            def gate_turn(pb, ub, i, first=None):
                o4, o = 4 * i, (4 * i if not isinstance(i, int) else 4 * i)
                for U in (ub, ub + 1):
                    split_w(U + LEAD, o)
                if first is not None:
                    root(first, META)
                for m in range(2):
                    act.wait_ge(tile_read, 2 * pb + m + 1 + o4)
                    activation(ffn_s[:, m, :], ffn_t[:, m, :], ACT.Silu).then_inc(silu_done, 1)
                for U in (ub + 2, ub + 3):
                    split_w(U + LEAD, o)
                for m in range(2):
                    act.wait_ge(tile_read, 2 * pb + 2 + m + 1 + o4)
                    if isinstance(i, int):
                        dst = xview(y_hi, 2 * i + m, SEQ)
                    else:
                        dst = y_hi[:, bass.ds(i * (2 * SEQ) + m * SEQ, SEQ)]
                        act.wait_ge(tile_read, 1)
                    nc.scalar.copy(dst, ffn_h[:, m, :]).then_inc(act_hi, 1)

            def in_phase(name, n):
                ub, pb, _ = PHASES[name]
                gate_turn(pb, ub, 0, first=n)
                with act.Fori(1, FF // CU) as i:
                    gate_turn(pb, ub, i)

            def out_phase(name, g, N=SEQ, T0=META):
                ub, pb, npairs = PHASES[name]
                for p in range(npairs):
                    ahead(pb + p)
                    for m in range(2):
                        c = 2 * p + m
                        act.wait_ge(tile_read, 2 * (pb + p) + m + 1)
                        if g is not None:
                            split_x(x_hi, c, N, h[:, c, T0:L], g(c))

            act.wait_ge(par_ready, 1)
            act.wait_ge(decay_v, 1)
            activation(decay[:, 1, :], decay[:, 0, :], ACT.Exp).then_inc(decay_e, 1)
            for c in range(NC8):
                act.wait_ge(xt_read, c + 1)
                split_x(x_hi, c, SEQ, h[:, c, META:L], pcol("ffn1_norm", c))
            for U in range(LEAD):
                split_w(U)
            in_phase("in01", 0)
            out_phase("out01", lambda c: pcol("mix_norm", c))

            _, pb, _ = PHASES["rec_b"]
            for p in range(4):
                ahead(pb + p)
                if p == 0:
                    root(1, META)
            _, pb, _ = PHASES["rec_a"]
            T = 2 * pb
            ahead(pb)
            for c in range(NC8):
                act.wait_ge(gates_mm, c + 1)
                activation(rec_a[:, c, :], bank[4 + c % 4][:, 0:SEQ], ACT.Sigmoid,
                           bias=pcol("rec_gate_a_b", c)).then_inc(gates_sig, 1)
                activation(rec_g[:, c, :], bank[4 + c % 4][:, SEQ:2 * SEQ], ACT.Sigmoid,
                           bias=pcol("rec_gate_x_b", c)).then_inc(gates_sig, 1)
                if c == 3:
                    ahead(pb + 1)
            for c in range(NC8):
                act.wait_ge(gates_sig, 2 * c + 1)
                if c == 0:
                    act.wait_ge(decay_v, 2)
                if c >= 2:
                    act.wait_ge(mult2, c - 1)
                activation(ffn_t[:, c % 2, :], rec_a[:, c, :], ACT.Tanh, scale=decay[:, 3, c:c + 1]).then_inc(ach, 1)
                chain[0] += 1
                act.wait_ge(ach, chain[0])
                activation(rec_a[:, c, :], rec_a[:, c, :], ACT.Exp, scale=decay[:, 2, c:c + 1]).then_inc(ax_new, 1)
                if c == 3:
                    ahead(pb + 2)
            for c in range(NC8):
                act.wait_ge(mult2, c + 1)
                activation(rec_p[:, c, 0:SEQ], rec_p[:, c, 0:SEQ], ACT.Sqrt).then_inc(mult_new, 1)
            ahead(pb + 3)
            for c in range(NC8):
                act.wait_ge(tile_read, T + c + 1)
                activation(rec_y[:, c, :], rec_y[:, c, :], ACT.Gelu_apprx_tanh).then_inc(rec_gelu, 1)
            for c in range(NC8):
                act.wait_ge(act_new, c + 1)
                split_x(y_hi, c, SEQ, rec_y[:, c, :])
            out_phase("rec_out", lambda c: pcol("ffn2_norm", c))

            in_phase("in02", 2)
            out_phase("out02", lambda c: pcol("ffn1_norm", NC8 + c))
            in_phase("in11", 3)
            out_phase("out11", lambda c: pcol("mix_norm", NC8 + c))

            _, pb, _ = PHASES["sg_b"]
            for p in range(4):
                ahead(pb + p)
                if p == 0:
                    root(4, META)
                for m in range(2):
                    c = 2 * p + m
                    act.wait_ge(tile_read, 2 * pb + c + 1)
                    activation(sg_v[:, c, :], sg_v[:, c, :], ACT.Gelu_apprx_tanh).then_inc(sg_gelu, 1)
            _, pb, _ = PHASES["sg_a"]
            for p in range(4):
                ahead(pb + p)
                if p == 0:
                    act.wait_ge(sg_sum, 1)
                    activation(sg_r[:, 0, :], bank[4][:, 0:2], ACT.Sqrt, scale=1.0 / D, bias=epsc[:, 0:1]).then_inc(sg_rms, 1)
                for m in range(2):
                    c = 2 * p + m
                    act.wait_ge(tile_read, 2 * pb + c + 1)
                    activation(sg_u[:, c, :], sg_u[:, c, :], ACT.Gelu_apprx_tanh).then_inc(sg_gelu, 1)
            for c in range(NC8):
                act.wait_ge(act_new, NC8 + c + 1)
                split_x(y_hi, c, SEQ, sg_s[:, c, :])
            out_phase("sg_out", lambda c: pcol("ffn2_norm", NC8 + c))

            in_phase("in12", 5)
            out_phase("out12", None)
            root(6, META)
            for c in range(NC8):
                act.wait_ge(final_new, c + 1)
                split_x(x_hi, c, L, h[:, c, :], pcol("norm_g_2", c))

            for l in range(DEPTH):
                ahead(PHASES[f"kv{l}"][1])
                root(7 + l, 0)
                ahead(PHASES[f"mif{l}"][1])
                act.wait_ge(g_nx, l + 1)
                activation(g_row[0:4, 2, :], g_row[0:4, 1, :], ACT.Exp).then_inc(g_e, 1)
                for p in range(4):
                    ahead(PHASES[f"aq{l}"][1] + p)
                for c in range(9):
                    n = 9 * l + c
                    act.wait_ge(qn_mm, n + 1)
                    if n >= 2:
                        act.wait_ge(q_ready, n - 1)
                    activation(qtmp2[:, n % 2, :], bank[4 + 2 * (n % 2)][:, 0:L], ACT.Sqrt,
                               bias=epsc[:, 0:1]).then_inc(qn_sqrt, 1)
                act.wait_ge(kx_mm, l + 1)
                nc.scalar.copy(k_swap, bank[4][:, 0:L]).then_inc(k_swapped, 1)
                act.wait_ge(k_swapped, l + 1)
                act.wait_ge(g_cm, l + 1)
                activation(g_row[0:4, 5, :], g_row[0:4, 5, :], ACT.Exp, scale=-1.0).then_inc(g_exp, 1)

                def attention(n):
                    N0 = ATT_H * l
                    if n < ATT_H:
                        i = n % 2
                        act.wait_ge(s_max, N0 + n + 1)
                        if n >= 2:
                            act.wait_ge(s_tr, N0 + n - 1)
                        s, pr = score[:, i, :], prob[:, i, :]
                        nm, den, es = att_s[:, 3 * i + 1, :], att_s[:, 3 * i + 2, :], att_s[:, 6 + i, :]
                        activation(es[:, 0:3], nm[:, 0:3], ACT.Exp, bias=sinks[:, l * ATT_H + n:l * ATT_H + n + 1])
                        activation(pr[:, 0:KEYS1], s[:, 0:KEYS1], ACT.Exp, bias=nm[:, 0:1], accum_out=den[:, 0:1])
                        activation(pr[0:META, SW:SW + META], s[0:META, SW:SW + META], ACT.Exp, bias=nm[0:META, 2:3],
                                   accum_out=den[0:META, 2:3])
                        activation(pr[:, KEYS1:SW], s[:, KEYS1:SW], ACT.Exp, bias=nm[:, 1:2],
                                   accum_out=den[:, 1:2]).then_inc(s_exp, 1)
                    if 1 <= n <= ATT_H:
                        m = n - 1
                        act.wait_ge(s_tr, N0 + m + 1)
                        if N0 + m >= 2:
                            act.wait_ge(s_pv, N0 + m - 1)
                        nc.scalar.copy(pt_big[:, m % 2, :], bank[5][:, 0:3 * P]).then_inc(s_ptb, 1)

                n = 0
                for ph in ("mqk", "mv"):
                    for p in range(4):
                        for U, _, _ in units_of(PHASES[f"{ph}{l}"][1] + p):
                            split_w(U + LEAD)
                            attention(n)
                            n += 1
                attention(16)
                for c in range(NC8):
                    act.wait_ge(conv2_new, NC8 * l + c + 1)
                    activation(qk[:, c, :], qk[:, c, :], ACT.Silu).then_inc(qk_new, 1)
                for hd in range(M_H):
                    n = M_H * l + hd
                    act.wait_ge(m_bc, 2 * n + 1)
                    nc.scalar.copy(exp_b, bank[5][:, 0:L]).then_inc(m_eb, 1)
                    act.wait_ge(m_arg_new, n + 1)
                    for t, (a, b) in enumerate(LT):
                        i_ = activation(m_arg[0:b - a, MOFF[t]:MOFF[t] + L - a], m_arg[0:b - a, MOFF[t]:MOFF[t] + L - a],
                                        ACT.Exp, scale=-1.0, bias=g_tok[0:b - a, t, hd:hd + 1])
                    i_.then_inc(m_exp_new, 1)
                for hd in range(M_H):
                    n = M_H * l + hd
                    act.wait_ge(n_mm, n + 1)
                    if hd >= 2:
                        act.wait_ge(n_new, n - 1)
                    activation(score[:, hd % 2, 0:L], bank[4 + hd][:, 0:L], ACT.Sqrt, scale=1.0 / 256,
                               bias=epsc[:, 0:1]).then_inc(n_sqrt, 1)
                for ph, f in (("ag", ACT.Silu), ("mo", ACT.Sigmoid), ("mg", ACT.Silu)):
                    pb = PHASES[f"{ph}{l}"][1]
                    for p in range(4):
                        ahead(pb + p)
                        for m in range(2):
                            c = 2 * p + m
                            act.wait_ge(tile_read, 2 * (pb + p) + m + 1)
                            activation(prob[:, m, 0:L], prob[:, m, 0:L], f).then_inc(gate_act, 1)
                        if ph != "mo":
                            for m in range(2):
                                c = 2 * p + m
                                act.wait_ge(act_new, 16 + 16 * l + (c if ph == "ag" else NC8 + c) + 1)
                                src = q if ph == "ag" else hm
                                split_x(y_hi, c if ph == "ag" else NC8 + c, L, src[:, c, :])
                out_phase(f"proj{l}", (lambda c: pcol("norm_g_2", NC8 + c)) if l == 0 else None, N=L, T0=0)

        @block.gpsimd
        def _(pool):
            nc.gpsimd.memset(ones[:, :], 1.0)
            nc.gpsimd.memset(epsc[:, :], EPS).then_inc(ones_set, 1)
            nc.gpsimd.memset(blocks_a[:, :, :], 0.0)
            nc.gpsimd.memset(blocks_x[:, :, :], 0.0)
            nc.gpsimd.memset(pre[:, :, 0:3], 0.0)
            nc.gpsimd.memset(rec_p[:, :, 0:3], 0.0).then_inc(zero_set, 1)
            TT = nc.gpsimd.tensor_tensor
            chain = [0]

            def link(i_):
                chain[0] += 1
                i_.then_inc(pool_ch, 1)
                pool.wait_ge(pool_ch, chain[0])

            def squares(src, wait, T0, done):
                for c in range(NC8):
                    wait(c)
                    if c == 0:
                        link(TT(sumsq[:, T0:L], src(c), src(c), MUL))
                    else:
                        link(TT(sq[:, T0:L], src(c), src(c), MUL))
                        i_ = TT(sumsq[:, T0:L], sumsq[:, T0:L], sq[:, T0:L], ADD)
                        if c < NC8 - 1:
                            link(i_)
                        else:
                            i_.then_inc(done, 1)

            def h_squares(n, name, T0):
                pb = PHASES[name][1]
                if n:
                    pool.wait_ge(sum_done, n)
                squares(lambda c: h[:, c, T0:L], lambda c: pool.wait_ge(tile_read, 2 * pb + c + 1), T0, sq_done)

            def gate_scale(f):
                def turn(i):
                    for m in range(2):
                        pool.wait_ge(silu_done, 22 * f + m + 1 + 2 * i)
                        TT(ffn_r[:, m, :], ffn_s[:, m, :], rstd[:, META:L], MUL).then_inc(gate_scaled, 1)
                with pool.Fori(0, FF // CU) as i:
                    turn(i)

            squares(lambda c: h[:, c, META:L], lambda c: pool.wait_ge(xt_read, c + 1), META, sq_done)
            gate_scale(0)
            h_squares(1, "out01", META)
            for c in range(NC8):
                pool.wait_ge(gates_sig, 2 * c + 2)
                i_ = TT(rec_x[:, c, :], rec_x[:, c, :], rec_g[:, c, :], MUL)
                i_.then_inc(pool_ch, 1)
                chain[0] += 1
            for c in range(NC8):
                pool.wait_ge(mult_new, c + 1)
                pool.wait_ge(pool_ch, chain[0])
                TT(rec_x[:, c, :], rec_x[:, c, :], rec_p[:, c, 0:SEQ], MUL).then_inc(rec_bx, 1)
            h_squares(2, "rec_out", META)
            gate_scale(1)
            h_squares(3, "out02", META)
            gate_scale(2)
            h_squares(4, "out11", META)
            pool.wait_ge(sum_done, 5)
            squares(lambda c: sg_v[:, c, :], lambda c: pool.wait_ge(sg_gelu, c + 1), META, sg_sqs)
            pool.wait_ge(sg_sum, 1)
            h_squares(5, "sg_out", META)
            gate_scale(3)
            h_squares(6, "out12", META)
            pool.wait_ge(sum_done, 7)
            squares(lambda c: h[:, c, :], lambda c: pool.wait_ge(final_new, c + 1), 0, sq_done)
            for l in range(DEPTH):
                for n in range(ATT_H):
                    m = ATT_H * l + n
                    i = n % 2
                    pr, rec = prob[:, i, :], att_s[:, 8 + i, :]
                    TS = nc.gpsimd.tensor_scalar
                    pool.wait_ge(s_exp, m + 1)
                    pool.wait_ge(g_tok_new, m + 1)
                    TS(pr[:, 0:KEYS1], pr[:, 0:KEYS1], rec[:, 0:1], None, MUL)
                    TS(pr[0:META, SW:SW + META], pr[0:META, SW:SW + META], rec[0:META, 2:3], None, MUL)
                    TS(pr[:, KEYS1:SW], pr[:, KEYS1:SW], rec[:, 1:2], None, MUL).then_inc(s_prob, 1)
                for hd in range(M_H):
                    n = M_H * l + hd
                    pool.wait_ge(m_hm, n + 1)
                    if n:
                        pool.wait_ge(n_sq, n)
                    if hd >= 2:
                        pool.wait_ge(n_mm, n - 1)
                    link(TT(sq[:, :], hm[:, 2 * hd, :], hm[:, 2 * hd, :], MUL))
                    link(TT(qtmp2[:, hd % 2, :], hm[:, 2 * hd + 1, :], hm[:, 2 * hd + 1, :], MUL))
                    TT(qtmp2[:, hd % 2, :], qtmp2[:, hd % 2, :], sq[:, :], ADD).then_inc(n_sq, 1)
                if l == 0:
                    h_squares(8, "proj0", 0)

        @block.vector
        def _(dve):
            V = nc.vector
            TT, TS, STT = V.tensor_tensor, V.tensor_scalar, V.scalar_tensor_tensor
            chain = [0]

            def link(i_):
                chain[0] += 1
                i_.then_inc(dch, 1)
                dve.wait_ge(dch, chain[0])

            def split_w(U, off=0):
                if U >= NU:
                    return
                n, s = UNITS[U][3], U % RING
                dve.wait_ge(hi_made, U + 1 + off)
                TT(w_lo[:, s, 0:n, :], raw[:, s, 0:n, :], w_hi[:, s, 0:n, :].bitcast(fp32), SUB).then_inc(lo_made, 1)

            def ahead(pr):
                for U, _, _ in units_of(pr):
                    split_w(U + LEAD)

            def split_x(dst_lo, dst_hi, k, N, src, count, scale=None):
                dve.wait_ge(act_hi, count + 1)
                hi = xview(dst_hi, k, N).bitcast(fp32)
                if scale is None:
                    i_ = TT(xview(dst_lo, k, N), src, hi, SUB)
                else:
                    i_ = STT(out=xview(dst_lo, k, N), in0=src, scalar=scale, in1=hi, op0=MUL, op1=SUB)
                i_.then_inc(act_ready, 1)

            def inverse(n, T0):
                dve.wait_ge(rms_done, n + 1)
                link(V.reciprocal(rstd[:, T0:L], rms[:, T0:L]))

            def wait_tile(pr, m, off=0):
                if m == 0 and len(units_of(pr)) and pr not in ONE_TILE:
                    dve.wait_ge(first_done, FIRSTS[pr] + 1 + (off // 2 if isinstance(off, int) else 2 * off_i[0]))
                else:
                    dve.wait_ge(unit_done, units_of(pr)[-1][0] + 1 + off)

            off_i = [0]
            ONE_TILE = {PHASES[f"mif{l}"][1] for l in range(DEPTH)}
            FIRSTS = {}
            k_ = 0
            for pr_ in range(len(PAIRS)):
                FIRSTS[pr_] = k_
                k_ += pr_ not in ONE_TILE

            def tile(pr, m, N):
                return bank[(2 * pr + m) % 4][:, 0:N]

            def scaled(pr, m, dst, N, T0, off=0):
                wait_tile(pr, m, off)
                TT(dst, tile(pr, m, N), rstd[:, T0:L], MUL).then_inc(tile_read, 1)

            def gate_turn(pb, ub, i, f, count, first=None):
                o = 4 * i
                off_i[0] = i
                for U in (ub, ub + 1):
                    split_w(U + LEAD, o)
                if first is not None:
                    inverse(first, META)
                for m in range(2):
                    scaled(pb, m, ffn_t[:, m, :], SEQ, META, o)
                for U in (ub + 2, ub + 3):
                    split_w(U + LEAD, o)
                for m in range(2):
                    wait_tile(pb + 1, m, o)
                    dve.wait_ge(gate_scaled, 22 * f + m + 1 + 2 * i)
                    TT(ffn_h[:, m, :], tile(pb + 1, m, SEQ), ffn_r[:, m, :], MUL).then_inc(tile_read, 1)
                for m in range(2):
                    dve.wait_ge(act_hi, count + m + 1 + 2 * i)
                    if isinstance(i, int):
                        lo, hi = (xview(t, 2 * i + m, SEQ) for t in (y_lo, y_hi))
                    else:
                        lo, hi = (t[:, bass.ds(i * (2 * SEQ) + m * SEQ, SEQ)] for t in (y_lo, y_hi))
                    TT(lo, ffn_h[:, m, :], hi.bitcast(fp32), SUB).then_inc(act_ready, 1)

            def in_phase(name, f, n, count):
                ub, pb, _ = PHASES[name]
                gate_turn(pb, ub, 0, f, count, first=n)
                with dve.Fori(1, FF // CU) as i:
                    gate_turn(pb, ub, i, f, count)

            def out_phase(name, g, count, half=0.5, N=SEQ, T0=META):
                ub, pb, npairs = PHASES[name]
                for p in range(npairs):
                    ahead(pb + p)
                    for m in range(2):
                        c = 2 * p + m
                        wait_tile(pb + p, m)
                        STT(out=h[:, c, T0:L], in0=tile(pb + p, m, N), scalar=half, in1=h[:, c, T0:L], op0=MUL,
                            op1=ADD).then_inc(tile_read, 1)
                        if g is not None:
                            split_x(x_lo, x_hi, c, N, h[:, c, T0:L], count + c, g(c))

            dve.wait_ge(par_t, 1)
            rows1 = sum(k for (t, _, k) in PAR.values() if t == 1)
            V.tensor_copy(par[:, 0, :], bank[4][:, 0:P])
            V.tensor_copy(par[:, 1, 0:rows1], bank[4][:, P:P + rows1]).then_inc(par_ready, 1)
            dve.wait_ge(par_ready, 1)
            for c in range(NC8):
                dve.wait_ge(xt_done, c + 1)
                V.tensor_copy(h[:, c, :], bank[c % 4][:, 0:L]).then_inc(xt_read, 1)
            dve.wait_ge(zero_set, 1)
            dve.wait_ge(xt_read, NC8)
            lam_t, lam_r, _ = PAR["rec_lambda"]
            lam = par[:, lam_t, lam_r:lam_r + NC8]
            link(STT(out=decay[:, 0, :], in0=lam, scalar=-1.0, in1=lam, op0=MUL, op1=MIN))

            def log1p(dst, e, t0, t1, t2):
                link(TS(t0, e, 2.0, None, ADD))
                link(V.reciprocal(t1, t0))
                link(TT(t0, e, t1, MUL))
                link(TT(t1, t0, t0, MUL))
                link(TS(t2, t1, 1.0 / 17, None, MUL))
                for k in (15, 13, 11, 9, 7, 5, 3):
                    link(STT(out=t2, in0=t2, scalar=1.0 / k, in1=t1, op0=ADD, op1=MUL))
                link(STT(out=t2, in0=t2, scalar=1.0, in1=t0, op0=ADD, op1=MUL))
                link(TS(dst, t2, 2.0, None, MUL))

            V.tensor_copy(decay[:, 11, :], decay[:, 0, :]).then_inc(decay_v, 1)
            dve.wait_ge(decay_e, 1)
            log1p(decay[:, 4, :], decay[:, 1, :], decay[:, 5, :], decay[:, 6, :], decay[:, 7, :])
            link(TS(decay[:, 8, :], lam, -1.0, 0.0, MUL, MAX))
            link(TT(decay[:, 9, :], decay[:, 8, :], decay[:, 4, :], ADD))
            TS(decay[:, 2, :], decay[:, 9, :], -8.0, None, MUL)
            TS(decay[:, 3, :], decay[:, 9, :], 8.0, None, MUL).then_inc(decay_v, 1)
            for c in range(NC8):
                split_x(x_lo, x_hi, c, SEQ, h[:, c, META:L], c, pcol("ffn1_norm", c))
            for U in range(LEAD):
                split_w(U)

            in_phase("in01", 0, 0, SPLITS["y_out01"])
            out_phase("out01", lambda c: pcol("mix_norm", c), SPLITS["x_rec_b"])

            _, pb, _ = PHASES["rec_b"]
            for p in range(4):
                ahead(pb + p)
                if p == 0:
                    inverse(1, META)
                for m in range(2):
                    scaled(pb + p, m, rec_p[:, 2 * p + m, 3:3 + SEQ], SEQ, META)
                dve.wait_ge(tile_read, 2 * (pb + p) + 2)
                for k in range(4):
                    for m in range(2):
                        c = 2 * p + m
                        src, w = rec_p[:, c, k:k + SEQ], pcol("rec_conv_w", k * NC8 + c)
                        if k == 0:
                            i_ = TS(rec_x[:, c, :], src, w, pcol("rec_conv_b", c), MUL, ADD)
                        else:
                            i_ = STT(out=rec_x[:, c, :], in0=src, scalar=w, in1=rec_x[:, c, :], op0=MUL, op1=ADD)
                        if k == 3:
                            i_.then_inc(conv_new, 1)
                        elif m == 1:
                            link(i_)
            _, pb, _ = PHASES["rec_a"]
            ahead(pb)
            for m in range(2):
                scaled(pb, m, rec_y[:, m, :], SEQ, META)
            ahead(pb + 1)
            for m in range(2):
                scaled(pb + 1, m, rec_y[:, 2 + m, :], SEQ, META)

            def mult_square(c):
                dve.wait_ge(ax_new, c + 1)
                t = ffn_t[:, c % 2, :]
                link(TS(ffn_r[:, c % 2, :], t, 1.0, None, ADD))
                link(V.reciprocal(ffn_h[:, c % 2, :], ffn_r[:, c % 2, :]))
                STT(out=rec_p[:, c, 0:SEQ], in0=t, scalar=2.0, in1=ffn_h[:, c % 2, :], op0=MUL, op1=MUL).then_inc(mult2, 1)

            for c in range(4):
                mult_square(c)
            ahead(pb + 2)
            for c in range(4, NC8):
                mult_square(c)
            for m in range(2):
                scaled(pb + 2, m, rec_y[:, 4 + m, :], SEQ, META)
            ahead(pb + 3)
            for m in range(2):
                scaled(pb + 3, m, rec_y[:, 6 + m, :], SEQ, META)
            dve.wait_ge(mult2, NC8)
            for c in range(NC8):
                dve.wait_ge(rec_bx, c + 1)
                link(V.tensor_tensor_scan(rec_g[:, c, :], rec_a[:, c, :], rec_x[:, c, :], 0.0, MUL, ADD))
                dve.wait_ge(rec_gelu, c + 1)
                TT(rec_y[:, c, :], rec_y[:, c, :], rec_g[:, c, :], MUL).then_inc(act_new, 1)
            for c in range(NC8):
                split_x(y_lo, y_hi, c, SEQ, rec_y[:, c, :], SPLITS["y_rec_out"] + c)
            out_phase("rec_out", lambda c: pcol("ffn2_norm", c), SPLITS["x_in02"], half=1.0)

            in_phase("in02", 1, 2, SPLITS["y_out02"])
            out_phase("out02", lambda c: pcol("ffn1_norm", NC8 + c), SPLITS["x_in11"])
            in_phase("in11", 2, 3, SPLITS["y_out11"])
            out_phase("out11", lambda c: pcol("mix_norm", NC8 + c), SPLITS["x_sg_b"])

            _, pb, _ = PHASES["sg_b"]
            for p in range(4):
                ahead(pb + p)
                if p == 0:
                    inverse(4, META)
                for m in range(2):
                    scaled(pb + p, m, sg_v[:, 2 * p + m, :], SEQ, META)
                if p == 1:
                    dve.wait_ge(ws_tr, 1)
                    for c in range(NC8):
                        i_ = TT(ws_t[:, c, :], bank[5 + c // 4][:, (c % 4) * P:(c % 4 + 1) * P], tri, MUL)
                        if c % 4 == 3:
                            i_.then_inc(ws_read, 1)
            _, pb, _ = PHASES["sg_a"]
            ahead(pb)
            for m in range(2):
                scaled(pb, m, sg_u[:, m, :], SEQ, META)
            dve.wait_ge(sg_rms, 1)
            link(V.reciprocal(sg_r[:, 1, :], sg_r[:, 0, :]))
            for g in range(4):
                t, c0 = g // 2, 4 * (g % 2)
                dve.wait_ge(vt_tr, g + 1)
                TS(v_tok[:, t, c0 * P:(c0 + 4) * P], bank[5 + g % 3][:, :], sg_r[:, 1, t:t + 1], None, MUL).then_inc(vt_read, 1)
            ahead(pb + 1)
            for m in range(2):
                scaled(pb + 1, m, sg_u[:, 2 + m, :], SEQ, META)
            for c in range(NC8):
                dve.wait_ge(sg_mm, c + 1)
                for t in range(2):
                    i_ = STT(out=sg_s[:, c, t * P:(t + 1) * P], in0=bank[4 + c % 4][:, t * P:(t + 1) * P],
                             scalar=pcol("sg_v_norm", c), in1=bs_all[:, c, :], op0=MUL, op1=ADD)
                i_.then_inc(sg_read, 1)
            for p in (2, 3):
                ahead(pb + p)
                for m in range(2):
                    scaled(pb + p, m, sg_u[:, 2 * p + m, :], SEQ, META)
            dve.wait_ge(sg_read, NC8)
            for c in range(NC8):
                dve.wait_ge(sg_gelu, NC8 + c + 1)
                TT(sg_s[:, c, :], sg_s[:, c, :], sg_u[:, c, :], MUL).then_inc(act_new, 1)
            for c in range(NC8):
                split_x(y_lo, y_hi, c, SEQ, sg_s[:, c, :], SPLITS["y_sg_out"] + c)
            out_phase("sg_out", lambda c: pcol("ffn2_norm", NC8 + c), SPLITS["x_in12"], half=1.0)

            in_phase("in12", 3, 5, SPLITS["y_out12"])
            out_phase("out12", None, 0)
            inverse(6, META)
            for c in range(NC8):
                STT(out=h[:, c, META:L], in0=h[:, c, META:L], scalar=pcol("final_norm", c), in1=rstd[:, META:L], op0=MUL,
                    op1=MUL).then_inc(final_new, 1)
            V.memset(att_s[:, :, :], 0.0).then_inc(final_new, 1)
            for c in range(NC8):
                split_x(x_lo, x_hi, c, L, h[:, c, :], SPLITS["x_kv0"] + c, pcol("norm_g_2", c))

            for l in range(DEPTH):
                pb = PHASES[f"kv{l}"][1]
                ahead(pb)
                inverse(7 + l, 0)
                scaled(pb, 0, k_att, L, 0)
                scaled(pb, 1, v_att, L, 0)
                gq, gk = pcol("attn_q_norm_g_2", l), pcol("attn_k_norm_g_2", l)
                sc = DH ** -0.5
                TS(cos_g[:, 0, :], cst("cos"), gq, sc, MUL, MUL)
                TS(cos_g[:, 1, :], cst("cos"), gk, None, MUL)
                TS(rot_g[:, 0, :], cst("rot"), gq, sc, MUL, MUL)
                link(TS(rot_g[:, 1, :], cst("rot"), gk, None, MUL))

                pb = PHASES[f"mif{l}"][1]
                ahead(pb)
                wait_tile(pb, 1)
                b0 = bank[(2 * pb) % 4]
                TT(g_row[0:4, 3, :], b0[0:4, 0:L], rstd[0:4, :], MUL)
                link(TT(g_row[0:4, 0, :], b0[32:36, 0:L], rstd[32:36, :], MUL))
                TS(g_row[0:4, 3, :], g_row[0:4, 3, :], gbias[:, l:l + 1], None, ADD)
                link(TS(g_row[0:4, 0, :], g_row[0:4, 0, :], gbias[:, DEPTH + l:DEPTH + l + 1], None, ADD))
                V.tensor_copy(g_row[0:1, 4, 0:1], g_row[0:1, 0, 0:1]).then_inc(tile_read, 2)
                STT(out=g_row[0:4, 1, :], in0=g_row[0:4, 0, :], scalar=-1.0, in1=g_row[0:4, 0, :], op0=MUL,
                    op1=MIN).then_inc(g_nx, 1)

                def key_or_query(c):
                    n = 9 * l + c
                    src = k_att if c == 0 else q[:, c - 1, :]
                    if n >= 2:
                        dve.wait_ge(qn_mm, n - 1)
                    TT(qtmp[:, n % 2, :], src, src, MUL).then_inc(qsq_new, 1)

                def rotate(c):
                    n = 9 * l + c
                    src = k_att if c == 0 else q[:, c - 1, :]
                    dve.wait_ge(qn_mm, n + 1)
                    t = score[:, n % 2, 0:L]
                    TT(t, bank[5 + 2 * (n % 2)][:, 0:L], cst("sin"), MUL).then_inc(qn_read, 1)
                    link(TT(src, src, cos_g[:, 0 if c else 1, :], MUL))
                    link(TT(src, src, t, ADD))
                    dve.wait_ge(qn_sqrt, n + 1)
                    link(V.reciprocal(t, qtmp2[:, n % 2, :]))
                    TT(src, src, t, MUL).then_inc(q_ready, 1)

                pb = PHASES[f"aq{l}"][1]
                dve.wait_ge(g_e, l + 1)
                log1p(g_row[0:4, 5, :], g_row[0:4, 2, :], g_row[0:4, 1, :], exp_b[0:4, :], m_b[0:4, :])
                link(STT(out=g_row[0:4, 1, :], in0=g_row[0:4, 0, :], scalar=0.0, in1=g_row[0:4, 5, :], op0=MIN, op1=SUB))
                link(V.memset(g_row[0:4, 0, :], 1.0))
                link(V.tensor_tensor_scan(g_row[0:4, 2, :], g_row[0:4, 0, :], g_row[0:4, 1, :], 0.0, MUL, ADD))
                link(TT(g_row[0:4, 3, :], g_row[0:4, 3, :], g_row[0:4, 2, :], SUB))
                link(V.tensor_tensor_scan(g_row[0:4, 4, :], g_row[0:4, 3, :], g_row[0:4, 3, :], 0.0, MAX, MAX))
                TT(g_row[0:4, 5, :], g_row[0:4, 2, :], g_row[0:4, 4, :], ADD).then_inc(g_cm, 1)
                for p in range(4):
                    ahead(pb + p)
                    for m in range(2):
                        scaled(pb + p, m, q[:, 2 * p + m, :], L, 0)
                    dve.wait_ge(tile_read, 2 * (pb + p) + 2)
                    if p == 3:
                        key_or_query(0)
                        for c in range(9):
                            if c < 8:
                                key_or_query(c + 1)
                            rotate(c)
                dve.wait_ge(kx_mm, l + 1)
                for t, (a, b) in enumerate(QT):
                    V.tensor_copy(va_t[0:b - a, t, :], bank[5][0:b - a, t * P:(t + 1) * P])
                dve.wait_ge(g_exp, l + 1)
                for t, (a, b) in enumerate(LT):
                    i_ = V.tensor_copy(g_tok[0:b - a, t, :], bank[6][0:b - a, 4 * t:4 * t + 4])
                i_.then_inc(kx_read, 1)

                def attention(n):
                    N0 = ATT_H * l
                    if n < ATT_H:
                        i = n % 2
                        s, mx, nm = score[:, i, :], att_s[:, 3 * i, :], att_s[:, 3 * i + 1, :]
                        sink = sinks[:, l * ATT_H + n:l * ATT_H + n + 1]
                        dve.wait_ge(s_mm, N0 + n + 1)
                        if n >= 2:
                            dve.wait_ge(s_exp, N0 + n - 1)
                        for r, a, b, col in ((P, 0, KEYS1, 0), (P, KEYS1, SW, 1), (META, SW, SW + META, 2)):
                            i_ = TT(s[0:r, a:b], bank[4][0:r, a:b], con[0:r, CONST_AT["amask"] + a:CONST_AT["amask"] + b], ADD)
                        link(i_)
                        for r, a, b, col in ((P, 0, KEYS1, 0), (P, KEYS1, SW, 1), (META, SW, SW + META, 2)):
                            i_ = V.reduce_max(mx[0:r, col:col + 1], s[0:r, a:b], mybir.AxisListType.X)
                        link(i_)
                        TS(nm[:, 0:3], mx[:, 0:3], sink, -1.0, MAX, MUL).then_inc(s_max, 1)
                    if 1 <= n <= ATT_H:
                        m = n - 1
                        i = m % 2
                        dve.wait_ge(s_exp, N0 + m + 1)
                        link(TT(att_s[:, 10 + i, 0:3], att_s[:, 3 * i + 2, 0:3], att_s[:, 6 + i, 0:3], ADD))
                        V.reciprocal(att_s[:, 8 + i, 0:3], att_s[:, 10 + i, 0:3]).then_inc(g_tok_new, 1)
                        if N0 + m >= 2:
                            dve.wait_ge(s_pv, N0 + m - 1)
                        dve.wait_ge(s_tr, N0 + m + 1)
                        V.tensor_copy(pt_meta[0:META, m % 2, :], bank[6][0:META, 0:L]).then_inc(s_ptm, 1)
                    if n >= 2 and n % 2 == 1:
                        m = n - 2
                        dve.wait_ge(s_pv, N0 + m + 1)
                        V.tensor_copy(q[:, m // 2, :], bank[7][:, 0:L]).then_inc(s_out, 1)

                def conv(c):
                    src = pre[:, c % 2, :]
                    for k in range(4):
                        w = pcol("mlstm_conv_w_2", (l * 4 + k) * NC8 + c)
                        if k == 0:
                            link(TS(qk[:, c, :], src[:, 0:L], w, pcol("mlstm_conv_b_2", l * NC8 + c), MUL, ADD))
                        else:
                            i_ = STT(out=qk[:, c, :], in0=src[:, k:k + L], scalar=w, in1=qk[:, c, :], op0=MUL, op1=ADD)
                            if k < 3:
                                link(i_)
                    i_.then_inc(conv2_new, 1)

                n = 0
                for ph in ("mqk", "mv"):
                    for p in range(4):
                        pr = PHASES[f"{ph}{l}"][1] + p
                        for U, _, _ in units_of(pr):
                            split_w(U + LEAD)
                            attention(n)
                            n += 1
                        for m in range(2):
                            c = 2 * p + m
                            if ph == "mqk":
                                if c >= 2:
                                    dve.wait_ge(conv2_new, NC8 * l + c - 1)
                                scaled(pr, m, pre[:, m, 3:3 + L], L, 0)
                            else:
                                scaled(pr, m, mv[:, c, :], L, 0)
                        if ph == "mqk":
                            dve.wait_ge(tile_read, 2 * pr + 2)
                            for m in range(2):
                                conv(2 * p + m)
                attention(16)
                attention(17)

                for c in range(NC8):
                    dve.wait_ge(mt_tr, NC8 * l + c + 1)
                    b = bank[4 + c % 4]
                    V.tensor_copy(mvt[:, 0:2, c * P:(c + 1) * P], b[:, 0:2 * P].rearrange("p (t n) -> p t n", n=P))
                    V.tensor_copy(mvt[0:16, 2, c * P:(c + 1) * P], b[0:16, 2 * P:3 * P]).then_inc(mt_read, 1)
                for hd in range(M_H):
                    n = M_H * l + hd
                    dve.wait_ge(m_bc, 2 * n + 1)
                    if n:
                        dve.wait_ge(m_nd, n)
                    for t, (a, b) in enumerate(LT):
                        mo_ = CONST_AT["mmask"] + MOFF[t]
                        i_ = TT(m_arg[0:b - a, MOFF[t]:MOFF[t] + L - a], bank[4][0:b - a, a:L], con[0:b - a, mo_:mo_ + L - a], ADD)
                    i_.then_inc(m_arg_new, 1)
                    dve.wait_ge(m_bc, 2 * n + 2)
                    dve.wait_ge(m_exp_new, n + 1)
                    W01 = MOFF[2]
                    STT(out=m_pt[:, 0:W01], in0=bank[6][:, 0:W01], scalar=QK_D ** -0.5, in1=m_arg[:, 0:W01], op0=MUL, op1=MUL)
                    STT(out=m_pt[0:16, W01:MW], in0=bank[6][0:16, W01:MW], scalar=QK_D ** -0.5, in1=m_arg[0:16, W01:MW],
                        op0=MUL, op1=MUL).then_inc(m_pt_new, 1)
                    dve.wait_ge(m_nd, n + 1)
                    dve.wait_ge(m_eb, n + 1)
                    link(TS(m_b, bank[5][:, 0:L], -1.0, None, MUL))
                    link(TT(m_b, bank[5][:, 0:L], m_b, MAX))
                    link(TT(m_b, m_b, exp_b, MAX))
                    link(V.reciprocal(m_b, m_b))
                    TT(hm[:, 2 * hd, :], bank[7][:, 0:L], m_b, MUL)
                    TT(hm[:, 2 * hd + 1, :], bank[4][:, 0:L], m_b, MUL).then_inc(m_hm, 1)
                for hd in range(M_H):
                    n = M_H * l + hd
                    dve.wait_ge(n_sqrt, n + 1)
                    t = score[:, hd % 2, 0:L]
                    link(V.reciprocal(t, t))
                    for w in range(2):
                        c = 2 * hd + w
                        i_ = STT(out=hm[:, c, :], in0=hm[:, c, :], scalar=pcol("mlstm_out_norm_g_2", l * NC8 + c), in1=t,
                                 op0=MUL, op1=MUL)
                    i_.then_inc(n_new, 1)
                dve.wait_ge(n_new, M_H * (l + 1))
                dve.wait_ge(s_out, 8 * (l + 1))
                G0 = 24 * l
                for g, ph in enumerate(("ag", "mo", "mg")):
                    pb = PHASES[f"{ph}{l}"][1]
                    dst = q if ph == "ag" else hm
                    for p in range(4):
                        ahead(pb + p)
                        for m in range(2):
                            scaled(pb + p, m, prob[:, m, 0:L], L, 0)
                        for m in range(2):
                            c = 2 * p + m
                            dve.wait_ge(gate_act, G0 + 8 * g + c + 1)
                            i_ = TT(dst[:, c, :], dst[:, c, :], prob[:, m, 0:L], MUL)
                            if ph == "mo":
                                link(i_)
                            else:
                                i_.then_inc(act_new, 1)
                        if ph != "mo":
                            for m in range(2):
                                c = 2 * p + m
                                k = c if ph == "ag" else NC8 + c
                                split_x(y_lo, y_hi, k, L, dst[:, c, :], SPLITS[f"y_proj{l}"] + k)
                out_phase(f"proj{l}", (lambda c: pcol("norm_g_2", NC8 + c)) if l == 0 else None,
                          SPLITS.get("x_kv1"), half=1.0, N=L, T0=0)
            for g in range(4):
                t, c0 = g // 2, 4 * (g % 2)
                dve.wait_ge(ot_tr, g + 1)
                V.tensor_copy(orow[:, t, c0 * P:(c0 + 4) * P], bank[4 + g][:, :]).then_inc(ot_read, 1)


_INS = ['x', 'ffn1_norm', 'ffn1_w_in', 'ffn1_w_out', 'mix_norm', 'ffn2_norm', 'ffn2_w_in', 'ffn2_w_out', 'rec_w_in',
        'rec_conv_w', 'rec_conv_b', 'rec_gate_a_w', 'rec_gate_a_b', 'rec_gate_x_w', 'rec_gate_x_b', 'rec_lambda',
        'rec_w_out', 'sg_w_in', 'sg_v_norm', 'sg_w_s', 'sg_b_s', 'sg_w_out', 'final_norm', 'meta_2', 'norm_g_2',
        'w_in_2', 'attn_q_norm_g_2', 'attn_k_norm_g_2', 'attn_sink_2', 'mlstm_conv_w_2', 'mlstm_conv_b_2',
        'mlstm_b_i_2', 'mlstm_b_f_2', 'mlstm_out_norm_g_2', 'w_out_2']
_OUTS = [((1, SEQ, D), 'float32')]


def kernel(**inputs):
    import numpy as _np
    import concourse.bacc as _bacc
    from concourse import mybir as _mybir
    from concourse.bass_utils import run_bass_kernel_spmd as _run

    nc = _bacc.Bacc("TRN2", target_bir_lowering=False, num_devices=1)
    arrays = {"in_consts_dram": constants()}
    for name in _INS:
        arrays[f"in_{name}_dram"] = _np.ascontiguousarray(inputs[name])
    args = [nc.dram_tensor(n, a.shape, _mybir.dt.from_np(a.dtype), kind="ExternalInput").ap() for n, a in arrays.items()]
    for i, (shape, dtype) in enumerate(_OUTS):
        args.append(nc.dram_tensor(f"out_{i}_dram", shape, _mybir.dt.from_np(_np.dtype(dtype)), kind="ExternalOutput").ap())
    build_stack(nc, *args)
    r = _run(nc, [arrays], core_ids=[0])
    return r.results[0]["out_0_dram"]
```

```python
import numpy as np
import concourse.bass as bass
from concourse import mybir
from contextlib import ExitStack

P = 128
D = 1024
NC8 = D // P
SEQ = 256
META = 16
L = META + SEQ
FF = 2816
NF = FF // P
DEPTH = 2
KU = 4
CU = 256
RING = 4
LEAD = 3
EPS = 1e-6
NEG = -1e30
BIG = 1e30
ATT_H, DH, M_H, QK_D = 16, 64, 4, 128
ROT = 16
IN2 = 6408
M_MIN = -41.0
WORK_SLOTS = 65
AW = 3 * P
LT = [(0, 128), (128, 256), (256, 272)]
NT = len(LT)
TAIL = 16
NR = 2 * (NC8 + 1)
MOFF = [0, L, L + (L - 128)]
MW = MOFF[2] + 16
C_AQ, C_KV, C_AG, C_MQK, C_MV, C_MIF, C_MO, C_MG = 0, 1024, 1280, 2304, 3328, 4352, 4360, 5384

CONST_W = dict(ident=P, tri=P, amask=AW, tmask=L, mmask=P, rot=P, swap=P, head_mean=2, cos=L, sin=L, sel=(NC8 + 1) * P)
CONST_AT = {}
_at = 0
for _n, _w in CONST_W.items():
    CONST_AT[_n] = _at
    _at += _w
CONST_ALL = _at


def constants():
    c = {n: np.zeros((P, w), np.float32) for n, w in CONST_W.items()}
    i = np.arange(P)
    c["ident"][i, i] = 1
    c["tri"][:] = i[:, None] <= i[None, :]

    def hidden(q, k):
        return ~((k <= q) & ((k < META) | (q - k < P)))

    c["amask"][:, :P] = NEG * hidden(i[:, None], i[None])
    c["amask"][:, P:] = NEG * hidden(P + i[:, None], np.arange(2 * P)[None])
    c["tmask"][:] = NEG * hidden(2 * P + i[:, None] % TAIL, np.arange(L)[None])
    c["mmask"][:] = BIG * (i[None] < i[:, None])
    half = ROT // 2
    for h0 in (0, DH):
        for d in range(half):
            c["rot"][h0 + half + d, h0 + d] = -1
            c["rot"][h0 + d, h0 + half + d] = 1
    c["swap"][i, (i + DH) % P] = 1
    c["head_mean"][i, i // DH] = 1.0 / DH
    inv = (500000.0 ** (-np.arange(0, ROT, 2, dtype=np.float32) / ROT)).astype(np.float32)
    ang = np.arange(L, dtype=np.float32)[None] * inv[:, None]
    c["cos"][:] = 1
    for h0 in (0, DH):
        for k in (0, half):
            c["cos"][h0 + k:h0 + k + half] = np.cos(ang)
            c["sin"][h0 + k:h0 + k + half] = np.sin(ang)
    for k in range(NC8 + 1):
        for e in range(2):
            c["sel"][2 * k + e, k * P + e * DH:k * P + (e + 1) * DH] = 1
    return np.concatenate([c[n] for n in CONST_W], 1)


PAR = {}
for _t, _rows in enumerate([
    [("ffn1_norm", 16), ("ffn2_norm", 16), ("mix_norm", 16), ("final_norm", 8), ("rec_conv_w", 32), ("rec_conv_b", 8),
     ("rec_gate_a_b", 8), ("rec_gate_x_b", 8), ("rec_lambda", 8), ("sg_v_norm", 8)],
    [("norm_g_2", 16), ("mlstm_conv_w_2", 64), ("mlstm_conv_b_2", 16), ("mlstm_out_norm_g_2", 16),
     ("attn_q_norm_g_2", 2), ("attn_k_norm_g_2", 2)],
]):
    _r = 0
    for _n, _k in _rows:
        PAR[_n] = (_t, _r, _k)
        _r += _k


def plan():
    units, pairs, phases = [], [], {}

    def phase(name, src, layer, rows, cols):
        ub, pb = len(units), len(pairs)
        for c0 in cols:
            ks = []
            k = 0
            while k < rows:
                n = min(KU, rows - k) if rows - k != 6 else 3
                ks.append((k, n))
                k += n
            pairs.append([(len(units) + j, k0, n) for j, (k0, n) in enumerate(ks)])
            units.extend((src, layer, k0, n, c0) for k0, n in ks)
        phases[name] = (ub, pb, len(cols))

    wide = range(0, D, CU)
    for l in range(DEPTH):
        for f in (1, 2):
            gate_up = [c + s * FF for c in range(0, FF, CU) for s in (0, 1)]
            phase(f"in{l}{f}", f"ffn{f}_w_in", l, NC8, gate_up)
            phase(f"out{l}{f}", f"ffn{f}_w_out", l, NF, wide)
            if f == 1:
                m = ("rec", "sg")[l]
                phase(m + "_b", m + "_w_in", 0, NC8, [D + c for c in wide])
                phase(m + "_a", m + "_w_in", 0, NC8, wide)
                phase(m + "_out", m + "_w_out", 0, NC8, wide)
    for l in range(DEPTH):
        for n, c in (("kv", [C_KV]), ("mif", [C_MIF]), ("aq", [C_AQ + c for c in wide]),
                     ("mqk", [C_MQK + c for c in wide]), ("mv", [C_MV + c for c in wide]),
                     ("mo", [C_MO + c for c in wide]), ("ag", [C_AG + c for c in wide]),
                     ("mg", [C_MG + c for c in wide])):
            phase(f"{n}{l}", "w_in_2", l, NC8, c)
        phase(f"proj{l}", "w_out_2", l, 2 * NC8, wide)
    return units, pairs, phases


UNITS, PAIRS, PHASES = plan()

STREAM = ("kv", "mif", "aq", "mqk", "mv", "mo", "ag", "mg")
STREAM_UNITS = sum(2 * PHASES[n + "0"][2] for n in STREAM)
ITEMS = [(g, hd) for g in range(2) for hd in [None, *range(8 * g, 8 * g + 8)]]
VISITS = {u: [] for u in range(STREAM_UNITS)}
for _c in range(9):
    VISITS[4 if _c == 0 else 7 + 2 * ((_c - 1) // 2)].append(("turn", _c))
VISITS[14].append(("rs", 0))
VISITS[15].append(("rt", 0))
VISITS[16].append(("kx", 0))
for _p in range(4):
    VISITS[14 + 2 * _p].insert(0, ("silu", _p))
ATT_STEPS = len(ITEMS) + 3
for _v in range(ATT_STEPS):
    VISITS[18 + _v * 17 // ATT_STEPS].append(("att", _v))
for _c in range(8):
    VISITS[23 + _c].append(("mvt", _c))
for _h in range(M_H):
    for _s, _at in enumerate((0, 2, 3, 5)):
        VISITS[min(35 + 4 * _h + _at, STREAM_UNITS - 1)].append(("ml", (_h, _s)))


def build_stack(nc: bass.Bass, consts, x, ffn1_norm, ffn1_w_in, ffn1_w_out, mix_norm, ffn2_norm, ffn2_w_in, ffn2_w_out,
                rec_w_in, rec_conv_w, rec_conv_b, rec_gate_a_w, rec_gate_a_b, rec_gate_x_w, rec_gate_x_b, rec_lambda,
                rec_w_out, sg_w_in, sg_v_norm, sg_w_s, sg_b_s, sg_w_out, final_norm, meta_2, norm_g_2, w_in_2,
                attn_q_norm_g_2, attn_k_norm_g_2, attn_sink_2, mlstm_conv_w_2, mlstm_conv_b_2, mlstm_b_i_2,
                mlstm_b_f_2, mlstm_out_norm_g_2, w_out_2, out):
    fp32, fp32r = mybir.dt.float32, mybir.dt.float32r
    ALU, ACT = mybir.AluOpType, mybir.ActivationFunctionType
    MUL, ADD, SUB, MAX, MIN = ALU.mult, ALU.add, ALU.subtract, ALU.max, ALU.min
    dram = dict(ffn1_w_in=ffn1_w_in, ffn1_w_out=ffn1_w_out, ffn2_w_in=ffn2_w_in, ffn2_w_out=ffn2_w_out,
                rec_w_in=rec_w_in, rec_w_out=rec_w_out, sg_w_in=sg_w_in, sg_w_out=sg_w_out, w_in_2=w_in_2,
                w_out_2=w_out_2)
    NU = len(UNITS)

    with ExitStack() as ctx:
        def sb(name, shape, dt=fp32):
            return ctx.enter_context(nc.sbuf_tensor(name, shape, dt))

        def sem(name):
            return ctx.enter_context(nc.semaphore(name))

        ctx.enter_context(nc.allow_non_contiguous_dma(reason="gate columns and biases of a few elements"))

        raw = sb("raw", [P, RING, KU, CU])
        w_hi = sb("w_hi", [P, RING, KU, CU], fp32r)
        w_lo = sb("w_lo", [P, RING, KU, CU], fp32r)
        h = sb("h", [P, NC8, L])
        x_hi = sb("x_hi", [P, NC8 * L], fp32r)
        x_lo = sb("x_lo", [P, NC8 * L], fp32r)
        y_hi = sb("y_hi", [P, NF * SEQ], fp32r)
        y_lo = sb("y_lo", [P, NF * SEQ], fp32r)
        con = sb("con", [P, CONST_ALL])
        ones = sb("ones", [P, P])
        par_rows = sb("par_rows", [P, 2, P])
        par = sb("par", [P, 2, P])
        rstd = sb("rstd", [P, L])
        rms = sb("rms", [P, L])
        sumsq = sb("sumsq", [P, L])
        sq = sb("sq", [P, L])
        epsc = sb("epsc", [P, 1])
        work = sb("work", [P, WORK_SLOTS * L])
        pre = sb("pre", [P, 2, L + 3])
        bank = [ctx.enter_context(nc.psum_tensor(f"bank{i}", [P, 512], fp32)) for i in range(8)]

        def cst(name, rows=P):
            return con[0:rows, CONST_AT[name]:CONST_AT[name] + CONST_W[name]]

        ident, tri = cst("ident"), cst("tri")

        def pcol(name, k, rows=P):
            t, r, _ = PAR[name]
            return par[0:rows, t, r + k:r + k + 1]

        at = [0]

        def region(slots, width=L):
            o = at[0]
            at[0] += slots * width
            assert at[0] <= WORK_SLOTS * L, at[0]
            return work[:, o:o + slots * width].rearrange("p (c n) -> p c n", n=width)

        ffn_t, ffn_s, ffn_r, ffn_h = (region(2, SEQ) for _ in range(4))
        mixer_at = at[0]
        rec_y, rec_x, rec_a, rec_g = (region(NC8, SEQ) for _ in range(4))
        rec_p = region(NC8, SEQ + 3)
        blocks_a, blocks_x = region(NC8, P), region(NC8, P)
        decay = region(12, NC8)
        ws_raw, ws_t, bs_all = region(NC8, P), region(NC8, P), region(NC8, P)
        at[0] = mixer_at
        sg_u, sg_v, sg_s = (region(NC8, SEQ) for _ in range(3))
        v_tok = region(2, D)
        sg_r = region(8, 2)
        at[0] = 0
        q = region(NC8)
        k_att, k_swap, v_att = region(1)[:, 0], region(1)[:, 0], region(1)[:, 0]
        qk = region(NC8)
        mv = region(NC8)
        mvt = region(3, D)
        prob = region(2, AW)
        score = region(2, MW)
        pt = region(2, AW)
        va_t = region(3, P)
        q_tail = region(2, P)
        cos_g = region(2)
        rot_g = region(2, P)
        qsq = score[:, :, 0:L]
        qc, qs = pt[:, :, 0:L], prob[:, :, 0:L]
        norms = region(4, NT * NR)
        r_t = region(1)[:, 0]
        att_s = region(12, 4)
        g_row = region(6)
        g_tok = region(3, 8)
        den_s = region(8, 4)
        s_b = region(1)[:, 0]
        diag = region(3, P)
        m_arg, m_pt = score[:, 0, :], score[:, 1, :]
        n_sq = pt[:, :, 0:L]
        gate_x, gate_t = prob[:, :, 0:L], region(2)
        exp_b, m_b = gate_t[:, 0, :], gate_t[:, 1, :]
        g_x2 = cos_g
        sinks = sb("sinks", [P, DEPTH * ATT_H])
        sink_tail = sb("sink_tail", [P, 2 * DEPTH])
        neg_sinks = sb("neg_sinks", [P, DEPTH * ATT_H])
        neg_tail = sb("neg_tail", [P, 2 * DEPTH])
        gbias = sb("gbias", [4, 2 * DEPTH])
        xrow = work[:, 0:3 * D].rearrange("p (t n) -> p t n", n=D)
        orow = work[:, 0:2 * D].rearrange("p (t n) -> p t n", n=D)

        w_loaded = [sem(f"w_loaded{i}") for i in range(RING)]
        hi_made = sem("hi_made")
        lo_made = sem("lo_made")
        unit_done = sem("unit_done")
        first_done = sem("first_done")
        tile_read = sem("tile_read")
        act_hi = sem("act_hi")
        act_ready = sem("act_ready")
        act_new = sem("act_new")
        silu_done = sem("silu_done")
        gate_scaled = sem("gate_scaled")
        par_loaded, con_loaded, x_loaded, blk_loaded, sg_loaded = (
            sem(n) for n in ("par_loaded", "con_loaded", "x_loaded", "blk_loaded", "sg_loaded"))
        ones_set, zero_set = sem("ones_set"), sem("zero_set")
        par_t, par_ready = sem("par_t"), sem("par_ready")
        xt_done, xt_read = sem("xt_done"), sem("xt_read")
        sq_done, sum_done, rms_done, rstd_ready = (sem(n) for n in ("sq_done", "sum_done", "rms_done", "rstd_ready"))
        pool_ch = sem("pool_ch")
        dch = sem("dch")
        ach = sem("ach")
        final_new, fin_sq = sem("final_new"), sem("fin_sq")
        conv_new, gates_mm, gates_sig, ax_new, mult2, mult_new, rec_gelu, rec_bx = (
            sem(n) for n in ("conv_new", "gates_mm", "gates_sig", "ax_new", "mult2", "mult_new", "rec_gelu", "rec_bx"))
        decay_e = sem("decay_e")
        decay_v = sem("decay_v")
        sg_gelu, sg_sum, sg_rms, ws_tr, vt_tr, vt_read, sg_mm, sg_read, ws_read, sg_rs, sg_sqs = (
            sem(n) for n in ("sg_gelu", "sg_sum", "sg_rms", "ws_tr", "vt_tr", "vt_read", "sg_mm", "sg_read", "ws_read",
                             "sg_rs", "sg_sqs"))
        qsq_new, turn_mm, rs_new, rt_mm, rt_read, k_ready, qc_new, q_ready = (
            sem(n) for n in ("qsq_new", "turn_mm", "rs_new", "rt_mm", "rt_read", "k_ready", "qc_new", "q_ready"))
        cos_ready, kx_mm, kx_read, k_swapped = sem("cos_ready"), sem("kx_mm"), sem("kx_read"), sem("k_swapped")
        tail_new = sem("tail_new")
        s_mm, s_max, s_exp, s_rec, s_prob, s_tr, s_pt, s_pv, s_out = (
            sem(n) for n in ("s_mm", "s_max", "s_exp", "s_rec", "s_prob", "s_tr", "s_pt", "s_pv", "s_out"))
        g_nx, g_e, g_cm, g_exp = (sem(n) for n in ("g_nx", "g_e", "g_cm", "g_exp"))
        tap0, conv2_new, qk_new = sem("tap0"), sem("conv2_new"), sem("qk_new")
        mt_tr, mt_read = sem("mt_tr"), sem("mt_read")
        ms_read = sem("ms_read")
        m_bc, m_qk, m_arg_new, m_exp_new, m_pt_new, m_num, m_sq, m_den, m_ms, m_diag, m_bb, m_sb, m_hm = (
            sem(n) for n in ("m_bc", "m_qk", "m_arg_new", "m_exp_new", "m_pt_new", "m_num", "m_sq", "m_den", "m_ms",
                             "m_diag", "m_bb", "m_sb", "m_hm"))
        gate_act = sem("gate_act")
        ot_tr, ot_read, stored = sem("ot_tr"), sem("ot_read"), sem("stored")

        block = ctx.enter_context(nc.Block())

        NORMS = ["in01", "rec_b", "in02", "in11", "sg_b", "in12", "final", "kv0", "kv1"]
        def xview(t, k, n):
            return t[:, k * n:(k + 1) * n]

        SPLITS = {}
        cnt = 0
        for name, k in [("x_in01", 8), ("y_out01", NF), ("x_rec_b", 8), ("y_rec_out", 8), ("x_in02", 8), ("y_out02", NF),
                        ("x_in11", 8), ("y_out11", NF), ("x_sg_b", 8), ("y_sg_out", 8), ("x_in12", 8), ("y_out12", NF),
                        ("x_kv0", 8), ("y_proj0", 16), ("x_kv1", 8), ("y_proj1", 16)]:
            SPLITS[name] = cnt
            cnt += k

        def units_of(pair):
            return PAIRS[pair]

        @block.sync
        def _(sp):
            sp.dma_start(xrow[:, 0:2, :], x[0].rearrange("(t p) d -> p t d", p=P)).then_inc(x_loaded, 16)
            sp.dma_start(xrow[0:META, 2, :], meta_2).then_inc(x_loaded, 16)
            sp.dma_start(con[:, :], consts).then_inc(con_loaded, 16)
            rows = dict(ffn1_norm=ffn1_norm, ffn2_norm=ffn2_norm, mix_norm=mix_norm,
                        rec_conv_b=rec_conv_b, rec_lambda=rec_lambda, sg_v_norm=sg_v_norm, norm_g_2=norm_g_2,
                        mlstm_conv_b_2=mlstm_conv_b_2, mlstm_out_norm_g_2=mlstm_out_norm_g_2)
            srcs = {n: a.rearrange("l (c p) -> (l c) p", p=P) for n, a in rows.items()}
            srcs["final_norm"] = final_norm.rearrange("(c p) -> c p", p=P)
            srcs["rec_conv_w"] = rec_conv_w[0].rearrange("k (c p) -> (k c) p", p=P)
            srcs["mlstm_conv_w_2"] = mlstm_conv_w_2.rearrange("l k (c p) -> (l k c) p", p=P)
            for n, a in (("rec_gate_a_b", rec_gate_a_b), ("rec_gate_x_b", rec_gate_x_b)):
                srcs[n] = a[0].rearrange("(c e) d -> c (e d)", e=2)
            for n, src in srcs.items():
                t, r, k = PAR[n]
                sp.dma_start(par_rows[r:r + k, t, :], src).then_inc(par_loaded, 16)
            for n, src in (("attn_q_norm_g_2", attn_q_norm_g_2), ("attn_k_norm_g_2", attn_k_norm_g_2)):
                t, r, k = PAR[n]
                for e in range(2):
                    sp.dma_start(par_rows[r:r + k, t, e * DH:(e + 1) * DH], src).then_inc(par_loaded, 16)

            def load(U, src, wait):
                n = UNITS[U][3]
                if wait is not None:
                    sp.wait_ge(lo_made, wait)
                sp.dma_start(raw[:, U % RING, 0:n, :], src).then_inc(w_loaded[U % RING], 16)

            def straight(name, first=0):
                ub, pb, npairs = PHASES[name]
                for pr in range(pb + first, pb + npairs):
                    for U, _, n in PAIRS[pr]:
                        src, l, k0, n, c0 = UNITS[U]
                        a = dram[src][l]
                        if name.startswith("mif"):
                            sp.wait_ge(lo_made, U - RING + 1)
                            for g in range(2):
                                sp.dma_start(raw[:, U % RING, 0:n, 32 * g:32 * g + 4],
                                             a[k0 * P:(k0 + n) * P, c0 + 4 * g:c0 + 4 * g + 4].rearrange(
                                                 "(k p) n -> p k n", p=P)).then_inc(w_loaded[U % RING], 16)
                            continue
                        load(U, a[k0 * P:(k0 + n) * P, c0:c0 + CU].rearrange("(k p) n -> p k n", p=P),
                             U - RING + 1 if U >= RING else None)

            def gate_up(name):
                ub, pb, _ = PHASES[name]
                src, l, _, _, _ = UNITS[ub]
                cols = dram[src][l].rearrange("(s k p) (f j n) -> s f j p k n", k=KU, p=P, f=2, n=CU)
                first = 1 if ub == 0 else 0

                def turn(i):
                    for j in range(4):
                        U = ub + j
                        wait = U - RING + 1 + 4 * i
                        load(U, cols[j % 2, j // 2, i], None if isinstance(i, int) and wait <= 0 else wait)

                if first:
                    turn(0)
                with sp.Fori(first, FF // CU) as i:
                    turn(i)

            gate_up_first = True
            sp.wait_ge(zero_set, 1)
            for dst, src in ((blocks_a, rec_gate_a_w), (blocks_x, rec_gate_x_w)):
                for e in range(2):
                    sp.dma_start(dst[e * DH:(e + 1) * DH, :, e * DH:(e + 1) * DH],
                                 src[0].rearrange("(c e) i j -> e i c j", e=2)[e]).then_inc(blk_loaded, 16)
            gate_up("in01")
            sp.dma_start(ws_raw[:, :, :], sg_w_s[0].rearrange("h p q -> p h q")).then_inc(sg_loaded, 16)
            sp.dma_start(bs_all[:, :, :], sg_b_s[0].rearrange("(o h) p -> o h p", o=1).broadcast_to((P, NC8, P))).then_inc(sg_loaded, 16)
            for l in range(DEPTH):
                heads = attn_sink_2[l].rearrange("(g c e) -> g e c", g=2, e=2)
                for g in range(2):
                    for e in range(2):
                        src = heads[g, e].rearrange("(c o) -> c o", o=1).broadcast_to((4, TAIL))
                        dst = sink_tail[e * DH:(e + 1) * DH, 2 * l + g:2 * l + g + 1]
                        for c in range(4):
                            sp.dma_start(dst[c * TAIL:(c + 1) * TAIL, :], src[c:c + 1, :].rearrange("c t -> t c")).then_inc(sg_loaded, 16)
            sp.dma_start(sinks[:, :], attn_sink_2.rearrange("(o l) h -> o (l h)", o=1).broadcast_to((P, DEPTH * ATT_H))).then_inc(sg_loaded, 16)
            for g, src in enumerate((mlstm_b_i_2, mlstm_b_f_2)):
                sp.dma_start(gbias[:, g * DEPTH:(g + 1) * DEPTH], src.rearrange("l h -> h l")).then_inc(sg_loaded, 16)
            straight("out01")
            for n in ("rec_b", "rec_a", "rec_out"):
                straight(n)
            gate_up("in02")
            straight("out02")
            gate_up("in11")
            straight("out11")
            for n in ("sg_b", "sg_a", "sg_out"):
                straight(n)
            gate_up("in12")
            straight("out12")
            for l in range(DEPTH):
                for n in (*STREAM, "proj"):
                    straight(f"{n}{l}")
            sp.wait_ge(ot_read, 4)
            sp.dma_start(out[0].rearrange("(t p) d -> p t d", p=P), orow[:, :, :]).then_inc(stored, 16)
            sp.wait_ge(stored, 16)

        SG_LOADS = 16 * (2 + 16 * DEPTH + 3)
        MIF_UNITS = {U for l in range(DEPTH) for U, _, _ in PAIRS[PHASES[f"mif{l}"][1]]}
        LANDED = {}
        _c = [0] * RING
        for U in range(NU):
            _c[U % RING] += 32 if U in MIF_UNITS else 16
            LANDED[U] = _c[U % RING]
        LOOPED = {name: PHASES[name] for name in ("in01", "in02", "in11", "in12")}

        @block.tensor
        def _(pe):
            mm = nc.tensor.matmul

            def unit(U, k0, n, pair, npair_off, xs, N, first, last, ready, off, tiles=2, wide_x=False):
                hi, lo = xs
                pe.wait_ge(lo_made, U + 1 + off)
                s = U % RING
                for m in range(tiles):
                    T = 2 * pair + m
                    acc = bank[T % 4][:, 0:N]
                    if first and not (isinstance(off, int) and T - 3 + off // 2 <= 0):
                        pe.wait_ge(tile_read, T - 3 + tile_off(off))
                    for j in range(n):
                        k = k0 + j
                        if m == 0 and ready is not None:
                            pe.wait_ge(act_ready, ready + k + 1)
                        wh, wl = (t[:, s, j, m * P:(m + 1) * P] for t in (w_hi, w_lo))
                        if N == SEQ and wide_x:
                            xh, xl = (t[:, k * L + META:(k + 1) * L] for t in (hi, lo))
                        else:
                            xh, xl = xview(hi, k, N), xview(lo, k, N)
                        mm(acc, wh, xh, start=first and j == 0, stop=False)
                        mm(acc, wh, xl, start=False, stop=False)
                        i_ = mm(acc, wl, xh, start=False, stop=last and j == n - 1)
                    if last and m == 0 and tiles == 2:
                        i_.then_inc(first_done, 1)
                i_.then_inc(unit_done, 1)

            def tile_off(off):
                return off // 2 if isinstance(off, int) else off_half[0]

            off_half = [0]

            def pair(pr, xs, N, ready=None, after=None, tiles=2, wide_x=False):
                us = units_of(pr)
                for j, (U, k0, n) in enumerate(us):
                    unit(U, k0, n, pr, 0, xs, N, j == 0, j == len(us) - 1, ready, 0, tiles, wide_x)
                    if after is not None:
                        after(j)

            xs, ys = (x_hi, x_lo), (y_hi, y_lo)

            def norm_sum(n, T0):
                pe.wait_ge(sq_done, n + 1)
                mm(bank[4][:, T0:L], ones[:, :], sumsq[:, T0:L], start=True, stop=True).then_inc(sum_done, 1)

            def in_phase(name, n, ready):
                ub, pb, _ = PHASES[name]
                for p in range(2):
                    pair(pb + p, xs, SEQ, ready=ready if p == 0 else None,
                         after=(lambda j: norm_sum(n, META) if j == 0 else None) if p == 0 else None)
                with pe.Fori(1, FF // CU) as i:
                    off_half[0] = 4 * i
                    for p in range(2):
                        us = units_of(pb + p)
                        for j, (U, k0, nk) in enumerate(us):
                            unit(U, k0, nk, pb + p, 0, xs, SEQ, j == 0, j == 1, None, 4 * i)

            def out_phase(name, ready, N=SEQ, after=None):
                ub, pb, npairs = PHASES[name]
                for p in range(npairs):
                    pair(pb + p, ys, N, ready=ready if p == 0 else None)

            pe.wait_ge(ones_set, 1)
            pe.wait_ge(con_loaded, 16)
            pe.wait_ge(par_loaded, 16 * 18)
            for t in range(2):
                rows = sum(k for (tt, _, k) in PAR.values() if tt == t)
                i_ = nc.tensor.transpose(bank[4][:, t * P:t * P + rows], par_rows[0:rows, t, :], ident[0:rows, 0:rows])
            i_.then_inc(par_t, 1)
            pe.wait_ge(x_loaded, 32)
            for c in range(NC8):
                b = bank[c % 4]
                if c >= 4:
                    pe.wait_ge(xt_read, c - 3)
                nc.tensor.transpose(b[:, 0:META], xrow[0:META, 2, c * P:(c + 1) * P], ident[0:META, 0:META])
                for t in range(2):
                    i_ = nc.tensor.transpose(b[:, META + t * P:META + (t + 1) * P], xrow[:, t, c * P:(c + 1) * P], ident)
                i_.then_inc(xt_done, 1)
            pe.wait_ge(xt_read, NC8)
            pe.wait_ge(par_ready, 1)

            in_phase("in01", 0, SPLITS["x_in01"])
            out_phase("out01", SPLITS["y_out01"])

            ub, pb, _ = PHASES["rec_b"]
            for p in range(4):
                pair(pb + p, xs, SEQ, ready=SPLITS["x_rec_b"] if p == 0 else None,
                     after=(lambda j: norm_sum(1, META) if j == 0 else None) if p == 0 else None)
            ub, pb, _ = PHASES["rec_a"]
            pair(pb, xs, SEQ)
            pe.wait_ge(blk_loaded, 64)
            for c in range(NC8):
                pe.wait_ge(conv_new, c + 1)
                if c >= 4:
                    pe.wait_ge(gates_sig, 2 * (c - 3))
                mm(bank[4 + c % 4][:, 0:SEQ], blocks_a[:, c, :], rec_x[:, c, :], start=True, stop=True)
                mm(bank[4 + c % 4][:, SEQ:2 * SEQ], blocks_x[:, c, :], rec_x[:, c, :], start=True,
                   stop=True).then_inc(gates_mm, 1)
            for p in range(1, 4):
                pair(pb + p, xs, SEQ)
            out_phase("rec_out", SPLITS["y_rec_out"])

            in_phase("in02", 2, SPLITS["x_in02"])
            out_phase("out02", SPLITS["y_out02"])
            in_phase("in11", 3, SPLITS["x_in11"])
            out_phase("out11", SPLITS["y_out11"])

            ub, pb, _ = PHASES["sg_b"]
            for p in range(4):
                pair(pb + p, xs, SEQ, ready=SPLITS["x_sg_b"] if p == 0 else None,
                     after=(lambda j: norm_sum(4, META) if j == 0 else None) if p == 0 else None)
                if p == 0:
                    pe.wait_ge(sg_loaded, SG_LOADS)
                    for c in range(NC8):
                        i_ = nc.tensor.transpose(bank[5 + c // 4][:, (c % 4) * P:(c % 4 + 1) * P], ws_raw[:, c, :], ident)
                    i_.then_inc(ws_tr, 1)
            ub, pb, _ = PHASES["sg_a"]
            pair(pb, xs, SEQ)
            pe.wait_ge(sg_sqs, 1)
            pe.wait_ge(rms_done, 5)
            for t in range(2):
                i_ = mm(bank[4][:, t:t + 1], sumsq[:, META + t * P:META + (t + 1) * P], ones[:, 0:1], start=True, stop=True)
            i_.then_inc(sg_sum, 1)
            pe.wait_ge(ws_read, 2)
            for g in range(4):
                t, c0 = g // 2, 4 * (g % 2)
                if g == 3:
                    pe.wait_ge(vt_read, 1)
                for c in range(c0, c0 + 4):
                    i_ = nc.tensor.transpose(bank[5 + g % 3][:, (c % 4) * P:(c % 4 + 1) * P],
                                             sg_v[:, c, t * P:(t + 1) * P], ident)
                i_.then_inc(vt_tr, 1)
            pair(pb + 1, xs, SEQ)
            for c in range(NC8):
                if c == 0:
                    pe.wait_ge(vt_read, 4)
                if c >= 4:
                    pe.wait_ge(sg_read, c - 3)
                for t in range(2):
                    i_ = mm(bank[4 + c % 4][:, t * P:(t + 1) * P], v_tok[:, t, c * P:(c + 1) * P], ws_t[:, c, :],
                            start=True, stop=True)
                i_.then_inc(sg_mm, 1)
            for p in range(2, 4):
                pair(pb + p, xs, SEQ)
            out_phase("sg_out", SPLITS["y_sg_out"])

            in_phase("in12", 5, SPLITS["x_in12"])
            out_phase("out12", SPLITS["y_out12"])
            norm_sum(6, META)

            tr = nc.tensor.transpose
            for l in range(DEPTH):
                I0 = len(ITEMS) * l

                def turn(c):
                    n = 9 * l + c
                    if c == 0:
                        pe.wait_ge(rms_done, 8 + l)
                        if l:
                            pe.wait_ge(m_hm, M_H * l)
                    pe.wait_ge(qsq_new, n + 1)
                    for t, (a, b) in enumerate(LT):
                        at = NR * t + 2 * c
                        mm(bank[4][0:b - a, at:at + 2], qsq[:, n % 2, a:b], cst("head_mean"), start=True, stop=True)
                    pe.wait_ge(qc_new, n + 1)
                    pe.wait_ge(cos_ready, l + 1)
                    if c >= 2:
                        pe.wait_ge(q_ready, n - 1)
                    mm(bank[5 + n % 2][:, 0:L], rot_g[:, 0 if c else 1, :], qs[:, n % 2, :], start=True,
                       stop=True).then_inc(turn_mm, 1)

                def rt():
                    pe.wait_ge(rs_new, l + 1)
                    pe.wait_ge(q_ready, 9 * (l + 1))
                    for t, (a, b) in enumerate(LT):
                        i_ = tr(bank[5][0:NR, a:b], norms[0:b - a, 3, NR * t:NR * (t + 1)], ident[0:b - a, 0:b - a])
                    i_.then_inc(rt_mm, 1)
                    pe.wait_ge(rt_read, l + 1)
                    at = CONST_AT["sel"]
                    mm(bank[6][:, 0:L], con[0:NR, at:at + P], r_t[0:NR, :], start=True, stop=True)
                    for c in range(NC8):
                        at = CONST_AT["sel"] + (c + 1) * P
                        i_ = mm(bank[7][:, c * TAIL:(c + 1) * TAIL], con[0:NR, at:at + P], r_t[0:NR, 2 * P:L], start=True,
                                stop=True)
                    i_.then_inc(rt_mm, 1)

                def kx():
                    pe.wait_ge(k_ready, l + 1)
                    mm(bank[4][:, 0:L], cst("swap"), k_att, start=True, stop=True)
                    for t, (a, b) in enumerate(LT):
                        tr(bank[5][0:b - a, t * P:(t + 1) * P], v_att[:, a:b], ident)
                    pe.wait_ge(g_exp, l + 1)
                    for t, (a, b) in enumerate(LT):
                        for w, r in enumerate((3, 5)):
                            at = 3 * P + 8 * t + 4 * w
                            i_ = tr(bank[5][0:b - a, at:at + 4], g_row[0:4, r, a:b], ident[0:4, 0:4])
                    i_.then_inc(kx_mm, 1)

                def att(v):
                    if v < len(ITEMS):
                        g, hd = ITEMS[v]
                        n = I0 + v
                        if v == 0:
                            pe.wait_ge(k_swapped, l + 1)
                            pe.wait_ge(kx_read, l + 1)
                        else:
                            pe.wait_ge(s_max, n)
                        if hd is None:
                            pe.wait_ge(tail_new, 2 * l + g + 1)
                            rows = slice(g * DH, (g + 1) * DH)
                            i_ = mm(bank[4][:, 0:L], q_tail[rows, g, :], k_att[rows, :], start=True, stop=True)
                        else:
                            e = hd % 2
                            rows = slice(e * DH, (e + 1) * DH)
                            kk = k_att if g == e else k_swap
                            qh = q[rows, hd // 2, :]
                            mm(bank[4][:, 0:P], qh[:, 0:P], kk[rows, 0:P], start=True, stop=True)
                            i_ = mm(bank[4][:, P:3 * P], qh[:, P:2 * P], kk[rows, 0:2 * P], start=True, stop=True)
                        i_.then_inc(s_mm, 1)
                    if v >= 3:
                        g, hd = ITEMS[v - 3]
                        n = I0 + v - 3
                        vc = slice(g * DH, (g + 1) * DH)
                        p = pt[:, (v - 3) % 2, :]
                        pe.wait_ge(s_pt, n + 1)
                        if hd is None:
                            if n > 0:
                                pe.wait_ge(s_out, (n // 9) * 5)
                            for e in range(2):
                                o, cols = bank[7][e * DH:(e + 1) * DH, 0:DH], slice(e * DH, (e + 1) * DH)
                                mm(o, va_t[:, 0, vc], p[:, 0:P][:, cols], start=True, stop=False)
                                mm(o, va_t[:, 1, vc], p[:, P:2 * P][:, cols], start=False, stop=False)
                                i_ = mm(o, va_t[0:TAIL, 2, vc], p[0:TAIL, 2 * P:3 * P][:, cols], start=False, stop=True)
                        else:
                            e = hd % 2
                            if e == 0:
                                pe.wait_ge(s_out, (n // 9) * 5 + 1 + (n % 9 - 1) // 2)
                            o = bank[7][e * DH:(e + 1) * DH, :]
                            mm(o[:, 0:2 * P], va_t[:, 0, vc], p[:, 0:2 * P], start=True, stop=False)
                            i_ = mm(o[:, P:2 * P], va_t[:, 1, vc], p[:, 2 * P:3 * P], start=False, stop=True)
                        i_.then_inc(s_pv, 1)
                    if 2 <= v <= len(ITEMS) + 1:
                        g, hd = ITEMS[v - 2]
                        n = I0 + v - 2
                        p = prob[:, v % 2, :]
                        pe.wait_ge(s_prob, n + 1)
                        if v >= 3:
                            pe.wait_ge(s_pt, n)
                        for j in range(3):
                            if hd is None and j == 2:
                                i_ = tr(bank[5][0:TAIL, 2 * P:3 * P], p[:, 2 * P:2 * P + TAIL], ident)
                            else:
                                i_ = tr(bank[5][:, j * P:(j + 1) * P], p[:, j * P:(j + 1) * P], ident)
                        i_.then_inc(s_tr, 1)

                def mvt_chunk(c):
                    n = NC8 * l + c
                    pe.wait_ge(tile_read, 2 * PHASES[f"mv{l}"][1] + c + 1)
                    if n:
                        pe.wait_ge(mt_read, n)
                    for t, (a, b) in enumerate(LT):
                        i_ = tr(bank[6][0:b - a, t * P:(t + 1) * P], mv[:, c, a:b], ident)
                    i_.then_inc(mt_tr, 1)

                def ml(hd, stage):
                    n = M_H * l + hd
                    if stage == 0:
                        if hd == 0:
                            pe.wait_ge(qk_new, NC8 * (l + 1))
                            pe.wait_ge(s_max, I0 + len(ITEMS))
                            pe.wait_ge(s_pt, I0 + len(ITEMS))
                        else:
                            pe.wait_ge(ms_read, n)
                        mm(bank[4][:, 0:L], ident[0:4, hd:hd + 1].broadcast_to((4, P)), g_row[0:4, 4, :], start=True,
                           stop=True).then_inc(m_bc, 1)
                        for t, (a, b) in enumerate(LT):
                            i_ = mm(bank[5][0:b - a, MOFF[t]:MOFF[t] + L - a], qk[:, 4 + hd, a:b], qk[:, hd, a:L],
                                    start=True, stop=True)
                        i_.then_inc(m_qk, 1)
                    if stage == 1:
                        pe.wait_ge(m_pt_new, n + 1)
                        if hd == 0:
                            pe.wait_ge(mt_read, NC8 * (l + 1))
                            pe.wait_ge(s_out, 10 * (l + 1))
                        else:
                            pe.wait_ge(m_hm, n)
                        for w in range(2):
                            for t, (a, b) in enumerate(LT):
                                at = (2 * hd + w) * P
                                mm(bank[6 + w][:, a:L], mvt[0:b - a, t, at:at + P], m_pt[0:b - a, MOFF[t]:MOFF[t] + L - a],
                                   start=t == 0, stop=t == 2)
                        for j, (ja, jb) in enumerate(LT):
                            for t, (a, b) in enumerate(LT[:j + 1]):
                                at = MOFF[t] + ja - a
                                i_ = mm(bank[4][0:jb - ja, 400 + j:401 + j], m_pt[0:b - a, at:at + jb - ja],
                                        ones[0:b - a, 0:1], start=t == 0, stop=t == j)
                        i_.then_inc(m_num, 1)
                    if stage == 2:
                        pe.wait_ge(m_sq, n + 1)
                        pe.wait_ge(m_den, n + 1)
                        for j, (a, b) in enumerate(LT):
                            for w in range(2):
                                i_ = mm(bank[4][0:b - a, 408 + j:409 + j], n_sq[:, w, a:b], ones[:, 0:1], start=w == 0,
                                        stop=w == 1)
                        i_.then_inc(m_ms, 1)
                    if stage == 3:
                        pe.wait_ge(m_diag, n + 1)
                        if hd < M_H - 1:
                            pe.wait_ge(m_pt_new, n + 2)
                        for j, (a, b) in enumerate(LT):
                            i_ = mm(bank[5][:, a:b], ones[0:b - a, :], diag[0:b - a, j, 0:b - a], start=True, stop=True)
                        i_.then_inc(m_bb, 1)

                do = dict(turn=turn, rs=lambda n: None, rt=lambda n: rt(), kx=lambda n: kx(), att=att,
                          silu=lambda n: None, mvt=mvt_chunk, ml=lambda hs: ml(*hs))
                u = [0]

                def visits(j):
                    if l == 0 and u[0] == 1:
                        for c in range(NC8):
                            pe.wait_ge(fin_sq, c + 1)
                            i_ = mm(bank[4][:, 0:L], ones[:, :], mv[:, c, :], start=c == 0, stop=c == NC8 - 1)
                        i_.then_inc(sum_done, 1)
                    if l == 1 and u[0] == 0:
                        norm_sum(7, 0)
                    for kind, n in VISITS[u[0]]:
                        do[kind](n)
                    u[0] += 1

                for ph in STREAM:
                    pb = PHASES[f"{ph}{l}"][1]
                    narrow = l == DEPTH - 1 and ph in ("aq", "mo", "ag", "mg")
                    for p in range(PHASES[f"{ph}{l}"][2]):
                        pair(pb + p, xs, SEQ if narrow else L, ready=SPLITS[f"x_kv{l}"] if ph == "kv" else None,
                             after=visits, tiles=1 if ph == "mif" else 2, wide_x=narrow)
                pb = PHASES[f"proj{l}"][1]
                narrow = l == DEPTH - 1
                for p in range(4):
                    pair(pb + p, ys, SEQ if narrow else L, ready=SPLITS[f"y_proj{l}"] if p == 0 else None, wide_x=narrow)

            last_tile = 2 * len(PAIRS)
            for g in range(4):
                t, c0 = g // 2, 4 * (g % 2)
                pe.wait_ge(tile_read, last_tile)
                for c in range(c0, c0 + 4):
                    i_ = nc.tensor.transpose(bank[4 + g][:, (c % 4) * P:(c % 4 + 1) * P],
                                             h[:, c, META + t * P:META + (t + 1) * P], ident)
                i_.then_inc(ot_tr, 1)

        @block.scalar
        def _(act):
            activation = nc.scalar.activation
            chain = [0]

            def split_w(U, off=0):
                if U >= NU:
                    return
                n, s = UNITS[U][3], U % RING
                act.wait_ge(w_loaded[s], LANDED[U] + (off * 4 if not isinstance(off, int) else 4 * off))
                if not (isinstance(off, int) and U - RING + 1 + off <= 0):
                    act.wait_ge(unit_done, U - RING + 1 + off)
                nc.scalar.copy(w_hi[:, s, 0:n, :], raw[:, s, 0:n, :]).then_inc(hi_made, 1)

            def split_x(dst, k, N, src, scale=None):
                if scale is None:
                    i_ = nc.scalar.copy(xview(dst, k, N), src)
                else:
                    i_ = activation(xview(dst, k, N), src, ACT.Copy, scale=scale)
                i_.then_inc(act_hi, 1)

            def ahead(pr):
                for U, _, _ in units_of(pr):
                    split_w(U + LEAD)

            def root(n, T0):
                act.wait_ge(sum_done, n + 1)
                activation(rms[:, T0:L], bank[4][:, T0:L], ACT.Sqrt, scale=1.0 / D, bias=epsc[:, 0:1]).then_inc(rms_done, 1)

            def gate_turn(pb, ub, i, first=None):
                o4, o = 4 * i, (4 * i if not isinstance(i, int) else 4 * i)
                for U in (ub, ub + 1):
                    split_w(U + LEAD, o)
                if first is not None:
                    root(first, META)
                for m in range(2):
                    act.wait_ge(tile_read, 2 * pb + m + 1 + o4)
                    activation(ffn_s[:, m, :], ffn_t[:, m, :], ACT.Silu).then_inc(silu_done, 1)
                for U in (ub + 2, ub + 3):
                    split_w(U + LEAD, o)
                for m in range(2):
                    act.wait_ge(tile_read, 2 * pb + 2 + m + 1 + o4)
                    if isinstance(i, int):
                        dst = xview(y_hi, 2 * i + m, SEQ)
                    else:
                        dst = y_hi[:, bass.ds(i * (2 * SEQ) + m * SEQ, SEQ)]
                        act.wait_ge(tile_read, 1)
                    nc.scalar.copy(dst, ffn_h[:, m, :]).then_inc(act_hi, 1)

            def in_phase(name, n):
                ub, pb, _ = PHASES[name]
                gate_turn(pb, ub, 0, first=n)
                with act.Fori(1, FF // CU) as i:
                    gate_turn(pb, ub, i)

            def out_phase(name, g, N=SEQ, T0=META, before=None):
                ub, pb, npairs = PHASES[name]
                for p in range(npairs):
                    for U, _, _ in units_of(pb + p):
                        split_w(U + LEAD)
                        if before is not None:
                            before()
                            before = None
                    for m in range(2):
                        c = 2 * p + m
                        act.wait_ge(tile_read, 2 * (pb + p) + m + 1)
                        if g is not None:
                            split_x(x_hi, c, N, h[:, c, T0:L], g(c))

            act.wait_ge(par_ready, 1)
            act.wait_ge(decay_v, 1)
            activation(decay[:, 1, :], decay[:, 0, :], ACT.Exp).then_inc(decay_e, 1)
            for c in range(NC8):
                act.wait_ge(xt_read, c + 1)
                split_x(x_hi, c, SEQ, h[:, c, META:L], pcol("ffn1_norm", c))
            for U in range(LEAD):
                split_w(U)
            in_phase("in01", 0)
            out_phase("out01", lambda c: pcol("mix_norm", c))

            _, pb, _ = PHASES["rec_b"]
            for p in range(4):
                ahead(pb + p)
                if p == 0:
                    root(1, META)
            _, pb, _ = PHASES["rec_a"]
            T = 2 * pb
            ahead(pb)
            for c in range(NC8):
                act.wait_ge(gates_mm, c + 1)
                activation(rec_a[:, c, :], bank[4 + c % 4][:, 0:SEQ], ACT.Sigmoid,
                           bias=pcol("rec_gate_a_b", c)).then_inc(gates_sig, 1)
                activation(rec_g[:, c, :], bank[4 + c % 4][:, SEQ:2 * SEQ], ACT.Sigmoid,
                           bias=pcol("rec_gate_x_b", c)).then_inc(gates_sig, 1)
                if c == 3:
                    ahead(pb + 1)
            for c in range(NC8):
                act.wait_ge(gates_sig, 2 * c + 1)
                if c == 0:
                    act.wait_ge(decay_v, 2)
                if c >= 2:
                    act.wait_ge(mult2, c - 1)
                activation(ffn_t[:, c % 2, :], rec_a[:, c, :], ACT.Tanh, scale=decay[:, 3, c:c + 1]).then_inc(ach, 1)
                chain[0] += 1
                act.wait_ge(ach, chain[0])
                activation(rec_a[:, c, :], rec_a[:, c, :], ACT.Exp, scale=decay[:, 2, c:c + 1]).then_inc(ax_new, 1)
                if c == 3:
                    ahead(pb + 2)
            for c in range(NC8):
                act.wait_ge(mult2, c + 1)
                activation(rec_p[:, c, 0:SEQ], rec_p[:, c, 0:SEQ], ACT.Sqrt).then_inc(mult_new, 1)
            ahead(pb + 3)
            for c in range(NC8):
                act.wait_ge(tile_read, T + c + 1)
                activation(rec_y[:, c, :], rec_y[:, c, :], ACT.Gelu_apprx_tanh).then_inc(rec_gelu, 1)
            for c in range(NC8):
                act.wait_ge(act_new, c + 1)
                split_x(y_hi, c, SEQ, rec_y[:, c, :])
            out_phase("rec_out", lambda c: pcol("ffn2_norm", c))

            in_phase("in02", 2)
            out_phase("out02", lambda c: pcol("ffn1_norm", NC8 + c))
            in_phase("in11", 3)
            out_phase("out11", lambda c: pcol("mix_norm", NC8 + c))

            _, pb, _ = PHASES["sg_b"]
            for p in range(4):
                ahead(pb + p)
                if p == 0:
                    root(4, META)
                for m in range(2):
                    c = 2 * p + m
                    act.wait_ge(tile_read, 2 * pb + c + 1)
                    activation(sg_v[:, c, :], sg_v[:, c, :], ACT.Gelu_apprx_tanh).then_inc(sg_gelu, 1)
            _, pb, _ = PHASES["sg_a"]
            for p in range(4):
                ahead(pb + p)
                if p == 0:
                    act.wait_ge(sg_sum, 1)
                    activation(sg_r[:, 0, :], bank[4][:, 0:2], ACT.Sqrt, scale=1.0 / D, bias=epsc[:, 0:1]).then_inc(sg_rms, 1)
                for m in range(2):
                    c = 2 * p + m
                    act.wait_ge(tile_read, 2 * pb + c + 1)
                    activation(sg_u[:, c, :], sg_u[:, c, :], ACT.Gelu_apprx_tanh).then_inc(sg_gelu, 1)
            for c in range(NC8):
                act.wait_ge(act_new, NC8 + c + 1)
                split_x(y_hi, c, SEQ, sg_s[:, c, :])
            out_phase("sg_out", lambda c: pcol("ffn2_norm", NC8 + c))

            in_phase("in12", 5)
            out_phase("out12", None)
            root(6, META)
            for c in range(NC8):
                act.wait_ge(final_new, c + 1)
                split_x(x_hi, c, L, h[:, c, :], pcol("norm_g_2", c))
                activation(mv[:, c, :], h[:, c, :], ACT.Square).then_inc(fin_sq, 1)

            for l in range(DEPTH):
                I0 = len(ITEMS) * l
                T0 = META if l == DEPTH - 1 else 0

                def turn(c):
                    n = 9 * l + c
                    src = k_att if c == 0 else q[:, c - 1, :]
                    act.wait_ge(tile_read, 2 * PHASES[f"kv{l}"][1] + 1 if c == 0 else 2 * PHASES[f"aq{l}"][1] + c)
                    if n >= 2:
                        act.wait_ge(turn_mm, n - 1)
                    if c == 0 and l:
                        act.wait_ge(m_hm, M_H * l)
                    activation(qsq[:, n % 2, :], src, ACT.Square).then_inc(qsq_new, 1)

                def rt():
                    act.wait_ge(rt_mm, 2 * l + 1)
                    nc.scalar.copy(r_t[0:NR, :], bank[5][0:NR, 0:L]).then_inc(rt_read, 1)

                def kx():
                    act.wait_ge(kx_mm, l + 1)
                    nc.scalar.copy(k_swap, bank[4][:, 0:L]).then_inc(k_swapped, 1)

                def att(v):
                    if v < len(ITEMS):
                        g, hd = ITEMS[v]
                        n = I0 + v
                        i = v % 2
                        act.wait_ge(s_max, n + 1)
                        if v >= 2:
                            act.wait_ge(s_tr, n - 1)
                        s, pr = score[:, i, :], prob[:, i, :]
                        nm, den, es = att_s[:, 3 * i + 1, :], att_s[:, 3 * i + 2, :], att_s[:, 6 + i, :]
                        sink = sink_tail[:, 2 * l + g:2 * l + g + 1] if hd is None else sinks[:, l * ATT_H + hd:l * ATT_H + hd + 1]
                        activation(es[:, 0:2], nm[:, 0:2], ACT.Exp, bias=sink)
                        rq = [norms[:, 3, NR * t + 2 + hd:NR * t + 3 + hd] for t in range(2)] if hd is not None else None
                        if hd is None:
                            i_ = activation(pr[:, 0:L], s[:, 0:L], ACT.Exp, bias=nm[:, 0:1], accum_out=den[:, 0:1])
                        else:
                            activation(pr[:, 0:P], s[:, 0:P], ACT.Exp, scale=rq[0], bias=nm[:, 0:1], accum_out=den[:, 0:1])
                            i_ = activation(pr[:, P:AW], s[:, P:AW], ACT.Exp, scale=rq[1], bias=nm[:, 1:2],
                                            accum_out=den[:, 1:2])
                        i_.then_inc(s_exp, 1)
                    if 2 <= v <= len(ITEMS) + 1:
                        g, hd = ITEMS[v - 2]
                        n = I0 + v - 2
                        act.wait_ge(s_tr, n + 1)
                        if v >= 4:
                            act.wait_ge(s_pv, n - 1)
                        dst = pt[:, v % 2, :]
                        if hd is None:
                            nc.scalar.copy(dst[:, 0:2 * P], bank[5][:, 0:2 * P])
                            i_ = nc.scalar.copy(dst[0:TAIL, 2 * P:AW], bank[5][0:TAIL, 2 * P:AW])
                        else:
                            i_ = nc.scalar.copy(dst, bank[5][:, 0:AW])
                        i_.then_inc(s_pt, 1)

                def silu(p):
                    for c in (2 * p, 2 * p + 1):
                        act.wait_ge(conv2_new, NC8 * l + c + 1)
                        activation(qk[:, c, :], qk[:, c, :], ACT.Silu).then_inc(qk_new, 1)

                def mvt_chunk(c):
                    act.wait_ge(mt_tr, NC8 * l + c + 1)
                    nc.scalar.copy(mvt[:, 0:2, c * P:(c + 1) * P], bank[6][:, 0:2 * P].rearrange("p (t n) -> p t n", n=P))
                    nc.scalar.copy(mvt[0:TAIL, 2, c * P:(c + 1) * P], bank[6][0:TAIL, 2 * P:3 * P]).then_inc(mt_read, 1)

                def ml(hd, stage):
                    n = M_H * l + hd
                    if stage == 0:
                        act.wait_ge(m_bc, n + 1)
                        if n:
                            act.wait_ge(m_pt_new, n)
                        def e(t, x0, x1, src):
                            a, b = LT[t]
                            return activation(m_arg[0:b - a, MOFF[t] + x0 - a:MOFF[t] + x1 - a], src, ACT.Exp, scale=-1.0,
                                              bias=g_tok[0:b - a, t, hd:hd + 1])
                        act.wait_ge(m_arg_new, n + 1)
                        e(0, P, L, bank[4][:, P:L])
                        e(1, 2 * P, L, bank[4][:, 2 * P:L])
                        for t, (a, b) in enumerate(LT):
                            i_ = e(t, a, b, m_arg[0:b - a, MOFF[t]:MOFF[t] + b - a])
                        i_.then_inc(m_exp_new, 1)
                    if stage == 1:
                        act.wait_ge(m_num, n + 1)
                        for w in range(2):
                            i_ = activation(n_sq[:, w, :], bank[6 + w][:, 0:L], ACT.Square)
                        i_.then_inc(m_sq, 1)
                    if stage == 3:
                        act.wait_ge(m_bb, n + 1)
                        if n:
                            act.wait_ge(m_hm, n)
                        nc.scalar.copy(s_b, bank[5][:, 0:L]).then_inc(m_sb, 1)

                def nothing(n):
                    return None

                do = dict(turn=turn, rs=nothing, rt=lambda n: rt(), kx=lambda n: kx(), att=att,
                          silu=silu, mvt=mvt_chunk, ml=lambda hs: ml(*hs))

                def gate_chunks(ph, p):
                    for m in range(2):
                        c = 2 * p + m
                        k = c if ph == "ag" else NC8 + c
                        act.wait_ge(act_new, 16 + 16 * l + k + 1)
                        src = q if ph == "ag" else mv
                        i_ = nc.scalar.copy(y_hi[:, k * L + T0:(k + 1) * L], src[:, c, T0:L])
                        i_.then_inc(act_hi, 1)

                u = 0
                later = None
                for ph in STREAM:
                    pb = PHASES[f"{ph}{l}"][1]
                    for p in range(PHASES[f"{ph}{l}"][2]):
                        for j, (U, _, _) in enumerate(units_of(pb + p)):
                            split_w(U + LEAD)
                            if later:
                                gate_chunks(*later)
                                later = None
                            if u == 1 and l == 0 or u == 0 and l == 1:
                                root(7 + l, 0)
                            if j == 1:
                                T = 2 * (pb + p)
                                if ph == "mif":
                                    act.wait_ge(g_nx, l + 1)
                                    activation(g_row[0:4, 2, :], g_row[0:4, 1, :], ACT.Exp).then_inc(g_e, 1)
                                if ph == "mqk" and p == 0:
                                    act.wait_ge(g_cm, l + 1)
                                    activation(g_row[0:4, 5, :], g_row[0:4, 5, :], ACT.Exp, scale=-1.0).then_inc(g_exp, 1)
                                if ph == "mqk":
                                    for m in range(2):
                                        c = 2 * p + m
                                        act.wait_ge(tile_read, T + m + 1)
                                        activation(qk[:, c, :], pre[:, m, 0:L], ACT.Identity,
                                                   scale=pcol("mlstm_conv_w_2", l * 4 * NC8 + c),
                                                   bias=pcol("mlstm_conv_b_2", l * NC8 + c)).then_inc(tap0, 1)
                                if ph == "mo":
                                    for m in range(2):
                                        act.wait_ge(tile_read, T + m + 1)
                                        activation(mv[:, 2 * p + m, T0:L], mv[:, 2 * p + m, T0:L], ACT.Tanh,
                                                   scale=0.5).then_inc(gate_act, 1)
                                if ph in ("ag", "mg"):
                                    for m in range(2):
                                        act.wait_ge(tile_read, T + m + 1)
                                        activation(gate_t[:, m, T0:L], gate_x[:, m, T0:L], ACT.Tanh,
                                                   scale=0.5).then_inc(gate_act, 1)
                                    later = (ph, p)
                            for kind, n in VISITS[u]:
                                do[kind](n)
                            u += 1
                out_phase(f"proj{l}", (lambda c: pcol("norm_g_2", NC8 + c)) if l == 0 else None, N=L, T0=0,
                          before=lambda: gate_chunks(*later))

        @block.gpsimd
        def _(pool):
            nc.gpsimd.memset(ones[:, :], 1.0)
            nc.gpsimd.memset(epsc[:, :], EPS).then_inc(ones_set, 1)
            nc.gpsimd.memset(blocks_a[:, :, :], 0.0)
            nc.gpsimd.memset(blocks_x[:, :, :], 0.0)
            nc.gpsimd.memset(pre[:, :, 0:3], 0.0)
            nc.gpsimd.memset(rec_p[:, :, 0:3], 0.0).then_inc(zero_set, 1)
            TT = nc.gpsimd.tensor_tensor
            chain = [0]

            def link(i_):
                chain[0] += 1
                i_.then_inc(pool_ch, 1)
                pool.wait_ge(pool_ch, chain[0])

            def squares(src, wait, T0, done):
                for c in range(NC8):
                    wait(c)
                    if c == 0:
                        link(TT(sumsq[:, T0:L], src(c), src(c), MUL))
                    else:
                        link(TT(sq[:, T0:L], src(c), src(c), MUL))
                        i_ = TT(sumsq[:, T0:L], sumsq[:, T0:L], sq[:, T0:L], ADD)
                        if c < NC8 - 1:
                            link(i_)
                        else:
                            i_.then_inc(done, 1)

            def h_squares(n, name, T0):
                pb = PHASES[name][1]
                if n:
                    pool.wait_ge(sum_done, n + (n == 7))
                squares(lambda c: h[:, c, T0:L], lambda c: pool.wait_ge(tile_read, 2 * pb + c + 1), T0, sq_done)

            def gate_scale(f):
                def turn(i):
                    for m in range(2):
                        pool.wait_ge(silu_done, 22 * f + m + 1 + 2 * i)
                        TT(ffn_r[:, m, :], ffn_s[:, m, :], rstd[:, META:L], MUL).then_inc(gate_scaled, 1)
                with pool.Fori(0, FF // CU) as i:
                    turn(i)

            squares(lambda c: h[:, c, META:L], lambda c: pool.wait_ge(xt_read, c + 1), META, sq_done)
            gate_scale(0)
            h_squares(1, "out01", META)
            for c in range(NC8):
                pool.wait_ge(gates_sig, 2 * c + 2)
                i_ = TT(rec_x[:, c, :], rec_x[:, c, :], rec_g[:, c, :], MUL)
                i_.then_inc(pool_ch, 1)
                chain[0] += 1
            for c in range(NC8):
                pool.wait_ge(mult_new, c + 1)
                pool.wait_ge(pool_ch, chain[0])
                TT(rec_x[:, c, :], rec_x[:, c, :], rec_p[:, c, 0:SEQ], MUL).then_inc(rec_bx, 1)
            h_squares(2, "rec_out", META)
            gate_scale(1)
            h_squares(3, "out02", META)
            gate_scale(2)
            h_squares(4, "out11", META)
            pool.wait_ge(sum_done, 5)
            squares(lambda c: sg_v[:, c, :], lambda c: pool.wait_ge(sg_gelu, c + 1), META, sg_sqs)
            pool.wait_ge(sg_sum, 1)
            h_squares(5, "sg_out", META)
            gate_scale(3)
            h_squares(6, "out12", META)
            for l in range(DEPTH):
                I0 = len(ITEMS) * l

                def att(v):
                    if 1 <= v <= len(ITEMS):
                        g, hd = ITEMS[v - 1]
                        n = I0 + v - 1
                        i = (v - 1) % 2
                        pr, rec = prob[:, i, :], att_s[:, 8 + i, :]
                        TS = nc.gpsimd.tensor_scalar
                        pool.wait_ge(s_rec, n + 1)
                        if hd is None:
                            TS(pr[:, 0:L], pr[:, 0:L], rec[:, 0:1], None, MUL).then_inc(s_prob, 1)
                        else:
                            TS(pr[:, 0:P], pr[:, 0:P], rec[:, 0:1], None, MUL)
                            TS(pr[:, P:AW], pr[:, P:AW], rec[:, 1:2], None, MUL).then_inc(s_prob, 1)

                def turn(c):
                    n = 9 * l + c
                    src = k_att if c == 0 else q[:, c - 1, :]
                    pool.wait_ge(tile_read, 2 * PHASES[f"kv{l}"][1] + 1 if c == 0 else 2 * PHASES[f"aq{l}"][1] + c)
                    if c == 0:
                        pool.wait_ge(cos_ready, l + 1)
                        if l:
                            pool.wait_ge(m_hm, M_H * l)
                    if n >= 2:
                        pool.wait_ge(q_ready, n - 1)
                    TT(qs[:, n % 2, :], src, cst("sin"), MUL)
                    TT(qc[:, n % 2, :], src, cos_g[:, 0 if c else 1, :], MUL).then_inc(qc_new, 1)

                for u in range(STREAM_UNITS):
                    for kind, n in VISITS[u]:
                        if kind in ("att", "turn"):
                            dict(att=att, turn=turn)[kind](n)
                if l == 0:
                    h_squares(7, "proj0", 0)

        @block.vector
        def _(dve):
            V = nc.vector
            TT, TS, STT = V.tensor_tensor, V.tensor_scalar, V.scalar_tensor_tensor
            chain = [0]

            def link(i_):
                chain[0] += 1
                i_.then_inc(dch, 1)
                dve.wait_ge(dch, chain[0])

            def split_w(U, off=0):
                if U >= NU:
                    return
                n, s = UNITS[U][3], U % RING
                dve.wait_ge(hi_made, U + 1 + off)
                TT(w_lo[:, s, 0:n, :], raw[:, s, 0:n, :], w_hi[:, s, 0:n, :].bitcast(fp32), SUB).then_inc(lo_made, 1)

            def ahead(pr):
                for U, _, _ in units_of(pr):
                    split_w(U + LEAD)

            def split_x(dst_lo, dst_hi, k, N, src, count, scale=None):
                dve.wait_ge(act_hi, count + 1)
                hi = xview(dst_hi, k, N).bitcast(fp32)
                if scale is None:
                    i_ = TT(xview(dst_lo, k, N), src, hi, SUB)
                else:
                    i_ = STT(out=xview(dst_lo, k, N), in0=src, scalar=scale, in1=hi, op0=MUL, op1=SUB)
                i_.then_inc(act_ready, 1)

            def inverse(n, T0):
                dve.wait_ge(rms_done, n + 1)
                link(V.reciprocal(rstd[:, T0:L], rms[:, T0:L]))

            def wait_tile(pr, m, off=0):
                if m == 0 and len(units_of(pr)) and pr not in ONE_TILE:
                    dve.wait_ge(first_done, FIRSTS[pr] + 1 + (off // 2 if isinstance(off, int) else 2 * off_i[0]))
                else:
                    dve.wait_ge(unit_done, units_of(pr)[-1][0] + 1 + off)

            off_i = [0]
            ONE_TILE = {PHASES[f"mif{l}"][1] for l in range(DEPTH)}
            FIRSTS = {}
            k_ = 0
            for pr_ in range(len(PAIRS)):
                FIRSTS[pr_] = k_
                k_ += pr_ not in ONE_TILE

            def tile(pr, m, N):
                return bank[(2 * pr + m) % 4][:, 0:N]

            def scaled(pr, m, dst, N, T0, off=0):
                wait_tile(pr, m, off)
                TT(dst, tile(pr, m, N), rstd[:, T0:L], MUL).then_inc(tile_read, 1)

            def gate_turn(pb, ub, i, f, count, first=None):
                o = 4 * i
                off_i[0] = i
                for U in (ub, ub + 1):
                    split_w(U + LEAD, o)
                if first is not None:
                    inverse(first, META)
                for m in range(2):
                    scaled(pb, m, ffn_t[:, m, :], SEQ, META, o)
                for U in (ub + 2, ub + 3):
                    split_w(U + LEAD, o)
                for m in range(2):
                    wait_tile(pb + 1, m, o)
                    dve.wait_ge(gate_scaled, 22 * f + m + 1 + 2 * i)
                    TT(ffn_h[:, m, :], tile(pb + 1, m, SEQ), ffn_r[:, m, :], MUL).then_inc(tile_read, 1)
                for m in range(2):
                    dve.wait_ge(act_hi, count + m + 1 + 2 * i)
                    if isinstance(i, int):
                        lo, hi = (xview(t, 2 * i + m, SEQ) for t in (y_lo, y_hi))
                    else:
                        lo, hi = (t[:, bass.ds(i * (2 * SEQ) + m * SEQ, SEQ)] for t in (y_lo, y_hi))
                    TT(lo, ffn_h[:, m, :], hi.bitcast(fp32), SUB).then_inc(act_ready, 1)

            def in_phase(name, f, n, count):
                ub, pb, _ = PHASES[name]
                gate_turn(pb, ub, 0, f, count, first=n)
                with dve.Fori(1, FF // CU) as i:
                    gate_turn(pb, ub, i, f, count)

            def out_phase(name, g, count, half=0.5, N=SEQ, T0=META, before=None):
                ub, pb, npairs = PHASES[name]
                for p in range(npairs):
                    for U, _, _ in units_of(pb + p):
                        split_w(U + LEAD)
                        if before is not None:
                            before()
                            before = None
                    for m in range(2):
                        c = 2 * p + m
                        wait_tile(pb + p, m)
                        STT(out=h[:, c, T0:L], in0=tile(pb + p, m, N), scalar=half, in1=h[:, c, T0:L], op0=MUL,
                            op1=ADD).then_inc(tile_read, 1)
                        if g is not None:
                            split_x(x_lo, x_hi, c, N, h[:, c, T0:L], count + c, g(c))

            dve.wait_ge(par_t, 1)
            rows1 = sum(k for (t, _, k) in PAR.values() if t == 1)
            V.tensor_copy(par[:, 0, :], bank[4][:, 0:P])
            V.tensor_copy(par[:, 1, 0:rows1], bank[4][:, P:P + rows1]).then_inc(par_ready, 1)
            dve.wait_ge(par_ready, 1)
            for c in range(NC8):
                dve.wait_ge(xt_done, c + 1)
                V.tensor_copy(h[:, c, :], bank[c % 4][:, 0:L]).then_inc(xt_read, 1)
            dve.wait_ge(zero_set, 1)
            dve.wait_ge(xt_read, NC8)
            lam_t, lam_r, _ = PAR["rec_lambda"]
            lam = par[:, lam_t, lam_r:lam_r + NC8]
            link(STT(out=decay[:, 0, :], in0=lam, scalar=-1.0, in1=lam, op0=MUL, op1=MIN))

            def log1p(dst, e, t0, t1, t2, part=None):
                if part in (None, 0):
                    link(TS(t0, e, 2.0, None, ADD))
                    link(V.reciprocal(t1, t0))
                    link(TT(t0, e, t1, MUL))
                    link(TT(t1, t0, t0, MUL))
                    link(TS(t2, t1, 1.0 / 17, None, MUL))
                for k in {None: (15, 13, 11, 9, 7, 5, 3), 0: (), 1: (15, 13, 11, 9), 2: (7, 5, 3)}[part]:
                    link(STT(out=t2, in0=t2, scalar=1.0 / k, in1=t1, op0=ADD, op1=MUL))
                if part in (None, 2):
                    link(STT(out=t2, in0=t2, scalar=1.0, in1=t0, op0=ADD, op1=MUL))
                    link(TS(dst, t2, 2.0, None, MUL))

            V.tensor_copy(decay[:, 11, :], decay[:, 0, :]).then_inc(decay_v, 1)
            dve.wait_ge(decay_e, 1)
            log1p(decay[:, 4, :], decay[:, 1, :], decay[:, 5, :], decay[:, 6, :], decay[:, 7, :])
            link(TS(decay[:, 8, :], lam, -1.0, 0.0, MUL, MAX))
            link(TT(decay[:, 9, :], decay[:, 8, :], decay[:, 4, :], ADD))
            TS(decay[:, 2, :], decay[:, 9, :], -8.0, None, MUL)
            TS(decay[:, 3, :], decay[:, 9, :], 8.0, None, MUL).then_inc(decay_v, 1)
            for c in range(NC8):
                split_x(x_lo, x_hi, c, SEQ, h[:, c, META:L], c, pcol("ffn1_norm", c))
            for U in range(LEAD):
                split_w(U)

            in_phase("in01", 0, 0, SPLITS["y_out01"])
            out_phase("out01", lambda c: pcol("mix_norm", c), SPLITS["x_rec_b"])

            _, pb, _ = PHASES["rec_b"]
            for p in range(4):
                ahead(pb + p)
                if p == 0:
                    inverse(1, META)
                for m in range(2):
                    scaled(pb + p, m, rec_p[:, 2 * p + m, 3:3 + SEQ], SEQ, META)
                dve.wait_ge(tile_read, 2 * (pb + p) + 2)
                for k in range(4):
                    for m in range(2):
                        c = 2 * p + m
                        src, w = rec_p[:, c, k:k + SEQ], pcol("rec_conv_w", k * NC8 + c)
                        if k == 0:
                            i_ = TS(rec_x[:, c, :], src, w, pcol("rec_conv_b", c), MUL, ADD)
                        else:
                            i_ = STT(out=rec_x[:, c, :], in0=src, scalar=w, in1=rec_x[:, c, :], op0=MUL, op1=ADD)
                        if k == 3:
                            i_.then_inc(conv_new, 1)
                        elif m == 1:
                            link(i_)
            _, pb, _ = PHASES["rec_a"]
            ahead(pb)
            for m in range(2):
                scaled(pb, m, rec_y[:, m, :], SEQ, META)
            ahead(pb + 1)
            for m in range(2):
                scaled(pb + 1, m, rec_y[:, 2 + m, :], SEQ, META)

            def mult_square(c):
                dve.wait_ge(ax_new, c + 1)
                t = ffn_t[:, c % 2, :]
                link(TS(ffn_r[:, c % 2, :], t, 1.0, None, ADD))
                link(V.reciprocal(ffn_h[:, c % 2, :], ffn_r[:, c % 2, :]))
                STT(out=rec_p[:, c, 0:SEQ], in0=t, scalar=2.0, in1=ffn_h[:, c % 2, :], op0=MUL, op1=MUL).then_inc(mult2, 1)

            for c in range(4):
                mult_square(c)
            ahead(pb + 2)
            for c in range(4, NC8):
                mult_square(c)
            for m in range(2):
                scaled(pb + 2, m, rec_y[:, 4 + m, :], SEQ, META)
            ahead(pb + 3)
            for m in range(2):
                scaled(pb + 3, m, rec_y[:, 6 + m, :], SEQ, META)
            dve.wait_ge(mult2, NC8)
            for c in range(NC8):
                dve.wait_ge(rec_bx, c + 1)
                link(V.tensor_tensor_scan(rec_g[:, c, :], rec_a[:, c, :], rec_x[:, c, :], 0.0, MUL, ADD))
                dve.wait_ge(rec_gelu, c + 1)
                TT(rec_y[:, c, :], rec_y[:, c, :], rec_g[:, c, :], MUL).then_inc(act_new, 1)
            for c in range(NC8):
                split_x(y_lo, y_hi, c, SEQ, rec_y[:, c, :], SPLITS["y_rec_out"] + c)
            out_phase("rec_out", lambda c: pcol("ffn2_norm", c), SPLITS["x_in02"], half=1.0)

            in_phase("in02", 1, 2, SPLITS["y_out02"])
            out_phase("out02", lambda c: pcol("ffn1_norm", NC8 + c), SPLITS["x_in11"])
            in_phase("in11", 2, 3, SPLITS["y_out11"])
            out_phase("out11", lambda c: pcol("mix_norm", NC8 + c), SPLITS["x_sg_b"])

            _, pb, _ = PHASES["sg_b"]
            for p in range(4):
                ahead(pb + p)
                if p == 0:
                    inverse(4, META)
                for m in range(2):
                    scaled(pb + p, m, sg_v[:, 2 * p + m, :], SEQ, META)
                if p == 1:
                    dve.wait_ge(ws_tr, 1)
                    for c in range(NC8):
                        i_ = TT(ws_t[:, c, :], bank[5 + c // 4][:, (c % 4) * P:(c % 4 + 1) * P], tri, MUL)
                        if c % 4 == 3:
                            i_.then_inc(ws_read, 1)
            _, pb, _ = PHASES["sg_a"]
            ahead(pb)
            for m in range(2):
                scaled(pb, m, sg_u[:, m, :], SEQ, META)
            dve.wait_ge(sg_rms, 1)
            link(V.reciprocal(sg_r[:, 1, :], sg_r[:, 0, :]))
            for g in range(4):
                t, c0 = g // 2, 4 * (g % 2)
                dve.wait_ge(vt_tr, g + 1)
                TS(v_tok[:, t, c0 * P:(c0 + 4) * P], bank[5 + g % 3][:, :], sg_r[:, 1, t:t + 1], None, MUL).then_inc(vt_read, 1)
            ahead(pb + 1)
            for m in range(2):
                scaled(pb + 1, m, sg_u[:, 2 + m, :], SEQ, META)
            for c in range(NC8):
                dve.wait_ge(sg_mm, c + 1)
                for t in range(2):
                    i_ = STT(out=sg_s[:, c, t * P:(t + 1) * P], in0=bank[4 + c % 4][:, t * P:(t + 1) * P],
                             scalar=pcol("sg_v_norm", c), in1=bs_all[:, c, :], op0=MUL, op1=ADD)
                i_.then_inc(sg_read, 1)
            for p in (2, 3):
                ahead(pb + p)
                for m in range(2):
                    scaled(pb + p, m, sg_u[:, 2 * p + m, :], SEQ, META)
            dve.wait_ge(sg_read, NC8)
            for c in range(NC8):
                dve.wait_ge(sg_gelu, NC8 + c + 1)
                TT(sg_s[:, c, :], sg_s[:, c, :], sg_u[:, c, :], MUL).then_inc(act_new, 1)
            for c in range(NC8):
                split_x(y_lo, y_hi, c, SEQ, sg_s[:, c, :], SPLITS["y_sg_out"] + c)
            out_phase("sg_out", lambda c: pcol("ffn2_norm", NC8 + c), SPLITS["x_in12"], half=1.0)

            in_phase("in12", 3, 5, SPLITS["y_out12"])
            out_phase("out12", None, 0)
            inverse(6, META)
            for c in range(NC8):
                STT(out=h[:, c, META:L], in0=h[:, c, META:L], scalar=pcol("final_norm", c), in1=rstd[:, META:L], op0=MUL,
                    op1=MUL).then_inc(final_new, 1)
            V.memset(att_s[:, :, :], 0.0).then_inc(final_new, 1)
            for c in range(NC8):
                split_x(x_lo, x_hi, c, L, h[:, c, :], SPLITS["x_kv0"] + c, pcol("norm_g_2", c))

            def rsqrt(y, x, t):
                i32 = mybir.dt.int32
                link(TS(y.bitcast(i32), x.bitcast(i32), 1, None, ALU.logical_shift_right))
                link(TS(y.bitcast(i32), y.bitcast(i32), -1, 0x5F3759DF, MUL, ADD))
                for _ in range(3):
                    link(TT(t, y, y, MUL))
                    link(STT(out=t, in0=t, scalar=-0.5, in1=x, op0=MUL, op1=MUL))
                    link(STT(out=y, in0=t, scalar=1.5, in1=y, op0=ADD, op1=MUL))

            dve.wait_ge(sg_loaded, SG_LOADS)
            TS(neg_sinks[:, :], sinks[:, :], -1.0, None, MUL)
            link(TS(neg_tail[:, :], sink_tail[:, :], -1.0, None, MUL))
            link(V.memset(norms[:, :, :], 1.0))
            link(V.memset(den_s[:, :, :], 1.0))
            link(V.memset(g_tok[:, :, :], 0.0))
            for l in range(DEPTH):
                I0 = len(ITEMS) * l
                narrow = l == DEPTH - 1
                T0 = META if narrow else 0

                def tables():
                    gq, gk = pcol("attn_q_norm_g_2", l), pcol("attn_k_norm_g_2", l)
                    sc = DH ** -0.5
                    if l:
                        dve.wait_ge(m_hm, M_H * l)
                    TS(cos_g[:, 0, :], cst("cos"), gq, sc, MUL, MUL)
                    TS(cos_g[:, 1, :], cst("cos"), gk, None, MUL)
                    TS(rot_g[:, 0, :], cst("rot"), gq, sc, MUL, MUL)
                    TS(rot_g[:, 1, :], cst("rot"), gk, None, MUL).then_inc(cos_ready, 1)

                def gates_in(pr):
                    wait_tile(pr, 1)
                    b0 = bank[(2 * pr) % 4]
                    if l:
                        dve.wait_ge(m_hm, M_H * l)
                    TT(g_row[0:4, 3, :], b0[0:4, 0:L], rstd[0:4, :], MUL)
                    link(TT(g_row[0:4, 0, :], b0[32:36, 0:L], rstd[32:36, :], MUL))
                    TS(g_row[0:4, 3, :], g_row[0:4, 3, :], gbias[:, l:l + 1], None, ADD)
                    link(TS(g_row[0:4, 0, :], g_row[0:4, 0, :], gbias[:, DEPTH + l:DEPTH + l + 1], None, ADD))
                    V.tensor_copy(g_row[0:1, 4, 0:1], g_row[0:1, 0, 0:1]).then_inc(tile_read, 2)
                    STT(out=g_row[0:4, 1, :], in0=g_row[0:4, 0, :], scalar=-1.0, in1=g_row[0:4, 0, :], op0=MUL,
                        op1=MIN).then_inc(g_nx, 1)

                def forget_rows(part):
                    if part < 3:
                        if part == 0:
                            dve.wait_ge(g_e, l + 1)
                        log1p(g_row[0:4, 5, :], g_row[0:4, 2, :], g_row[0:4, 1, :], exp_b[0:4, :], m_b[0:4, :], part)
                        return
                    link(STT(out=g_row[0:4, 1, :], in0=g_row[0:4, 0, :], scalar=0.0, in1=g_row[0:4, 5, :], op0=MIN, op1=SUB))
                    link(V.memset(g_row[0:4, 0, :], 1.0))
                    link(V.tensor_tensor_scan(g_row[0:4, 2, :], g_row[0:4, 0, :], g_row[0:4, 1, :], 0.0, MUL, ADD))
                    link(TT(g_row[0:4, 3, :], g_row[0:4, 3, :], g_row[0:4, 2, :], SUB))
                    link(V.tensor_tensor_scan(g_row[0:4, 4, :], g_row[0:4, 3, :], g_row[0:4, 3, :], 0.0, MAX, MAX))
                    link(TT(g_row[0:4, 5, :], g_row[0:4, 2, :], g_row[0:4, 4, :], ADD))
                    TS(g_row[0:4, 5, :], g_row[0:4, 5, :], M_MIN, None, MAX).then_inc(g_cm, 1)

                def rs():
                    dve.wait_ge(turn_mm, 9 * (l + 1))
                    W = 2 * NR
                    TS(norms[:, 0, 0:W], bank[4][:, 0:W], EPS, None, ADD)
                    link(TS(norms[0:TAIL, 0, W:W + NR], bank[4][0:TAIL, W:W + NR], EPS, None, ADD))
                    rsqrt(norms[:, 3, :], norms[:, 0, :], norms[:, 1, :])
                    TS(norms[:, 2, :], norms[:, 3, :], -1.0, None, MUL).then_inc(rs_new, 1)

                def turn(c):
                    n = 9 * l + c
                    dst = k_att if c == 0 else q[:, c - 1, :]
                    dve.wait_ge(turn_mm, n + 1)
                    TT(dst, bank[5 + n % 2][:, 0:L], qc[:, n % 2, :], ADD).then_inc(q_ready, 1)

                def rt():
                    dve.wait_ge(rt_mm, 2 * l + 2)
                    TT(k_att, k_att, bank[6][:, 0:L], MUL).then_inc(k_ready, 1)
                    for g in range(2):
                        for e in range(2):
                            i_ = TT(q_tail[g * DH:(g + 1) * DH, g, e * DH:(e + 1) * DH].rearrange("p (c t) -> p c t", t=TAIL),
                                    q[e * DH:(e + 1) * DH, 4 * g:4 * g + 4, 2 * P:L],
                                    bank[7][e * DH:(e + 1) * DH, 4 * g * TAIL:4 * (g + 1) * TAIL].rearrange(
                                        "p (c t) -> p c t", t=TAIL), MUL)
                        i_.then_inc(tail_new, 1)

                def kx():
                    dve.wait_ge(kx_mm, l + 1)
                    V.tensor_copy(va_t[:, 0:2, :], bank[5][:, 0:2 * P].rearrange("p (t n) -> p t n", n=P))
                    V.tensor_copy(va_t[0:TAIL, 2, :], bank[5][0:TAIL, 2 * P:3 * P])
                    V.tensor_copy(g_tok[:, 0:2, :], bank[5][:, 3 * P:3 * P + 16].rearrange("p (t n) -> p t n", n=8))
                    V.tensor_copy(g_tok[0:TAIL, 2, :], bank[5][0:TAIL, 3 * P + 16:3 * P + 24]).then_inc(kx_read, 1)

                def att(v):
                    if v < len(ITEMS):
                        g, hd = ITEMS[v]
                        n = I0 + v
                        i = v % 2
                        s, mx, nm = score[:, i, :], att_s[:, 3 * i, :], att_s[:, 3 * i + 1, :]
                        dve.wait_ge(s_mm, n + 1)
                        if v >= 2:
                            dve.wait_ge(s_exp, n - 1)
                        if hd is None:
                            link(V.tensor_tensor_reduce(s[:, 0:L], bank[4][:, 0:L], cst("tmask"), 1.0, NEG, ADD, MAX, mx[:, 0:1]))
                            TS(nm[:, 0:1], mx[:, 0:1], -1.0, neg_tail[:, 2 * l + g:2 * l + g + 1], MUL, MIN).then_inc(s_max, 1)
                        else:
                            am = cst("amask")
                            V.tensor_tensor_reduce(s[:, 0:P], bank[4][:, 0:P], am[:, 0:P], 1.0, NEG, ADD, MAX, mx[:, 0:1])
                            link(V.tensor_tensor_reduce(s[:, P:AW], bank[4][:, P:AW], am[:, P:AW], 1.0, NEG, ADD, MAX,
                                                        mx[:, 1:2]))
                            for t in range(2):
                                at = NR * t + 2 + hd
                                i_ = TS(nm[:, t:t + 1], mx[:, t:t + 1], norms[:, 2, at:at + 1],
                                        neg_sinks[:, l * ATT_H + hd:l * ATT_H + hd + 1], MUL, MIN)
                            i_.then_inc(s_max, 1)
                    if v >= 3:
                        g, hd = ITEMS[v - 3]
                        n = I0 + v - 3
                        if hd is None:
                            dve.wait_ge(s_pv, n + 1)
                            V.tensor_copy(q[:, 4 * g:4 * g + 4, 2 * P:L],
                                          bank[7][:, 0:DH].rearrange("p (c t) -> p c t", t=TAIL)).then_inc(s_out, 1)
                        elif hd % 2:
                            dve.wait_ge(s_pv, n + 1)
                            V.tensor_copy(q[:, hd // 2, 0:2 * P], bank[7][:, 0:2 * P]).then_inc(s_out, 1)

                def att_later(v):
                    if v < len(ITEMS):
                        i = v % 2
                        dve.wait_ge(s_exp, I0 + v + 1)
                        link(TT(att_s[:, 10 + i, 0:2], att_s[:, 3 * i + 2, 0:2], att_s[:, 6 + i, 0:2], ADD))
                        V.reciprocal(att_s[:, 8 + i, 0:2], att_s[:, 10 + i, 0:2]).then_inc(s_rec, 1)

                def conv(p):
                    for k in range(1, 4):
                        for m in range(2):
                            c = 2 * p + m
                            w = pcol("mlstm_conv_w_2", (l * 4 + k) * NC8 + c)
                            if k == 1:
                                dve.wait_ge(tap0, NC8 * l + c + 1)
                            i_ = STT(out=qk[:, c, :], in0=pre[:, m, k:k + L], scalar=w, in1=qk[:, c, :], op0=MUL, op1=ADD)
                            if k == 3:
                                i_.then_inc(conv2_new, 1)
                        if k < 3:
                            link(i_)

                def ml(hd, stage):
                    n = M_H * l + hd
                    if stage == 0:
                        dve.wait_ge(m_bc, n + 1)
                        if n:
                            dve.wait_ge(m_pt_new, n)
                        for t, (a, b) in enumerate(LT):
                            i_ = TT(m_arg[0:b - a, MOFF[t]:MOFF[t] + b - a], bank[4][0:b - a, a:b],
                                    con[0:b - a, CONST_AT["mmask"]:CONST_AT["mmask"] + b - a], ADD)
                        i_.then_inc(m_arg_new, 1)

                def ml_later(hd, stage):
                    n = M_H * l + hd
                    small = ((slice(0, P), slice(0, 2)), (slice(0, TAIL), slice(2, 3)))
                    if stage == 0:
                        dve.wait_ge(m_qk, n + 1)
                        dve.wait_ge(m_exp_new, n + 1)
                        if n:
                            dve.wait_ge(m_num, n)
                        W01 = MOFF[2]
                        STT(out=m_pt[:, 0:W01], in0=bank[5][:, 0:W01], scalar=QK_D ** -0.5, in1=m_arg[:, 0:W01], op0=MUL,
                            op1=MUL)
                        STT(out=m_pt[0:TAIL, W01:MW], in0=bank[5][0:TAIL, W01:MW], scalar=QK_D ** -0.5,
                            in1=m_arg[0:TAIL, W01:MW], op0=MUL, op1=MUL).then_inc(m_pt_new, 1)
                    if stage == 1:
                        dve.wait_ge(m_num, n + 1)
                        for r, c in small:
                            i_ = TS(den_s[r, 0, c], bank[4][r, 400 + c.start:400 + c.stop], -1.0, None, MUL)
                        link(i_)
                        for r, c in small:
                            i_ = TT(den_s[r, 0, c], bank[4][r, 400 + c.start:400 + c.stop], den_s[r, 0, c], MAX)
                        i_.then_inc(m_den, 1)
                        dve.wait_ge(m_den, n + 1)
                        link(TT(den_s[:, 0, 0:3], den_s[:, 0, 0:3], g_tok[:, :, 4 + hd], MAX))
                        link(STT(out=den_s[:, 1, 0:3], in0=den_s[:, 0, 0:3], scalar=EPS, in1=den_s[:, 0, 0:3], op0=MUL, op1=MUL))
                    if stage == 2:
                        dve.wait_ge(m_ms, n + 1)
                        for r, c in small:
                            i_ = STT(out=den_s[r, 2, c], in0=bank[4][r, 408 + c.start:408 + c.stop], scalar=1.0 / 256,
                                     in1=den_s[r, 1, c], op0=MUL, op1=ADD)
                        i_.then_inc(ms_read, 1)
                        dve.wait_ge(ms_read, n + 1)
                        rsqrt(den_s[:, 5, 0:3], den_s[:, 2, 0:3], den_s[:, 4, 0:3])
                        if n:
                            dve.wait_ge(m_bb, n)
                        for j, (a, b) in enumerate(LT):
                            i_ = TS(diag[0:b - a, j, 0:b - a], ident[0:b - a, 0:b - a], den_s[0:b - a, 5, j:j + 1], 0.25,
                                    MUL, MUL)
                        i_.then_inc(m_diag, 1)
                    if stage == 3:
                        dve.wait_ge(m_sb, n + 1)
                        for w in range(2):
                            c = 2 * hd + w
                            t = gate_x2[:, w, :]
                            i_ = STT(out=t, in0=bank[6 + w][:, 0:L], scalar=pcol("mlstm_out_norm_g_2", l * NC8 + c),
                                     in1=s_b, op0=MUL, op1=MUL)
                        link(i_)
                        for w in range(2):
                            c = 2 * hd + w
                            dve.wait_ge(gate_act, G0 + c + 1)
                            i_ = STT(out=mv[:, c, T0:L], in0=mv[:, c, T0:L], scalar=1.0, in1=gate_x2[:, w, T0:L], op0=ADD,
                                     op1=MUL)
                        i_.then_inc(m_hm, 1)

                G0 = 24 * l
                gate_x2 = g_x2

                def gated(ph, p):
                    g = 1 if ph == "ag" else 2
                    for m in range(2):
                        dve.wait_ge(gate_act, G0 + 8 * g + 2 * p + m + 1)
                        i_ = STT(out=gate_x[:, m, T0:L], in0=gate_t[:, m, T0:L], scalar=1.0, in1=gate_x[:, m, T0:L], op0=ADD,
                                 op1=MUL)
                    link(i_)
                    for m in range(2):
                        c = 2 * p + m
                        if ph == "ag":
                            if m == 0:
                                dve.wait_ge(s_out, 10 * (l + 1))
                            i_ = STT(out=q[:, c, T0:L], in0=gate_x[:, m, T0:L], scalar=0.5, in1=q[:, c, T0:L], op0=MUL,
                                     op1=MUL)
                        else:
                            if m == 0:
                                dve.wait_ge(m_hm, M_H * l + p + 1)
                            i_ = TT(mv[:, c, T0:L], mv[:, c, T0:L], gate_x[:, m, T0:L], MUL)
                        i_.then_inc(act_new, 1)

                def gated_lo(ph, p):
                    for m in range(2):
                        c = 2 * p + m
                        k = c if ph == "ag" else NC8 + c
                        dve.wait_ge(act_hi, SPLITS[f"y_proj{l}"] + k + 1)
                        cols = slice(k * L + T0, (k + 1) * L)
                        src = q if ph == "ag" else mv
                        TT(y_lo[:, cols], src[:, c, T0:L], y_hi[:, cols].bitcast(fp32), SUB).then_inc(act_ready, 1)

                def nothing(n):
                    return None

                do = dict(turn=turn, rs=lambda n: rs(), rt=lambda n: rt(), kx=lambda n: kx(), att=att,
                          silu=nothing, mvt=nothing, ml=lambda hs: ml(*hs))
                do_later = dict(att=att_later, ml=lambda hs: ml_later(*hs))
                u = 0
                later, gate_later = [], None
                for ph in STREAM:
                    pb = PHASES[f"{ph}{l}"][1]
                    for p in range(PHASES[f"{ph}{l}"][2]):
                        pr = pb + p
                        for j, (U, _, _) in enumerate(units_of(pr)):
                            split_w(U + LEAD)
                            if gate_later:
                                gated(*gate_later)
                            for kind, n in later:
                                do_later[kind](n)
                            if gate_later:
                                gated_lo(*gate_later)
                                gate_later = None
                            later = []
                            if u == 1 and l == 0 or u == 0 and l == 1:
                                inverse(7 + l, 0)
                            if j == 1:
                                if ph == "kv":
                                    scaled(pr, 0, k_att, L, 0)
                                    scaled(pr, 1, v_att, L, 0)
                                    tables()
                                if ph == "mif":
                                    gates_in(pr)
                                if ph == "aq":
                                    for m in range(2):
                                        scaled(pr, m, q[:, 2 * p + m, T0:L], L - T0, T0)
                                    forget_rows(p)
                                if ph == "mqk":
                                    for m in range(2):
                                        if p:
                                            dve.wait_ge(conv2_new, NC8 * l + 2 * p)
                                        scaled(pr, m, pre[:, m, 3:3 + L], L, 0)
                                    conv(p)
                                if ph == "mv":
                                    for m in range(2):
                                        scaled(pr, m, mv[:, 2 * p + m, :], L, 0)
                                if ph == "mo":
                                    for m in range(2):
                                        dve.wait_ge(mt_tr, NC8 * l + 2 * p + m + 1)
                                        scaled(pr, m, mv[:, 2 * p + m, T0:L], L - T0, T0)
                                if ph in ("ag", "mg"):
                                    for m in range(2):
                                        scaled(pr, m, gate_x[:, m, T0:L], L - T0, T0)
                                    gate_later = (ph, p)
                            for kind, n in VISITS[u]:
                                for k_, n_ in later:
                                    do_later[k_](n_)
                                later = [(kind, n)] if kind in do_later else []
                                do[kind](n)
                            u += 1

                def rest():
                    for kind, n in later:
                        do_later[kind](n)
                    gated(*gate_later)
                    gated_lo(*gate_later)

                out_phase(f"proj{l}", (lambda c: pcol("norm_g_2", NC8 + c)) if l == 0 else None,
                          SPLITS.get("x_kv1"), half=1.0, N=L - T0, T0=T0, before=rest)
            for g in range(4):
                t, c0 = g // 2, 4 * (g % 2)
                dve.wait_ge(ot_tr, g + 1)
                V.tensor_copy(orow[:, t, c0 * P:(c0 + 4) * P], bank[4 + g][:, :]).then_inc(ot_read, 1)


_INS = ['x', 'ffn1_norm', 'ffn1_w_in', 'ffn1_w_out', 'mix_norm', 'ffn2_norm', 'ffn2_w_in', 'ffn2_w_out', 'rec_w_in',
        'rec_conv_w', 'rec_conv_b', 'rec_gate_a_w', 'rec_gate_a_b', 'rec_gate_x_w', 'rec_gate_x_b', 'rec_lambda',
        'rec_w_out', 'sg_w_in', 'sg_v_norm', 'sg_w_s', 'sg_b_s', 'sg_w_out', 'final_norm', 'meta_2', 'norm_g_2',
        'w_in_2', 'attn_q_norm_g_2', 'attn_k_norm_g_2', 'attn_sink_2', 'mlstm_conv_w_2', 'mlstm_conv_b_2',
        'mlstm_b_i_2', 'mlstm_b_f_2', 'mlstm_out_norm_g_2', 'w_out_2']
_OUTS = [((1, SEQ, D), 'float32')]


def kernel(**inputs):
    import numpy as _np
    import concourse.bacc as _bacc
    from concourse import mybir as _mybir
    from concourse.bass_utils import run_bass_kernel_spmd as _run

    nc = _bacc.Bacc("TRN2", target_bir_lowering=False, num_devices=1)
    arrays = {"in_consts_dram": constants()}
    for name in _INS:
        arrays[f"in_{name}_dram"] = _np.ascontiguousarray(inputs[name])
    args = [nc.dram_tensor(n, a.shape, _mybir.dt.from_np(a.dtype), kind="ExternalInput").ap() for n, a in arrays.items()]
    for i, (shape, dtype) in enumerate(_OUTS):
        args.append(nc.dram_tensor(f"out_{i}_dram", shape, _mybir.dt.from_np(_np.dtype(dtype)), kind="ExternalOutput").ap())
    build_stack(nc, *args)
    r = _run(nc, [arrays], core_ids=[0])
    return r.results[0]["out_0_dram"]
```

```python
import numpy as np
import concourse.bass as bass
from concourse import mybir
from contextlib import ExitStack

P = 128
D = 1024
NC8 = D // P
SEQ = 256
META = 16
L = META + SEQ
FF = 2816
NF = FF // P
DEPTH = 2
KU = 4
CU = 256
RING = 4
LEAD = 3
EPS = 1e-6
NEG = -1e30
BIG = 1e30
ATT_H, DH, M_H, QK_D = 16, 64, 4, 128
ROT = 16
M_MIN = -41.0
WORK_SLOTS = 65
AW = 3 * P
LT = [(0, 128), (128, 256), (256, 272)]
NT = len(LT)
TAIL = 16
NR = 2 * (NC8 + 1)
MOFF = [0, L, L + (L - 128)]
MW = MOFF[2] + 16
C_AQ, C_KV, C_AG, C_MQK, C_MV, C_MIF, C_MO, C_MG = 0, 1024, 1280, 2304, 3328, 4352, 4360, 5384

CONST_W = dict(ident=P, tri=P, amask=AW, tmask=L, mmask=P, rot=P, swap=P, head_mean=2, cos=L, sin=L, sel=(NC8 + 1) * P)
CONST_AT = {}
_at = 0
for _n, _w in CONST_W.items():
    CONST_AT[_n] = _at
    _at += _w
CONST_ALL = _at


def constants():
    c = {n: np.zeros((P, w), np.float32) for n, w in CONST_W.items()}
    i = np.arange(P)
    c["ident"][i, i] = 1
    c["tri"][:] = i[:, None] <= i[None, :]

    def hidden(q, k):
        return ~((k <= q) & ((k < META) | (q - k < P)))

    c["amask"][:, :P] = NEG * hidden(i[:, None], i[None])
    c["amask"][:, P:] = NEG * hidden(P + i[:, None], np.arange(2 * P)[None])
    c["tmask"][:] = NEG * hidden(2 * P + i[:, None] % TAIL, np.arange(L)[None])
    c["mmask"][:] = BIG * (i[None] < i[:, None])
    half = ROT // 2
    for h0 in (0, DH):
        for d in range(half):
            c["rot"][h0 + half + d, h0 + d] = -1
            c["rot"][h0 + d, h0 + half + d] = 1
    c["swap"][i, (i + DH) % P] = 1
    c["head_mean"][i, i // DH] = 1.0 / DH
    inv = (500000.0 ** (-np.arange(0, ROT, 2, dtype=np.float32) / ROT)).astype(np.float32)
    ang = np.arange(L, dtype=np.float32)[None] * inv[:, None]
    c["cos"][:] = 1
    for h0 in (0, DH):
        for k in (0, half):
            c["cos"][h0 + k:h0 + k + half] = np.cos(ang)
            c["sin"][h0 + k:h0 + k + half] = np.sin(ang)
    for k in range(NC8 + 1):
        for e in range(2):
            c["sel"][2 * k + e, k * P + e * DH:k * P + (e + 1) * DH] = 1
    return np.concatenate([c[n] for n in CONST_W], 1)


PAR = {}
for _t, _rows in enumerate([
    [("ffn1_norm", 16), ("ffn2_norm", 16), ("mix_norm", 16), ("final_norm", 8), ("rec_conv_w", 32), ("rec_conv_b", 8),
     ("rec_gate_a_b", 8), ("rec_gate_x_b", 8), ("rec_lambda", 8), ("sg_v_norm", 8)],
    [("norm_g_2", 16), ("mlstm_conv_w_2", 64), ("mlstm_conv_b_2", 16), ("mlstm_out_norm_g_2", 16),
     ("attn_q_norm_g_2", 2), ("attn_k_norm_g_2", 2)],
]):
    _r = 0
    for _n, _k in _rows:
        PAR[_n] = (_t, _r, _k)
        _r += _k


def plan():
    units, pairs, phases = [], [], {}

    def phase(name, src, layer, rows, cols):
        ub, pb = len(units), len(pairs)
        for c0 in cols:
            ks = []
            k = 0
            while k < rows:
                n = min(KU, rows - k) if rows - k != 6 else 3
                ks.append((k, n))
                k += n
            pairs.append([(len(units) + j, k0, n) for j, (k0, n) in enumerate(ks)])
            units.extend((src, layer, k0, n, c0) for k0, n in ks)
        phases[name] = (ub, pb, len(cols))

    wide = range(0, D, CU)
    for l in range(DEPTH):
        for f in (1, 2):
            gate_up = [c + s * FF for c in range(0, FF, CU) for s in (0, 1)]
            phase(f"in{l}{f}", f"ffn{f}_w_in", l, NC8, gate_up)
            phase(f"out{l}{f}", f"ffn{f}_w_out", l, NF, wide)
            if f == 1:
                m = ("rec", "sg")[l]
                phase(m + "_b", m + "_w_in", 0, NC8, [D + c for c in wide])
                phase(m + "_a", m + "_w_in", 0, NC8, wide)
                phase(m + "_out", m + "_w_out", 0, NC8, wide)
    for l in range(DEPTH):
        for n, c in (("kv", [C_KV]), ("mif", [C_MIF]), ("aq", [C_AQ + c for c in wide]),
                     ("mqk", [C_MQK + c for c in wide]), ("mv", [C_MV + c for c in wide]),
                     ("mo", [C_MO + c for c in wide]), ("ag", [C_AG + c for c in wide]),
                     ("mg", [C_MG + c for c in wide])):
            phase(f"{n}{l}", "w_in_2", l, NC8, c)
        phase(f"proj{l}", "w_out_2", l, 2 * NC8, wide)
    return units, pairs, phases


UNITS, PAIRS, PHASES = plan()

STREAM = ("kv", "mif", "aq", "mqk", "mv", "mo", "ag", "mg")
STREAM_UNITS = sum(2 * PHASES[n + "0"][2] for n in STREAM)
ITEMS = [(g, hd) for g in range(2) for hd in [None, *range(8 * g, 8 * g + 8)]]
VISITS = {u: [] for u in range(STREAM_UNITS)}
for _c in range(9):
    VISITS[5 if _c == 0 else 7 + 2 * ((_c - 1) // 2)].append(("turn", _c))
VISITS[14].append(("rs", 0))
VISITS[15].append(("rt", 0))
VISITS[16].append(("rt", 1))
VISITS[17].append(("kx", 0))
for _c in range(6):
    VISITS[14 + 2 * (_c // 2)].append(("silu", _c))
DOUBLE = (22, 26, 30, 32)
for _v, _u in enumerate(sorted([*range(18, 35), *DOUBLE])):
    VISITS[_u].append(("att", _v))
assert _v == len(ITEMS) + 2
VISITS[24].append(("silu", 6))
VISITS[25].append(("silu", 7))
for _c in range(8):
    VISITS[23 + _c].append(("mvt", _c))
for _h in range(M_H):
    for _s, _at in enumerate((34, 36, 37, 39)):
        VISITS[4 * _h + _at].append(("ml", (_h, _s)))


OUT_GROUPS = [(0, 4, [0]), (0, 4, [1]), (4, 2, [0, 1]), (6, 2, [0, 1])]

GATES_AT = (3, 5, 7, 8)


def build_stack(nc: bass.Bass, consts, x, ffn1_norm, ffn1_w_in, ffn1_w_out, mix_norm, ffn2_norm, ffn2_w_in, ffn2_w_out,
                rec_w_in, rec_conv_w, rec_conv_b, rec_gate_a_w, rec_gate_a_b, rec_gate_x_w, rec_gate_x_b, rec_lambda,
                rec_w_out, sg_w_in, sg_v_norm, sg_w_s, sg_b_s, sg_w_out, final_norm, meta_2, norm_g_2, w_in_2,
                attn_q_norm_g_2, attn_k_norm_g_2, attn_sink_2, mlstm_conv_w_2, mlstm_conv_b_2, mlstm_b_i_2,
                mlstm_b_f_2, mlstm_out_norm_g_2, w_out_2, out):
    fp32, fp32r = mybir.dt.float32, mybir.dt.float32r
    ALU, ACT = mybir.AluOpType, mybir.ActivationFunctionType
    MUL, ADD, SUB, MAX, MIN = ALU.mult, ALU.add, ALU.subtract, ALU.max, ALU.min
    dram = dict(ffn1_w_in=ffn1_w_in, ffn1_w_out=ffn1_w_out, ffn2_w_in=ffn2_w_in, ffn2_w_out=ffn2_w_out,
                rec_w_in=rec_w_in, rec_w_out=rec_w_out, sg_w_in=sg_w_in, sg_w_out=sg_w_out, w_in_2=w_in_2,
                w_out_2=w_out_2)
    NU = len(UNITS)

    with ExitStack() as ctx:
        def sb(name, shape, dt=fp32):
            return ctx.enter_context(nc.sbuf_tensor(name, shape, dt))

        def sem(name):
            return ctx.enter_context(nc.semaphore(name))

        ctx.enter_context(nc.allow_non_contiguous_dma(reason="gate columns and biases of a few elements"))

        raw = sb("raw", [P, RING, KU, CU])
        w_hi = sb("w_hi", [P, RING, KU, CU], fp32r)
        w_lo = sb("w_lo", [P, RING, KU, CU], fp32r)
        h = sb("h", [P, NC8, L])
        x_hi = sb("x_hi", [P, NC8 * L], fp32r)
        x_lo = sb("x_lo", [P, NC8 * L], fp32r)
        y_hi = sb("y_hi", [P, NF * SEQ], fp32r)
        y_lo = sb("y_lo", [P, NF * SEQ], fp32r)
        con = sb("con", [P, CONST_ALL])
        ones = sb("ones", [P, P])
        par_rows = sb("par_rows", [P, 2, P])
        par = sb("par", [P, 2, P])
        rstd = sb("rstd", [P, L])
        rms = sb("rms", [P, L])
        sumsq = sb("sumsq", [P, L])
        sq = sb("sq", [P, L])
        epsc = sb("epsc", [P, 1])
        root_of_eps = sb("root_of_eps", [P, 1])
        work = sb("work", [P, WORK_SLOTS * L])
        pre = sb("pre", [P, 2, L + 3])
        bank = [ctx.enter_context(nc.psum_tensor(f"bank{i}", [P, 512], fp32)) for i in range(8)]

        def cst(name, rows=P):
            return con[0:rows, CONST_AT[name]:CONST_AT[name] + CONST_W[name]]

        ident, tri = cst("ident"), cst("tri")

        def pcol(name, k, rows=P):
            t, r, _ = PAR[name]
            return par[0:rows, t, r + k:r + k + 1]

        at = [0]

        def region(slots, width=L):
            o = at[0]
            at[0] += slots * width
            assert at[0] <= WORK_SLOTS * L, at[0]
            return work[:, o:o + slots * width].rearrange("p (c n) -> p c n", n=width)

        ffn_t, ffn_s, ffn_r, ffn_h = (region(2, SEQ) for _ in range(4))
        mixer_at = at[0]
        rec_t, rec_s = (work[:, o * SEQ:(o + 4) * SEQ].rearrange("p (c n) -> p c n", n=SEQ) for o in (0, 4))
        rec_y, rec_x, rec_a, rec_g = (region(NC8, SEQ) for _ in range(4))
        rec_p = region(NC8, SEQ + 3)
        blocks_a, blocks_x = region(NC8, P), region(NC8, P)
        decay = region(12, NC8)
        ws_raw, ws_t, bs_all = region(NC8, P), region(NC8, P), region(NC8, P)
        at[0] = mixer_at
        sg_u, sg_v, sg_s = (region(NC8, SEQ) for _ in range(3))
        v_tok = region(2, D)
        sg_r = region(8, 2)
        at[0] = 0
        q = region(NC8)
        k_att, k_swap, v_att = region(1)[:, 0], region(1)[:, 0], region(1)[:, 0]
        qk = region(NC8)
        mv = region(NC8)
        mvt = region(3, D)
        prob = region(2, AW)
        score = region(2, MW)
        pt = region(2, AW)
        va_t = region(3, P)
        q_tail = region(2, P)
        cos_g = region(2)
        rot_g = region(2, P)
        qsq = score[:, :, 0:L]
        qc, qs = pt[:, :, 0:L], prob[:, :, 0:L]
        norms = region(4, NT * NR)
        r_t = region(1)[:, 0]
        att_s = region(12, 4)
        g_row = region(6)
        g_tok = region(3, 8)
        den_s = region(8, 4)
        s_b = region(1)[:, 0]
        diag = region(3, P)
        m_arg, m_pt = score[:, 0, :], score[:, 1, :]
        n_sq = pt[:, :, 0:L]
        gate_x, gate_t = prob[:, :, 0:L], region(2)
        exp_b, m_b = gate_t[:, 0, :], gate_t[:, 1, :]
        g_x2 = cos_g
        sinks = sb("sinks", [P, DEPTH * ATT_H])
        sink_tail = sb("sink_tail", [P, 2 * DEPTH])
        neg_sinks = sb("neg_sinks", [P, DEPTH * ATT_H])
        neg_tail = sb("neg_tail", [P, 2 * DEPTH])
        gbias = sb("gbias", [4, 2 * DEPTH])
        xrow = work[:, 0:3 * D].rearrange("p (t n) -> p t n", n=D)
        orow = work[:, 0:2 * D].rearrange("p (t n) -> p t n", n=D)

        w_loaded = [sem(f"w_loaded{i}") for i in range(RING)]
        hi_made = sem("hi_made")
        lo_made = sem("lo_made")
        unit_done = sem("unit_done")
        first_done = sem("first_done")
        tile_read = sem("tile_read")
        act_hi = sem("act_hi")
        act_ready = sem("act_ready")
        act_new = sem("act_new")
        silu_done, gate_scaled = sem("silu_done"), sem("gate_scaled")
        par_loaded, con_loaded, x_loaded, blk_loaded, sg_loaded, first_par = (
            sem(n) for n in ("par_loaded", "con_loaded", "x_loaded", "blk_loaded", "sg_loaded", "first_par"))
        ones_set, zero_set, cleared = sem("ones_set"), sem("zero_set"), sem("cleared")
        par_t, par_ready, xt_done, xt_read = sem("par_t"), sem("par_ready"), sem("xt_done"), sem("xt_read")
        sq_done, last_sq, sum_done, rms_done = sem("sq_done"), sem("last_sq"), sem("sum_done"), sem("rms_done")
        pool_ch, dch, ach = sem("pool_ch"), sem("dch"), sem("ach")
        final_new, fin_sq, fin_sum = sem("final_new"), sem("fin_sq"), sem("fin_sum")
        decay_e, decay_v = sem("decay_e"), sem("decay_v")
        conv_new, gates_mm, gates_sig, gated_in, ax_new, a2_new, mult2, mult_new = (
            sem(n) for n in ("conv_new", "gates_mm", "gates_sig", "gated_in", "ax_new", "a2_new", "mult2", "mult_new"))
        rec_gelu, rec_bx, scanned = sem("rec_gelu"), sem("rec_bx"), sem("scanned")
        sg_gelu, sg_sqs, sg_sum, sg_rms = sem("sg_gelu"), sem("sg_sqs"), sem("sg_sum"), sem("sg_rms")
        ws_tr, ws_read, vt_tr, vt_read, sg_mm, sg_read = (
            sem(n) for n in ("ws_tr", "ws_read", "vt_tr", "vt_read", "sg_mm", "sg_read"))
        cos_ready, qsq_new, qc_new, turn_mm, q_ready = (
            sem(n) for n in ("cos_ready", "qsq_new", "qc_new", "turn_mm", "q_ready"))
        rs_new, rt_mm, rt_read, k_ready, tail_new = (
            sem(n) for n in ("rs_new", "rt_mm", "rt_read", "k_ready", "tail_new"))
        kx_mm, kx_read, k_swapped = sem("kx_mm"), sem("kx_read"), sem("k_swapped")
        s_mm, s_max, s_exp, s_rec, s_prob0, s_prob = (
            sem(n) for n in ("s_mm", "s_max", "s_exp", "s_rec", "s_prob0", "s_prob"))
        s_tr, s_pt, s_pv, s_out = sem("s_tr"), sem("s_pt"), sem("s_pv"), sem("s_out")
        g_nx, g_e, g_cm, g_exp = sem("g_nx"), sem("g_e"), sem("g_cm"), sem("g_exp")
        tap0, conv2_new, qk_tanh, qk_new, mt_tr, mt_read = (
            sem(n) for n in ("tap0", "conv2_new", "qk_tanh", "qk_new", "mt_tr", "mt_read"))
        m_bc, m_qk, m_arg_new, m_exp_new, m_pt_new = (
            sem(n) for n in ("m_bc", "m_qk", "m_arg_new", "m_exp_new", "m_pt_new"))
        m_num, m_sq, m_den, m_ms, ms_read = sem("m_num"), sem("m_sq"), sem("m_den"), sem("m_ms"), sem("ms_read")
        m_diag, m_bb, m_sb, m_hm = sem("m_diag"), sem("m_bb"), sem("m_sb"), sem("m_hm")
        gate_act, ot_tr, stored = sem("gate_act"), sem("ot_tr"), sem("stored")
        ot_read = [sem(f"ot_read{g}") for g in range(4)]

        block = ctx.enter_context(nc.Block())

        def xview(t, k, n):
            return t[:, k * n:(k + 1) * n]

        SPLITS = {}
        cnt = 0
        for name, k in [("x_in01", 8), ("y_out01", NF), ("x_rec_b", 8), ("y_rec_out", 8), ("x_in02", 8), ("y_out02", NF),
                        ("x_in11", 8), ("y_out11", NF), ("x_sg_b", 8), ("y_sg_out", 8), ("x_in12", 8), ("y_out12", NF),
                        ("x_kv0", 8), ("y_proj0", 16), ("x_kv1", 8), ("y_proj1", 16)]:
            SPLITS[name] = cnt
            cnt += k

        def units_of(pair):
            return PAIRS[pair]

        SG_LOADS = 16 * (3 + 16 * DEPTH + 3)

        @block.sync
        def _(sp):
            sp.dma_start(con[:, 0:P], consts[:, 0:P]).then_inc(con_loaded, 16)
            t, r, k = PAR["ffn1_norm"]
            sp.dma_start(par_rows[r:r + k, t, :], ffn1_norm.rearrange("l (c p) -> (l c) p", p=P)).then_inc(first_par, 16)
            for t in range(2):
                sp.dma_start(xrow[:, t, :], x[0, t * P:(t + 1) * P, :]).then_inc(x_loaded, 16)
            sp.dma_start(xrow[0:META, 2, :], meta_2).then_inc(x_loaded, 16)
            rows = dict(ffn1_norm=ffn1_norm, ffn2_norm=ffn2_norm, mix_norm=mix_norm,
                        rec_conv_b=rec_conv_b, rec_lambda=rec_lambda, sg_v_norm=sg_v_norm, norm_g_2=norm_g_2,
                        mlstm_conv_b_2=mlstm_conv_b_2, mlstm_out_norm_g_2=mlstm_out_norm_g_2)
            srcs = {n: a.rearrange("l (c p) -> (l c) p", p=P) for n, a in rows.items()}
            srcs["final_norm"] = final_norm.rearrange("(c p) -> c p", p=P)
            srcs["rec_conv_w"] = rec_conv_w[0].rearrange("k (c p) -> (k c) p", p=P)
            srcs["mlstm_conv_w_2"] = mlstm_conv_w_2.rearrange("l k (c p) -> (l k c) p", p=P)
            for n, a in (("rec_gate_a_b", rec_gate_a_b), ("rec_gate_x_b", rec_gate_x_b)):
                srcs[n] = a[0].rearrange("(c e) d -> c (e d)", e=2)
            srcs.pop("ffn1_norm")

            def parameters():
                for n, src in srcs.items():
                    t, r, k = PAR[n]
                    sp.dma_start(par_rows[r:r + k, t, :], src).then_inc(par_loaded, 16)
                for n, src in (("attn_q_norm_g_2", attn_q_norm_g_2), ("attn_k_norm_g_2", attn_k_norm_g_2)):
                    t, r, k = PAR[n]
                    for e in range(2):
                        sp.dma_start(par_rows[r:r + k, t, e * DH:(e + 1) * DH], src).then_inc(par_loaded, 16)

            def load(U, src, wait):
                n = UNITS[U][3]
                if wait is not None:
                    sp.wait_ge(lo_made, wait)
                sp.dma_start(raw[:, U % RING, 0:n, :], src).then_inc(w_loaded[U % RING], 16)

            small = [(ws_raw[:, :, :], sg_w_s[0].rearrange("h p q -> p h q")),
                     (bs_all[:, :, :], sg_b_s[0].rearrange("(o h) p -> o h p", o=1).broadcast_to((P, NC8, P))),
                     (sinks[:, :], attn_sink_2.rearrange("(o l) h -> o (l h)", o=1).broadcast_to((P, DEPTH * ATT_H)))]
            for g, src in enumerate((mlstm_b_i_2, mlstm_b_f_2)):
                small.append((gbias[:, g * DEPTH:(g + 1) * DEPTH], src.rearrange("l h -> h l")))
            for l in range(DEPTH):
                heads = attn_sink_2[l].rearrange("(g c e) -> g e c", g=2, e=2)
                for g in range(2):
                    for e in range(2):
                        src = heads[g, e].rearrange("(c o) -> c o", o=1).broadcast_to((4, TAIL))
                        dst = sink_tail[e * DH:(e + 1) * DH, 2 * l + g:2 * l + g + 1]
                        for c in range(4):
                            small.append((dst[c * TAIL:(c + 1) * TAIL, :], src[c:c + 1, :].rearrange("c t -> t c")))
            small.append((con[:, P:CONST_ALL], consts[:, P:CONST_ALL]))
            assert 16 * len(small) == SG_LOADS

            def straight(name, first=0):
                ub, pb, npairs = PHASES[name]
                for pr in range(pb + first, pb + npairs):
                    for U, _, n in PAIRS[pr]:
                        src, l, k0, n, c0 = UNITS[U]
                        a = dram[src][l]
                        if name == "out01":
                            for dst, s_ in small[2 * (U - ub):2 * (U - ub) + 2]:
                                sp.dma_start(dst, s_).then_inc(sg_loaded, 16)
                        if name.startswith("mif"):
                            sp.wait_ge(lo_made, U - RING + 1)
                            for g in range(2):
                                sp.dma_start(raw[:, U % RING, 0:n, 32 * g:32 * g + 4],
                                             a[k0 * P:(k0 + n) * P, c0 + 4 * g:c0 + 4 * g + 4].rearrange(
                                                 "(k p) n -> p k n", p=P)).then_inc(w_loaded[U % RING], 16)
                            continue
                        load(U, a[k0 * P:(k0 + n) * P, c0:c0 + CU].rearrange("(k p) n -> p k n", p=P),
                             U - RING + 1 if U >= RING else None)

            def gate_up(name):
                ub, pb, _ = PHASES[name]
                src, l, _, _, _ = UNITS[ub]
                cols = dram[src][l].rearrange("(s k p) (f j n) -> s f j p k n", k=KU, p=P, f=2, n=CU)
                first = 1 if ub == 0 else 0

                def turn(i):
                    for j in range(4):
                        U = ub + j
                        wait = U - RING + 1 + 4 * i
                        load(U, cols[j % 2, j // 2, i], None if isinstance(i, int) and wait <= 0 else wait)

                if first:
                    turn(0)
                    parameters()
                with sp.Fori(first, FF // CU) as i:
                    turn(i)

            gate_up("in01")
            sp.wait_ge(zero_set, 1)
            for dst, src in ((blocks_a, rec_gate_a_w), (blocks_x, rec_gate_x_w)):
                for e in range(2):
                    sp.dma_start(dst[e * DH:(e + 1) * DH, :, e * DH:(e + 1) * DH],
                                 src[0].rearrange("(c e) i j -> e i c j", e=2)[e]).then_inc(blk_loaded, 16)
            straight("out01")
            for n in ("rec_b", "rec_a", "rec_out"):
                straight(n)
            gate_up("in02")
            straight("out02")
            gate_up("in11")
            straight("out11")
            for n in ("sg_b", "sg_a", "sg_out"):
                straight(n)
            gate_up("in12")
            straight("out12")
            for l in range(DEPTH):
                for n in (*STREAM, "proj"):
                    straight(f"{n}{l}")
            for g, (c0, n, ts) in enumerate(OUT_GROUPS):
                sp.wait_ge(ot_read[g], 1)
                for t in ts:
                    cols = slice(c0 * P, (c0 + n) * P)
                    sp.dma_start(out[0, t * P:(t + 1) * P, cols], orow[:, t, cols]).then_inc(stored, 16)
            sp.wait_ge(stored, 16 * 6)

        MIF_UNITS = {U for l in range(DEPTH) for U, _, _ in PAIRS[PHASES[f"mif{l}"][1]]}
        LANDED = {}
        _c = [0] * RING
        for U in range(NU):
            _c[U % RING] += 32 if U in MIF_UNITS else 16
            LANDED[U] = _c[U % RING]
        LOOPED = {name: PHASES[name] for name in ("in01", "in02", "in11", "in12")}

        @block.tensor
        def _(pe):
            mm = nc.tensor.matmul

            def unit(U, k0, n, pair, npair_off, xs, N, first, last, ready, off, tiles=2, wide_x=False,
                     mid=None):
                hi, lo = xs
                pe.wait_ge(lo_made, U + 1 + off)
                s = U % RING
                for m in range(tiles):
                    T = 2 * pair + m
                    acc = bank[T % 4][:, 0:N]
                    if first and not (isinstance(off, int) and T - 3 + off // 2 <= 0):
                        pe.wait_ge(tile_read, T - 3 + tile_off(off))
                    for j in range(n):
                        k = k0 + j
                        if m == 0 and ready is not None:
                            pe.wait_ge(act_ready, ready + k + 1)
                        wh, wl = (t[:, s, j, m * P:(m + 1) * P] for t in (w_hi, w_lo))
                        if N == SEQ and wide_x:
                            xh, xl = (t[:, k * L + META:(k + 1) * L] for t in (hi, lo))
                        else:
                            xh, xl = xview(hi, k, N), xview(lo, k, N)
                        mm(acc, wh, xh, start=first and j == 0, stop=False)
                        mm(acc, wh, xl, start=False, stop=False)
                        i_ = mm(acc, wl, xh, start=False, stop=last and j == n - 1)
                    if last and m == 0 and tiles == 2:
                        i_.then_inc(first_done, 1)
                    if m == 0 and mid is not None:
                        mid()
                i_.then_inc(unit_done, 1)

            def tile_off(off):
                return off // 2 if isinstance(off, int) else off_half[0]

            off_half = [0]

            def pair(pr, xs, N, ready=None, after=None, tiles=2, wide_x=False, mid=None):
                us = units_of(pr)
                for j, (U, k0, n) in enumerate(us):
                    unit(U, k0, n, pr, 0, xs, N, j == 0, j == len(us) - 1, ready, 0, tiles, wide_x, mid)
                    if after is not None:
                        after(j)

            xs, ys = (x_hi, x_lo), (y_hi, y_lo)

            def norm_sum(n, T0):
                pe.wait_ge(sq_done, n + 1)
                mm(bank[4][:, T0:L], ones[:, :], sumsq[:, T0:L], start=True, stop=False)
                pe.wait_ge(last_sq, n + 1)
                mm(bank[4][:, T0:L], ones[:, :], rms[:, T0:L], start=False, stop=True).then_inc(sum_done, 1)

            def in_phase(name, n, ready):
                ub, pb, _ = PHASES[name]
                for p in range(2):
                    pair(pb + p, xs, SEQ, ready=ready if p == 0 else None,
                         after=(lambda j: norm_sum(n, META) if j == 1 else None) if p == 0 else None)
                if name == "in01":
                    parameters()
                with pe.Fori(1, FF // CU) as i:
                    off_half[0] = 4 * i
                    for p in range(2):
                        us = units_of(pb + p)
                        for j, (U, k0, nk) in enumerate(us):
                            unit(U, k0, nk, pb + p, 0, xs, SEQ, j == 0, j == 1, None, 4 * i)

            def out_phase(name, ready, N=SEQ, after=None):
                ub, pb, npairs = PHASES[name]
                for p in range(npairs):
                    pair(pb + p, ys, N, ready=ready if p == 0 else None)

            pe.wait_ge(con_loaded, 16)
            pe.wait_ge(first_par, 16)
            nc.tensor.transpose(bank[0][:, 0:16], par_rows[0:16, 0, :], ident[0:16, 0:16]).then_inc(par_t, 1)
            pe.wait_ge(x_loaded, 48)
            for c in range(NC8):
                b = bank[4 + c % 4]
                if c >= 4:
                    pe.wait_ge(xt_read, c - 3)
                nc.tensor.transpose(b[:, 0:META], xrow[0:META, 2, c * P:(c + 1) * P], ident[0:META, 0:META])
                for t in range(2):
                    i_ = nc.tensor.transpose(b[:, META + t * P:META + (t + 1) * P], xrow[:, t, c * P:(c + 1) * P], ident)
                i_.then_inc(xt_done, 1)
            pe.wait_ge(ones_set, 1)
            pe.wait_ge(par_ready, 1)

            def parameters():
                pe.wait_ge(par_loaded, 16 * 17)
                pe.wait_ge(xt_read, NC8)
                for t in range(2):
                    rows = sum(k for (tt, _, k) in PAR.values() if tt == t)
                    i_ = nc.tensor.transpose(bank[5][:, t * P:t * P + rows], par_rows[0:rows, t, :], ident[0:rows, 0:rows])
                i_.then_inc(par_t, 1)

            in_phase("in01", 0, SPLITS["x_in01"])
            out_phase("out01", SPLITS["y_out01"])

            def gate_products(p):
                for c in (2 * p, 2 * p + 1):
                    pe.wait_ge(conv_new, c + 1)
                    if c >= 4:
                        pe.wait_ge(gates_sig, 2 * (c - 3))
                    mm(bank[4 + c % 4][:, 0:SEQ], blocks_a[:, c, :], rec_x[:, c, :], start=True, stop=True)
                    mm(bank[4 + c % 4][:, SEQ:2 * SEQ], blocks_x[:, c, :], rec_x[:, c, :], start=True,
                       stop=True).then_inc(gates_mm, 1)

            pb = PHASES["rec_b"][1]
            for p in range(8):
                def after(j, r0=2 * p):
                    if r0 + j == 1:
                        norm_sum(1, META)
                    if r0 + j == 3:
                        pe.wait_ge(blk_loaded, 64)
                        pe.wait_ge(rms_done, 2)
                    if r0 + j in GATES_AT:
                        gate_products(GATES_AT.index(r0 + j))

                pair(pb + p, xs, SEQ, ready=SPLITS["x_rec_b"] if p == 0 else None, after=after)
            out_phase("rec_out", SPLITS["y_rec_out"])

            in_phase("in02", 2, SPLITS["x_in02"])
            out_phase("out02", SPLITS["y_out02"])
            in_phase("in11", 3, SPLITS["x_in11"])
            out_phase("out11", SPLITS["y_out11"])

            ub, pb, _ = PHASES["sg_b"]
            for p in range(4):
                pair(pb + p, xs, SEQ, ready=SPLITS["x_sg_b"] if p == 0 else None,
                     after=(lambda j: norm_sum(4, META) if j == 1 else None) if p == 0 else None)
                if p == 0:
                    pe.wait_ge(sg_loaded, SG_LOADS)
                    for c in range(NC8):
                        i_ = nc.tensor.transpose(bank[5 + c // 4][:, (c % 4) * P:(c % 4 + 1) * P], ws_raw[:, c, :], ident)
                    i_.then_inc(ws_tr, 1)
            ub, pb, _ = PHASES["sg_a"]
            pair(pb, xs, SEQ)
            pe.wait_ge(sg_sqs, 1)
            pe.wait_ge(rms_done, 5)
            for t in range(2):
                i_ = mm(bank[4][:, t:t + 1], sumsq[:, META + t * P:META + (t + 1) * P], ones[:, 0:1], start=True, stop=True)
            i_.then_inc(sg_sum, 1)
            pe.wait_ge(ws_read, 2)
            for g in range(4):
                t, c0 = g // 2, 4 * (g % 2)
                if g == 3:
                    pe.wait_ge(vt_read, 1)
                for c in range(c0, c0 + 4):
                    i_ = nc.tensor.transpose(bank[5 + g % 3][:, (c % 4) * P:(c % 4 + 1) * P],
                                             sg_v[:, c, t * P:(t + 1) * P], ident)
                i_.then_inc(vt_tr, 1)
            pair(pb + 1, xs, SEQ)
            for c in range(NC8):
                if c == 0:
                    pe.wait_ge(vt_read, 4)
                if c >= 4:
                    pe.wait_ge(sg_read, c - 3)
                for t in range(2):
                    i_ = mm(bank[4 + c % 4][:, t * P:(t + 1) * P], v_tok[:, t, c * P:(c + 1) * P], ws_t[:, c, :],
                            start=True, stop=True)
                i_.then_inc(sg_mm, 1)
            for p in range(2, 4):
                pair(pb + p, xs, SEQ)
            out_phase("sg_out", SPLITS["y_sg_out"])

            in_phase("in12", 5, SPLITS["x_in12"])
            out_phase("out12", SPLITS["y_out12"])
            norm_sum(6, META)

            tr = nc.tensor.transpose

            def rows_of(g, pb):
                c0, n, ts = OUT_GROUPS[g]
                pe.wait_ge(tile_read, 2 * pb + c0 + n)
                for i, t in enumerate(ts):
                    for c in range(n):
                        i_ = tr(bank[4 + g][:, (i * n + c) * P:(i * n + c + 1) * P],
                                h[:, c0 + c, META + t * P:META + (t + 1) * P], ident)
                i_.then_inc(ot_tr, 1)

            for l in range(DEPTH):
                I0 = len(ITEMS) * l

                def turn(c):
                    n = 9 * l + c
                    if c == 0:
                        pe.wait_ge(rms_done, 8 + l)
                        if l:
                            pe.wait_ge(m_hm, M_H * l)
                    pe.wait_ge(qsq_new, n + 1)
                    for t, (a, b) in enumerate(LT):
                        at = NR * t + 2 * c
                        mm(bank[4][0:b - a, at:at + 2], qsq[:, n % 2, a:b], cst("head_mean"), start=True, stop=True)
                    pe.wait_ge(qc_new, n + 1)
                    pe.wait_ge(cos_ready, l + 1)
                    if c >= 2:
                        pe.wait_ge(q_ready, n - 1)
                    mm(bank[5 + n % 2][:, 0:L], rot_g[:, 0 if c else 1, :], qs[:, n % 2, :], start=True,
                       stop=True).then_inc(turn_mm, 1)

                def rt(step):
                    if step:
                        pe.wait_ge(rt_read, l + 1)
                        at = CONST_AT["sel"]
                        mm(bank[6][:, 0:L], con[0:NR, at:at + P], r_t[0:NR, :], start=True, stop=True)
                        for c in range(NC8):
                            at = CONST_AT["sel"] + (c + 1) * P
                            i_ = mm(bank[7][:, c * TAIL:(c + 1) * TAIL], con[0:NR, at:at + P], r_t[0:NR, 2 * P:L],
                                    start=True, stop=True)
                        i_.then_inc(rt_mm, 1)
                        return
                    pe.wait_ge(rs_new, l + 1)
                    pe.wait_ge(q_ready, 9 * (l + 1))
                    for t, (a, b) in enumerate(LT):
                        i_ = tr(bank[5][0:NR, a:b], norms[0:b - a, 3, NR * t:NR * (t + 1)], ident[0:b - a, 0:b - a])
                    i_.then_inc(rt_mm, 1)

                def kx():
                    pe.wait_ge(k_ready, l + 1)
                    mm(bank[4][:, 0:L], cst("swap"), k_att, start=True, stop=True)
                    for t, (a, b) in enumerate(LT):
                        tr(bank[5][0:b - a, t * P:(t + 1) * P], v_att[:, a:b], ident)
                    pe.wait_ge(g_exp, l + 1)
                    for t, (a, b) in enumerate(LT):
                        for w, r in enumerate((3, 5)):
                            at = 3 * P + 8 * t + 4 * w
                            i_ = tr(bank[5][0:b - a, at:at + 4], g_row[0:4, r, a:b], ident[0:4, 0:4])
                    i_.then_inc(kx_mm, 1)

                def att(v):
                    if 2 <= v <= len(ITEMS) + 1:
                        g, hd = ITEMS[v - 2]
                        n = I0 + v - 2
                        p = prob[:, v % 2, :]
                        pe.wait_ge(s_prob0, n + 1)
                        if v >= 3:
                            pe.wait_ge(s_pt, n)
                        for j in range(3):
                            if j == 1:
                                pe.wait_ge(s_prob, n + 1)
                            if hd is None and j == 2:
                                i_ = tr(bank[5][0:TAIL, 2 * P:3 * P], p[:, 2 * P:2 * P + TAIL], ident)
                            else:
                                i_ = tr(bank[5][:, j * P:(j + 1) * P], p[:, j * P:(j + 1) * P], ident)
                        i_.then_inc(s_tr, 1)
                    if v < len(ITEMS):
                        g, hd = ITEMS[v]
                        n = I0 + v
                        if v == 0:
                            pe.wait_ge(k_swapped, l + 1)
                            pe.wait_ge(kx_read, l + 1)
                        else:
                            pe.wait_ge(s_max, n)
                        if hd is None:
                            pe.wait_ge(tail_new, 2 * l + g + 1)
                            rows = slice(g * DH, (g + 1) * DH)
                            i_ = mm(bank[4][:, 0:L], q_tail[rows, g, :], k_att[rows, :], start=True, stop=True)
                        else:
                            e = hd % 2
                            rows = slice(e * DH, (e + 1) * DH)
                            kk = k_att if g == e else k_swap
                            qh = q[rows, hd // 2, :]
                            mm(bank[4][:, 0:P], qh[:, 0:P], kk[rows, 0:P], start=True, stop=True)
                            i_ = mm(bank[4][:, P:3 * P], qh[:, P:2 * P], kk[rows, 0:2 * P], start=True, stop=True)
                        i_.then_inc(s_mm, 1)
                    if v >= 3:
                        g, hd = ITEMS[v - 3]
                        n = I0 + v - 3
                        vc = slice(g * DH, (g + 1) * DH)
                        p = pt[:, (v - 3) % 2, :]
                        pe.wait_ge(s_pt, n + 1)
                        if hd is None:
                            if n > 0:
                                pe.wait_ge(s_out, (n // 9) * 5)
                            for e in range(2):
                                o, cols = bank[7][e * DH:(e + 1) * DH, 0:DH], slice(e * DH, (e + 1) * DH)
                                mm(o, va_t[:, 0, vc], p[:, 0:P][:, cols], start=True, stop=False)
                                mm(o, va_t[:, 1, vc], p[:, P:2 * P][:, cols], start=False, stop=False)
                                i_ = mm(o, va_t[0:TAIL, 2, vc], p[0:TAIL, 2 * P:3 * P][:, cols], start=False, stop=True)
                        else:
                            e = hd % 2
                            if e == 0:
                                pe.wait_ge(s_out, (n // 9) * 5 + 1 + (n % 9 - 1) // 2)
                            o = bank[7][e * DH:(e + 1) * DH, :]
                            mm(o[:, 0:2 * P], va_t[:, 0, vc], p[:, 0:2 * P], start=True, stop=False)
                            i_ = mm(o[:, P:2 * P], va_t[:, 1, vc], p[:, 2 * P:3 * P], start=False, stop=True)
                        i_.then_inc(s_pv, 1)

                def mvt_chunk(c):
                    n = NC8 * l + c
                    pe.wait_ge(tile_read, 2 * PHASES[f"mv{l}"][1] + c + 1)
                    if n:
                        pe.wait_ge(mt_read, n)
                    for t, (a, b) in enumerate(LT):
                        i_ = tr(bank[6][0:b - a, t * P:(t + 1) * P], mv[:, c, a:b], ident)
                    i_.then_inc(mt_tr, 1)

                def ml(hd, stage):
                    n = M_H * l + hd
                    if stage == 0:
                        if hd == 0:
                            pe.wait_ge(qk_new, NC8 * (l + 1))
                            pe.wait_ge(s_max, I0 + len(ITEMS))
                            pe.wait_ge(s_pt, I0 + len(ITEMS))
                        else:
                            pe.wait_ge(ms_read, n)
                        mm(bank[4][:, 0:L], ident[0:4, hd:hd + 1].broadcast_to((4, P)), g_row[0:4, 4, :], start=True,
                           stop=True).then_inc(m_bc, 1)
                        for t, (a, b) in enumerate(LT):
                            i_ = mm(bank[5][0:b - a, MOFF[t]:MOFF[t] + L - a], qk[:, 4 + hd, a:b], qk[:, hd, a:L],
                                    start=True, stop=True)
                        i_.then_inc(m_qk, 1)
                    if stage == 1:
                        pe.wait_ge(m_pt_new, n + 1)
                        if hd == 0:
                            pe.wait_ge(mt_read, NC8 * (l + 1))
                            pe.wait_ge(s_out, 10 * (l + 1))
                        else:
                            pe.wait_ge(m_hm, n)
                        for w in range(2):
                            for t, (a, b) in enumerate(LT):
                                at = (2 * hd + w) * P
                                mm(bank[6 + w][:, a:L], mvt[0:b - a, t, at:at + P], m_pt[0:b - a, MOFF[t]:MOFF[t] + L - a],
                                   start=t == 0, stop=t == 2)
                        for j, (ja, jb) in enumerate(LT):
                            for t, (a, b) in enumerate(LT[:j + 1]):
                                at = MOFF[t] + ja - a
                                i_ = mm(bank[4][0:jb - ja, 400 + j:401 + j], m_pt[0:b - a, at:at + jb - ja],
                                        ones[0:b - a, 0:1], start=t == 0, stop=t == j)
                        i_.then_inc(m_num, 1)
                    if stage == 2:
                        pe.wait_ge(m_sq, n + 1)
                        pe.wait_ge(m_den, n + 1)
                        for j, (a, b) in enumerate(LT):
                            for w in range(2):
                                i_ = mm(bank[4][0:b - a, 408 + j:409 + j], n_sq[:, w, a:b], ones[:, 0:1], start=w == 0,
                                        stop=w == 1)
                        i_.then_inc(m_ms, 1)
                    if stage == 3:
                        pe.wait_ge(m_diag, n + 1)
                        if hd < M_H - 1:
                            pe.wait_ge(m_pt_new, n + 2)
                        for j, (a, b) in enumerate(LT):
                            i_ = mm(bank[5][:, a:b], ones[0:b - a, :], diag[0:b - a, j, 0:b - a], start=True, stop=True)
                        i_.then_inc(m_bb, 1)

                do = dict(turn=turn, rs=lambda n: None, rt=rt, kx=lambda n: kx(), att=att,
                          silu=lambda n: None, mvt=mvt_chunk, ml=lambda hs: ml(*hs))
                u = [0]

                def visits(j):
                    if l == 0 and u[0] == 1:
                        pe.wait_ge(fin_sum, 1)
                        mm(bank[4][:, 0:L], ones[:, :], sumsq[:, 0:L], start=True, stop=True).then_inc(sum_done, 1)
                    if l == 1 and u[0] == 0:
                        norm_sum(7, 0)
                    steps = VISITS[u[0]]
                    for kind, n in steps[early(steps):]:
                        do[kind](n)
                    u[0] += 1

                def early(steps):
                    return int([k for k, _ in steps[0:2]] == ["att", "att"])

                def mid():
                    steps = VISITS[u[0]]
                    for kind, n in steps[:early(steps)]:
                        do[kind](n)

                for ph in STREAM:
                    pb = PHASES[f"{ph}{l}"][1]
                    narrow = l == DEPTH - 1 and ph in ("aq", "mo", "ag", "mg")
                    for p in range(PHASES[f"{ph}{l}"][2]):
                        pair(pb + p, xs, SEQ if narrow else L, ready=SPLITS[f"x_kv{l}"] if ph == "kv" else None,
                             after=visits, tiles=1 if ph == "mif" else 2, wide_x=narrow, mid=mid)
                pb = PHASES[f"proj{l}"][1]
                narrow = l == DEPTH - 1
                for p in range(4):
                    pair(pb + p, ys, SEQ if narrow else L, ready=SPLITS[f"y_proj{l}"] if p == 0 else None, wide_x=narrow)
                    if narrow and p == 2:
                        rows_of(0, pb)
                        rows_of(1, pb)
                if narrow:
                    rows_of(2, pb)
                    rows_of(3, pb)

        @block.scalar
        def _(act):
            activation = nc.scalar.activation
            chain = [0]

            def split_w(U, off=0):
                if U >= NU:
                    return
                n, s = UNITS[U][3], U % RING
                act.wait_ge(w_loaded[s], LANDED[U] + (off * 4 if not isinstance(off, int) else 4 * off))
                if not (isinstance(off, int) and U - RING + 1 + off <= 0):
                    act.wait_ge(unit_done, U - RING + 1 + off)
                nc.scalar.copy(w_hi[:, s, 0:n, :], raw[:, s, 0:n, :]).then_inc(hi_made, 1)

            def split_x(dst, k, N, src, scale=None):
                if scale is None:
                    i_ = nc.scalar.copy(xview(dst, k, N), src)
                else:
                    i_ = activation(xview(dst, k, N), src, ACT.Copy, scale=scale)
                i_.then_inc(act_hi, 1)

            def ahead(pr):
                for U, _, _ in units_of(pr):
                    split_w(U + LEAD)

            def last_square(src, T0):
                activation(rms[:, T0:L], src, ACT.Square).then_inc(last_sq, 1)

            def root_table():
                activation(root_of_eps[:, 0:1], epsc[:, 0:1], ACT.Sqrt)

            def root(n, T0):
                root_table()
                act.wait_ge(sum_done, n + 1)
                activation(rms[:, T0:L], bank[4][:, T0:L], ACT.Sqrt, scale=1.0 / D, bias=epsc[:, 0:1]).then_inc(rms_done, 1)

            def gate_turn(pb, ub, i, first=None):
                o4, o = 4 * i, (4 * i if not isinstance(i, int) else 4 * i)
                for U in (ub, ub + 1):
                    split_w(U + LEAD, o)
                if first is not None:
                    root(first, META)
                for m in range(2):
                    act.wait_ge(tile_read, 2 * pb + m + 1 + o4)
                    activation(ffn_s[:, m, :], ffn_t[:, m, :], ACT.Silu).then_inc(silu_done, 1)
                for U in (ub + 2, ub + 3):
                    split_w(U + LEAD, o)
                for m in range(2):
                    act.wait_ge(tile_read, 2 * pb + 2 + m + 1 + o4)
                    if isinstance(i, int):
                        dst = xview(y_hi, 2 * i + m, SEQ)
                    else:
                        dst = y_hi[:, bass.ds(i * (2 * SEQ) + m * SEQ, SEQ)]
                        act.wait_ge(tile_read, 1)
                    nc.scalar.copy(dst, ffn_h[:, m, :]).then_inc(act_hi, 1)

            def in_phase(name, n):
                ub, pb, _ = PHASES[name]
                gate_turn(pb, ub, 0, first=n)
                with act.Fori(1, FF // CU) as i:
                    gate_turn(pb, ub, i)

            def out_phase(name, g, N=SEQ, T0=META, before=None, sq=True):
                ub, pb, npairs = PHASES[name]
                for p in range(npairs):
                    for U, _, _ in units_of(pb + p):
                        split_w(U + LEAD)
                        if before is not None:
                            before()
                            before = None
                    for m in range(2):
                        c = 2 * p + m
                        act.wait_ge(tile_read, 2 * (pb + p) + m + 1)
                        if g is not None:
                            split_x(x_hi, c, N, h[:, c, T0:L], g(c))
                        if c == NC8 - 1 and sq:
                            last_square(h[:, c, T0:L], T0)

            act.wait_ge(par_ready, 1)
            for c in range(NC8):
                act.wait_ge(xt_read, c + 1)
                split_x(x_hi, c, SEQ, h[:, c, META:L], pcol("ffn1_norm", c))
                if c == 2:
                    split_w(0)
            split_w(1)
            last_square(h[:, NC8 - 1, META:L], META)
            split_w(2)
            in_phase("in01", 0)
            act.wait_ge(decay_v, 1)
            activation(decay[:, 1, :], decay[:, 0, :], ACT.Exp).then_inc(decay_e, 1)
            out_phase("out01", lambda c: pcol("mix_norm", c))

            pb = PHASES["rec_b"][1]

            def gates(cs):
                for c in cs:
                    act.wait_ge(gates_mm, c + 1)
                    for k, (dst, b) in enumerate(((rec_a, "rec_gate_a_b"), (rec_g, "rec_gate_x_b"))):
                        activation(dst[:, c, :], bank[4 + c % 4][:, k * SEQ:(k + 1) * SEQ], ACT.Sigmoid,
                                   bias=pcol(b, c)).then_inc(gates_sig, 1)

            def decays(cs):
                act.wait_ge(decay_v, 2)
                act.wait_ge(gates_sig, 2 * cs[-1] + 2)
                if cs[0]:
                    act.wait_ge(mult2, 4)
                for c in cs:
                    activation(rec_t[:, c % 4, :], rec_a[:, c, :], ACT.Tanh, scale=decay[:, 3, c:c + 1]).then_inc(ach, 1)
                chain[0] += len(cs)
                act.wait_ge(ach, chain[0])
                for c in cs:
                    activation(rec_a[:, c, :], rec_a[:, c, :], ACT.Exp, scale=decay[:, 2, c:c + 1]).then_inc(ax_new, 1)

            def mult():
                for b in (0, 4):
                    act.wait_ge(mult2, b + 4)
                    r = rec_p[:, b:b + 4, 0:SEQ]
                    activation(r, r, ACT.Sqrt).then_inc(mult_new, 1)

            def gelu(c, n):
                act.wait_ge(tile_read, 2 * (pb + 4) + c + n)
                activation(rec_y[:, c:c + n, :], rec_y[:, c:c + n, :], ACT.Gelu_apprx_tanh).then_inc(rec_gelu, n)

            def upper(cs):
                for c in cs:
                    act.wait_ge(act_new, c + 1)
                    split_x(y_hi, c, SEQ, rec_y[:, c, :])

            r = 0
            for p in range(8):
                for U, _, _ in units_of(pb + p):
                    if r == 13:
                        gelu(0, 4)
                    split_w(U + LEAD)
                    if r == 1:
                        root(1, META)
                    if r == 5:
                        gates(range(4))
                    if r == 7:
                        decays(range(4))
                    if r == 8:
                        gates(range(4, 8))
                    if r == 10:
                        decays(range(4, 8))
                    if r == 12:
                        mult()
                    if r == 14:
                        upper(range(4))
                        gelu(4, 2)
                    r += 1
            gelu(6, 2)
            upper(range(4, 8))
            out_phase("rec_out", lambda c: pcol("ffn2_norm", c))

            in_phase("in02", 2)
            out_phase("out02", lambda c: pcol("ffn1_norm", NC8 + c))
            in_phase("in11", 3)
            out_phase("out11", lambda c: pcol("mix_norm", NC8 + c))

            _, pb, _ = PHASES["sg_b"]
            for p in range(4):
                ahead(pb + p)
                if p == 0:
                    root(4, META)
                for m in range(2):
                    c = 2 * p + m
                    act.wait_ge(tile_read, 2 * pb + c + 1)
                    activation(sg_v[:, c, :], sg_v[:, c, :], ACT.Gelu_apprx_tanh).then_inc(sg_gelu, 1)
            _, pb, _ = PHASES["sg_a"]
            for p in range(4):
                ahead(pb + p)
                if p == 0:
                    act.wait_ge(sg_sum, 1)
                    activation(sg_r[:, 0, :], bank[4][:, 0:2], ACT.Sqrt, scale=1.0 / D, bias=epsc[:, 0:1]).then_inc(sg_rms, 1)
                if p == 3:
                    for c in range(4):
                        act.wait_ge(act_new, NC8 + c + 1)
                        split_x(y_hi, c, SEQ, sg_s[:, c, :])
                for m in range(2):
                    c = 2 * p + m
                    act.wait_ge(tile_read, 2 * pb + c + 1)
                    activation(sg_u[:, c, :], sg_u[:, c, :], ACT.Gelu_apprx_tanh).then_inc(sg_gelu, 1)
            for c in range(4, NC8):
                act.wait_ge(act_new, NC8 + c + 1)
                split_x(y_hi, c, SEQ, sg_s[:, c, :])
            out_phase("sg_out", lambda c: pcol("ffn2_norm", NC8 + c))

            in_phase("in12", 5)
            out_phase("out12", None)
            root(6, META)
            for c in range(NC8):
                act.wait_ge(final_new, c + 1)
                split_x(x_hi, c, L, h[:, c, :], pcol("norm_g_2", c))
                activation(mv[:, c, :], h[:, c, :], ACT.Square).then_inc(fin_sq, 1)

            for l in range(DEPTH):
                I0 = len(ITEMS) * l
                T0 = META if l == DEPTH - 1 else 0

                def turn(c):
                    n = 9 * l + c
                    src = k_att if c == 0 else q[:, c - 1, :]
                    act.wait_ge(tile_read, 2 * PHASES[f"kv{l}"][1] + 1 if c == 0 else 2 * PHASES[f"aq{l}"][1] + c)
                    if n >= 2:
                        act.wait_ge(turn_mm, n - 1)
                    if c == 0 and l:
                        act.wait_ge(m_hm, M_H * l)
                    activation(qsq[:, n % 2, :], src, ACT.Square).then_inc(qsq_new, 1)

                def rt():
                    act.wait_ge(rt_mm, 2 * l + 1)
                    nc.scalar.copy(r_t[0:NR, :], bank[5][0:NR, 0:L]).then_inc(rt_read, 1)

                def kx():
                    act.wait_ge(kx_mm, l + 1)
                    nc.scalar.copy(k_swap, bank[4][:, 0:L]).then_inc(k_swapped, 1)

                def att(v):
                    if 2 <= v <= len(ITEMS) + 1:
                        g, hd = ITEMS[v - 2]
                        n = I0 + v - 2
                        act.wait_ge(s_tr, n + 1)
                        if v >= 4:
                            act.wait_ge(s_pv, n - 1)
                        dst = pt[:, v % 2, :]
                        if hd is None:
                            nc.scalar.copy(dst[:, 0:2 * P], bank[5][:, 0:2 * P])
                            i_ = nc.scalar.copy(dst[0:TAIL, 2 * P:AW], bank[5][0:TAIL, 2 * P:AW])
                        else:
                            i_ = nc.scalar.copy(dst, bank[5][:, 0:AW])
                        i_.then_inc(s_pt, 1)
                    if v < len(ITEMS):
                        g, hd = ITEMS[v]
                        n = I0 + v
                        i = v % 2
                        act.wait_ge(s_max, n + 1)
                        if v >= 2:
                            act.wait_ge(s_tr, n - 1)
                        s, pr = score[:, i, :], prob[:, i, :]
                        nm, den, es = att_s[:, 3 * i + 1, :], att_s[:, 3 * i + 2, :], att_s[:, 6 + i, :]
                        sink = sink_tail[:, 2 * l + g:2 * l + g + 1] if hd is None else sinks[:, l * ATT_H + hd:l * ATT_H + hd + 1]
                        activation(es[:, 0:2], nm[:, 0:2], ACT.Exp, bias=sink)
                        rq = [norms[:, 3, NR * t + 2 + hd:NR * t + 3 + hd] for t in range(2)] if hd is not None else None
                        if hd is None:
                            i_ = activation(pr[:, 0:L], s[:, 0:L], ACT.Exp, bias=nm[:, 0:1], accum_out=den[:, 0:1])
                        else:
                            activation(pr[:, 0:P], s[:, 0:P], ACT.Exp, scale=rq[0], bias=nm[:, 0:1], accum_out=den[:, 0:1])
                            i_ = activation(pr[:, P:AW], s[:, P:AW], ACT.Exp, scale=rq[1], bias=nm[:, 1:2],
                                            accum_out=den[:, 1:2])
                        i_.then_inc(s_exp, 1)

                def silu(c):
                    act.wait_ge(conv2_new, NC8 * l + c + 1)
                    if c >= 2:
                        act.wait_ge(qk_new, NC8 * l + c - 1)
                    activation(gate_t[:, c % 2, :], qk[:, c, :], ACT.Tanh, scale=0.5).then_inc(qk_tanh, 1)

                def mvt_chunk(c):
                    act.wait_ge(mt_tr, NC8 * l + c + 1)
                    nc.scalar.copy(mvt[:, 0:2, c * P:(c + 1) * P], bank[6][:, 0:2 * P].rearrange("p (t n) -> p t n", n=P))
                    nc.scalar.copy(mvt[0:TAIL, 2, c * P:(c + 1) * P], bank[6][0:TAIL, 2 * P:3 * P]).then_inc(mt_read, 1)

                def ml(hd, stage):
                    n = M_H * l + hd
                    if stage == 0:
                        act.wait_ge(m_bc, n + 1)
                        if n:
                            act.wait_ge(m_pt_new, n)
                        def e(t, x0, x1, src):
                            a, b = LT[t]
                            return activation(m_arg[0:b - a, MOFF[t] + x0 - a:MOFF[t] + x1 - a], src, ACT.Exp, scale=-1.0,
                                              bias=g_tok[0:b - a, t, hd:hd + 1])
                        act.wait_ge(m_arg_new, n + 1)
                        e(0, P, L, bank[4][:, P:L])
                        e(1, 2 * P, L, bank[4][:, 2 * P:L])
                        for t, (a, b) in enumerate(LT):
                            i_ = e(t, a, b, m_arg[0:b - a, MOFF[t]:MOFF[t] + b - a])
                        i_.then_inc(m_exp_new, 1)
                    if stage == 1:
                        act.wait_ge(m_num, n + 1)
                        for w in range(2):
                            i_ = activation(n_sq[:, w, :], bank[6 + w][:, 0:L], ACT.Square)
                        i_.then_inc(m_sq, 1)
                    if stage == 3:
                        act.wait_ge(m_bb, n + 1)
                        if n:
                            act.wait_ge(m_hm, n)
                        nc.scalar.copy(s_b, bank[5][:, 0:L]).then_inc(m_sb, 1)

                def nothing(n):
                    return None

                do = dict(turn=turn, rs=nothing, rt=lambda n: rt() if n == 0 else None, kx=lambda n: kx(), att=att,
                          silu=silu, mvt=mvt_chunk, ml=lambda hs: ml(*hs))

                def gate_chunks(ph, p):
                    for m in range(2):
                        c = 2 * p + m
                        k = c if ph == "ag" else NC8 + c
                        act.wait_ge(act_new, 16 + 16 * l + k + 1)
                        src = q if ph == "ag" else mv
                        i_ = nc.scalar.copy(y_hi[:, k * L + T0:(k + 1) * L], src[:, c, T0:L])
                        i_.then_inc(act_hi, 1)

                u = 0
                later = None
                for ph in STREAM:
                    pb = PHASES[f"{ph}{l}"][1]
                    for p in range(PHASES[f"{ph}{l}"][2]):
                        for j, (U, _, _) in enumerate(units_of(pb + p)):
                            split_w(U + LEAD)
                            steps = VISITS[u]
                            if len(steps) == 1 and steps[0][0] == "ml" and steps[0][1][1] == 0:
                                ml(*steps[0][1])
                                steps = []
                            if later:
                                gate_chunks(*later)
                                later = None
                            if u == 1 and l == 0 or u == 0 and l == 1:
                                root(7 + l, 0)
                            if j == 1:
                                T = 2 * (pb + p)
                                if ph == "mif":
                                    act.wait_ge(g_nx, l + 1)
                                    activation(g_row[0:4, 2, :], g_row[0:4, 1, :], ACT.Exp).then_inc(g_e, 1)
                                if ph == "mqk" and p == 0:
                                    act.wait_ge(g_cm, l + 1)
                                    activation(g_row[0:4, 5, :], g_row[0:4, 5, :], ACT.Exp, scale=-1.0).then_inc(g_exp, 1)
                                if ph == "mqk":
                                    for m in range(2):
                                        c = 2 * p + m
                                        act.wait_ge(tile_read, T + m + 1)
                                        activation(qk[:, c, :], pre[:, m, 0:L], ACT.Identity,
                                                   scale=pcol("mlstm_conv_w_2", l * 4 * NC8 + c),
                                                   bias=pcol("mlstm_conv_b_2", l * NC8 + c)).then_inc(tap0, 1)
                                if ph == "mo":
                                    for m in range(2):
                                        act.wait_ge(tile_read, T + m + 1)
                                        activation(mv[:, 2 * p + m, T0:L], mv[:, 2 * p + m, T0:L], ACT.Tanh,
                                                   scale=0.5).then_inc(gate_act, 1)
                                if ph in ("ag", "mg"):
                                    for m in range(2):
                                        act.wait_ge(tile_read, T + m + 1)
                                        activation(gate_t[:, m, T0:L], gate_x[:, m, T0:L], ACT.Tanh,
                                                   scale=0.5).then_inc(gate_act, 1)
                                    later = (ph, p)
                            for kind, n in [s for s in steps if s[0] != "turn"] + \
                                    [s for s in VISITS[min(u + 1, STREAM_UNITS - 1)] if s[0] == "turn"]:
                                do[kind](n)
                            u += 1
                out_phase(f"proj{l}", (lambda c: pcol("norm_g_2", NC8 + c)) if l == 0 else None, N=L, T0=0,
                          before=lambda: gate_chunks(*later), sq=l == 0)
            for g in range(2):
                act.wait_ge(ot_tr, g + 1)
                nc.scalar.copy(orow[:, g, 0:4 * P], bank[4 + g][:, :]).then_inc(ot_read[g], 1)

        @block.gpsimd
        def _(pool):
            nc.gpsimd.memset(ones[:, :], 1.0)
            nc.gpsimd.memset(epsc[:, :], EPS).then_inc(ones_set, 1)
            TT = nc.gpsimd.tensor_tensor
            chain = [0]

            def link(i_):
                chain[0] += 1
                i_.then_inc(pool_ch, 1)
                pool.wait_ge(pool_ch, chain[0])

            def squares(src, wait, T0, done, chunks=NC8 - 1):
                for c in range(chunks):
                    wait(c)
                    if c == 0:
                        link(TT(sumsq[:, T0:L], src(c), src(c), MUL))
                    else:
                        link(TT(sq[:, T0:L], src(c), src(c), MUL))
                        i_ = TT(sumsq[:, T0:L], sumsq[:, T0:L], sq[:, T0:L], ADD)
                        if c < chunks - 1:
                            link(i_)
                        else:
                            i_.then_inc(done, 1)

            def h_squares(n, name, T0):
                pb = PHASES[name][1]
                if n:
                    pool.wait_ge(sum_done, n + (n == 7))
                squares(lambda c: h[:, c, T0:L], lambda c: pool.wait_ge(tile_read, 2 * pb + c + 1), T0, sq_done)

            def gate_scale(f):
                def turn(i):
                    for m in range(2):
                        pool.wait_ge(silu_done, 22 * f + m + 1 + 2 * i)
                        TT(ffn_r[:, m, :], ffn_s[:, m, :], rstd[:, META:L], MUL).then_inc(gate_scaled, 1)
                with pool.Fori(0, FF // CU) as i:
                    turn(i)

            squares(lambda c: h[:, c, META:L], lambda c: pool.wait_ge(xt_read, c + 1), META, sq_done)
            nc.gpsimd.memset(blocks_a[:, :, :], 0.0)
            nc.gpsimd.memset(blocks_x[:, :, :], 0.0)
            nc.gpsimd.memset(pre[:, :, 0:3], 0.0)
            nc.gpsimd.memset(rec_p[:, :, 0:3], 0.0).then_inc(zero_set, 1)
            gate_scale(0)
            h_squares(1, "out01", META)
            for b in (0, 4):
                for c in range(b, b + 4):
                    pool.wait_ge(gates_sig, 2 * c + 2)
                    TT(rec_x[:, c, :], rec_x[:, c, :], rec_g[:, c, :], MUL).then_inc(gated_in, 1)
                if b:
                    pool.wait_ge(mult2, 4)
                for c in range(b, b + 4):
                    pool.wait_ge(ax_new, c + 1)
                    TT(rec_s[:, c % 4, :], rec_a[:, c, :], rec_a[:, c, :], MUL).then_inc(a2_new, 1)
            h_squares(2, "rec_out", META)
            gate_scale(1)
            h_squares(3, "out02", META)
            gate_scale(2)
            h_squares(4, "out11", META)
            pool.wait_ge(sum_done, 5)
            squares(lambda c: sg_v[:, c, :], lambda c: pool.wait_ge(sg_gelu, c + 1), META, sg_sqs, NC8)
            pool.wait_ge(sg_sum, 1)
            h_squares(5, "sg_out", META)
            pool.wait_ge(tile_read, 2 * PHASES["in12"][1])
            nc.gpsimd.memset(norms[:, :, :], 1.0)
            nc.gpsimd.memset(den_s[:, :, :], 1.0)
            nc.gpsimd.memset(g_tok[:, :, :], 0.0)
            nc.gpsimd.memset(att_s[:, :, :], 0.0)
            pool.wait_ge(sg_loaded, SG_LOADS)
            nc.gpsimd.tensor_scalar(neg_sinks[:, :], sinks[:, :], -1.0, None, MUL)
            nc.gpsimd.tensor_scalar(neg_tail[:, :], sink_tail[:, :], -1.0, None, MUL).then_inc(cleared, 1)
            gate_scale(3)
            h_squares(6, "out12", META)
            pool.wait_ge(fin_sq, 2)
            pool.wait_ge(sum_done, 7)
            link(TT(sumsq[:, 0:L], mv[:, 0, :], mv[:, 1, :], ADD))
            for c in range(2, NC8):
                pool.wait_ge(fin_sq, c + 1)
                i_ = TT(sumsq[:, 0:L], sumsq[:, 0:L], mv[:, c, :], ADD)
                if c < NC8 - 1:
                    link(i_)
            i_.then_inc(fin_sum, 1)
            for l in range(DEPTH):
                I0 = len(ITEMS) * l

                def att(v):
                    if 1 <= v <= len(ITEMS):
                        g, hd = ITEMS[v - 1]
                        n = I0 + v - 1
                        i = (v - 1) % 2
                        pr, rec = prob[:, i, :], att_s[:, 8 + i, :]
                        TS = nc.gpsimd.tensor_scalar
                        pool.wait_ge(s_rec, n + 1)
                        if hd is None:
                            TS(pr[:, P:L], pr[:, P:L], rec[:, 0:1], None, MUL).then_inc(s_prob, 1)
                        else:
                            TS(pr[:, P:AW], pr[:, P:AW], rec[:, 1:2], None, MUL).then_inc(s_prob, 1)

                def turn(c):
                    n = 9 * l + c
                    src = k_att if c == 0 else q[:, c - 1, :]
                    pool.wait_ge(tile_read, 2 * PHASES[f"kv{l}"][1] + 1 if c == 0 else 2 * PHASES[f"aq{l}"][1] + c)
                    if c == 0:
                        pool.wait_ge(cos_ready, l + 1)
                        if l:
                            pool.wait_ge(m_hm, M_H * l)
                    if n >= 2:
                        pool.wait_ge(q_ready, n - 1)
                    TT(qs[:, n % 2, :], src, cst("sin"), MUL)
                    TT(qc[:, n % 2, :], src, cos_g[:, 0 if c else 1, :], MUL).then_inc(qc_new, 1)

                def silu(c):
                    pool.wait_ge(qk_tanh, NC8 * l + c + 1)
                    link(TT(gate_t[:, c % 2, :], gate_t[:, c % 2, :], qk[:, c, :], MUL))
                    TT(qk[:, c, :], qk[:, c, :], gate_t[:, c % 2, :], ADD).then_inc(qk_new, 1)

                for u in range(STREAM_UNITS):
                    for kind, n in VISITS[u]:
                        if kind in ("att", "turn", "silu"):
                            dict(att=att, turn=turn, silu=silu)[kind](n)
                if l == 0:
                    h_squares(7, "proj0", 0)

        @block.vector
        def _(dve):
            V = nc.vector
            TT, TS, STT = V.tensor_tensor, V.tensor_scalar, V.scalar_tensor_tensor
            chain = [0]

            def link(i_):
                chain[0] += 1
                i_.then_inc(dch, 1)
                dve.wait_ge(dch, chain[0])

            def split_w(U, off=0):
                if U >= NU:
                    return
                n, s = UNITS[U][3], U % RING
                dve.wait_ge(hi_made, U + 1 + off)
                TT(w_lo[:, s, 0:n, :], raw[:, s, 0:n, :], w_hi[:, s, 0:n, :].bitcast(fp32), SUB).then_inc(lo_made, 1)

            def ahead(pr):
                for U, _, _ in units_of(pr):
                    split_w(U + LEAD)

            def split_x(dst_lo, dst_hi, k, N, src, count, scale=None):
                dve.wait_ge(act_hi, count + 1)
                hi = xview(dst_hi, k, N).bitcast(fp32)
                if scale is None:
                    i_ = TT(xview(dst_lo, k, N), src, hi, SUB)
                else:
                    i_ = STT(out=xview(dst_lo, k, N), in0=src, scalar=scale, in1=hi, op0=MUL, op1=SUB)
                i_.then_inc(act_ready, 1)

            def inverse(n, T0):
                dve.wait_ge(rms_done, n + 1)
                link(V.reciprocal(rstd[:, T0:L], rms[:, T0:L]))

            def wait_tile(pr, m, off=0):
                if m == 0 and len(units_of(pr)) and pr not in ONE_TILE:
                    dve.wait_ge(first_done, FIRSTS[pr] + 1 + (off // 2 if isinstance(off, int) else 2 * off_i[0]))
                else:
                    dve.wait_ge(unit_done, units_of(pr)[-1][0] + 1 + off)

            off_i = [0]
            ONE_TILE = {PHASES[f"mif{l}"][1] for l in range(DEPTH)}
            FIRSTS = {}
            k_ = 0
            for pr_ in range(len(PAIRS)):
                FIRSTS[pr_] = k_
                k_ += pr_ not in ONE_TILE

            def tile(pr, m, N):
                return bank[(2 * pr + m) % 4][:, 0:N]

            def scaled(pr, m, dst, N, T0, off=0):
                wait_tile(pr, m, off)
                TT(dst, tile(pr, m, N), rstd[:, T0:L], MUL).then_inc(tile_read, 1)

            def gate_turn(pb, ub, i, f, count, first=None):
                o = 4 * i
                off_i[0] = i
                for U in (ub, ub + 1):
                    split_w(U + LEAD, o)
                if first is not None:
                    inverse(first, META)
                for m in range(2):
                    scaled(pb, m, ffn_t[:, m, :], SEQ, META, o)
                for U in (ub + 2, ub + 3):
                    split_w(U + LEAD, o)
                for m in range(2):
                    wait_tile(pb + 1, m, o)
                    dve.wait_ge(gate_scaled, 22 * f + m + 1 + 2 * i)
                    TT(ffn_h[:, m, :], tile(pb + 1, m, SEQ), ffn_r[:, m, :], MUL).then_inc(tile_read, 1)
                for m in range(2):
                    dve.wait_ge(act_hi, count + m + 1 + 2 * i)
                    if isinstance(i, int):
                        lo, hi = (xview(t, 2 * i + m, SEQ) for t in (y_lo, y_hi))
                    else:
                        lo, hi = (t[:, bass.ds(i * (2 * SEQ) + m * SEQ, SEQ)] for t in (y_lo, y_hi))
                    TT(lo, ffn_h[:, m, :], hi.bitcast(fp32), SUB).then_inc(act_ready, 1)

            def in_phase(name, f, n, count):
                ub, pb, _ = PHASES[name]
                gate_turn(pb, ub, 0, f, count, first=n)
                if name == "in01":
                    parameters()
                with dve.Fori(1, FF // CU) as i:
                    gate_turn(pb, ub, i, f, count)

            def out_phase(name, g, count, half=0.5, N=SEQ, T0=META, before=None):
                ub, pb, npairs = PHASES[name]
                for p in range(npairs):
                    for U, _, _ in units_of(pb + p):
                        split_w(U + LEAD)
                        if before is not None:
                            before()
                            before = None
                    for m in range(2):
                        c = 2 * p + m
                        wait_tile(pb + p, m)
                        STT(out=h[:, c, T0:L], in0=tile(pb + p, m, N), scalar=half, in1=h[:, c, T0:L], op0=MUL,
                            op1=ADD).then_inc(tile_read, 1)
                        if g is not None:
                            split_x(x_lo, x_hi, c, N, h[:, c, T0:L], count + c, g(c))

            dve.wait_ge(par_t, 1)
            V.tensor_copy(par[:, 0, 0:16], bank[0][:, 0:16]).then_inc(par_ready, 1)
            dve.wait_ge(par_ready, 1)
            for c in range(NC8 + 1):
                if c < NC8:
                    dve.wait_ge(xt_done, c + 1)
                    V.tensor_copy(h[:, c, :], bank[4 + c % 4][:, 0:L]).then_inc(xt_read, 1)
                if c:
                    dve.wait_ge(xt_read, c)
                    split_x(x_lo, x_hi, c - 1, SEQ, h[:, c - 1, META:L], c - 1, pcol("ffn1_norm", c - 1))
                if c == 3:
                    split_w(0)
            split_w(1)
            split_w(2)

            def parameters():
                rows1 = sum(k for (t, _, k) in PAR.values() if t == 1)
                dve.wait_ge(par_t, 2)
                V.tensor_copy(par[:, 0, 16:P], bank[5][:, 16:P])
                V.tensor_copy(par[:, 1, 0:rows1], bank[5][:, P:P + rows1]).then_inc(par_ready, 1)
                dve.wait_ge(par_ready, 2)

            lam_t, lam_r, _ = PAR["rec_lambda"]
            lam = par[:, lam_t, lam_r:lam_r + NC8]
            def log1p(dst, e, t0, t1, t2, part=None):
                if part in (None, 0):
                    link(TS(t0, e, 2.0, None, ADD))
                    link(V.reciprocal(t1, t0))
                    link(TT(t0, e, t1, MUL))
                    link(TT(t1, t0, t0, MUL))
                    link(TS(t2, t1, 1.0 / 17, None, MUL))
                for k in {None: (15, 13, 11, 9, 7, 5, 3), 0: (), 1: (15, 13, 11, 9), 2: (7, 5, 3)}[part]:
                    link(STT(out=t2, in0=t2, scalar=1.0 / k, in1=t1, op0=ADD, op1=MUL))
                if part in (None, 2):
                    link(STT(out=t2, in0=t2, scalar=1.0, in1=t0, op0=ADD, op1=MUL))
                    link(TS(dst, t2, 2.0, None, MUL))

            in_phase("in01", 0, 0, SPLITS["y_out01"])
            link(STT(out=decay[:, 0, :], in0=lam, scalar=-1.0, in1=lam, op0=MUL, op1=MIN))
            V.tensor_copy(decay[:, 11, :], decay[:, 0, :]).then_inc(decay_v, 1)
            dve.wait_ge(decay_e, 1)
            log1p(decay[:, 4, :], decay[:, 1, :], decay[:, 5, :], decay[:, 6, :], decay[:, 7, :])
            link(TS(decay[:, 8, :], lam, -1.0, 0.0, MUL, MAX))
            link(TT(decay[:, 9, :], decay[:, 8, :], decay[:, 4, :], ADD))
            TS(decay[:, 2, :], decay[:, 9, :], -8.0, None, MUL)
            TS(decay[:, 3, :], decay[:, 9, :], 8.0, None, MUL).then_inc(decay_v, 1)
            out_phase("out01", lambda c: pcol("mix_norm", c), SPLITS["x_rec_b"])

            pb = PHASES["rec_b"][1]

            def conv1(p):
                for k in range(4):
                    for c in (2 * p, 2 * p + 1):
                        src, w = rec_p[:, c, k:k + SEQ], pcol("rec_conv_w", k * NC8 + c)
                        if k == 0:
                            i_ = TS(rec_x[:, c, :], src, w, pcol("rec_conv_b", c), MUL, ADD)
                        else:
                            i_ = STT(out=rec_x[:, c, :], in0=src, scalar=w, in1=rec_x[:, c, :], op0=MUL, op1=ADD)
                        if k == 3:
                            i_.then_inc(conv_new, 1)
                    if k < 3:
                        link(i_)

            def mult_squares(cs):
                for c in cs:
                    dve.wait_ge(a2_new, c + 1)
                    dve.wait_ge(conv_new, c + 1)
                    STT(out=rec_p[:, c, 0:SEQ], in0=rec_s[:, c % 4, :], scalar=1.0, in1=rec_t[:, c % 4, :], op0=ADD,
                        op1=MUL).then_inc(mult2, 1)

            def scans(cs):
                for c in cs:
                    dve.wait_ge(mult_new, c // 4 + 1)
                    dve.wait_ge(gated_in, c + 1)
                    TT(rec_x[:, c, :], rec_x[:, c, :], rec_p[:, c, 0:SEQ], MUL).then_inc(rec_bx, 1)
                for c in cs:
                    dve.wait_ge(rec_bx, c + 1)
                    V.tensor_tensor_scan(rec_g[:, c, :], rec_a[:, c, :], rec_x[:, c, :], 0.0, MUL, ADD).then_inc(scanned, 1)

            def outputs(cs):
                for c in cs:
                    dve.wait_ge(scanned, c + 1)
                    dve.wait_ge(rec_gelu, c + 1)
                    TT(rec_y[:, c, :], rec_y[:, c, :], rec_g[:, c, :], MUL).then_inc(act_new, 1)

            def lower(cs):
                for c in cs:
                    split_x(y_lo, y_hi, c, SEQ, rec_y[:, c, :], SPLITS["y_rec_out"] + c)

            r = 0
            for p in range(8):
                for j, (U, _, _) in enumerate(units_of(pb + p)):
                    if r == 9:
                        mult_squares(range(4))
                    if r == 12:
                        mult_squares(range(4, 8))
                    if r == 14:
                        outputs(range(4))
                    if r == 15:
                        outputs(range(4, 6))
                    split_w(U + LEAD)
                    if r == 1:
                        inverse(1, META)
                    if r == 12:
                        scans(range(4))
                    if r == 13:
                        scans(range(4, 6))
                    if r == 14:
                        lower(range(4))
                        scans(range(6, 8))
                    if j == 1:
                        for m in range(2):
                            c = 2 * (p % 4) + m
                            scaled(pb + p, m, rec_p[:, c, 3:3 + SEQ] if p < 4 else rec_y[:, c, :], SEQ, META)
                        if p < 4:
                            dve.wait_ge(tile_read, 2 * (pb + p) + 2)
                            conv1(p)
                    r += 1
            lower(range(4, 6))
            outputs(range(6, 8))
            lower(range(6, 8))
            out_phase("rec_out", lambda c: pcol("ffn2_norm", c), SPLITS["x_in02"], half=1.0)

            in_phase("in02", 1, 2, SPLITS["y_out02"])
            out_phase("out02", lambda c: pcol("ffn1_norm", NC8 + c), SPLITS["x_in11"])
            in_phase("in11", 2, 3, SPLITS["y_out11"])
            out_phase("out11", lambda c: pcol("mix_norm", NC8 + c), SPLITS["x_sg_b"])

            _, pb, _ = PHASES["sg_b"]
            for p in range(4):
                ahead(pb + p)
                if p == 0:
                    inverse(4, META)
                for m in range(2):
                    scaled(pb + p, m, sg_v[:, 2 * p + m, :], SEQ, META)
                if p == 1:
                    dve.wait_ge(ws_tr, 1)
                    for c in range(NC8):
                        i_ = TT(ws_t[:, c, :], bank[5 + c // 4][:, (c % 4) * P:(c % 4 + 1) * P], tri, MUL)
                        if c % 4 == 3:
                            i_.then_inc(ws_read, 1)
            _, pb, _ = PHASES["sg_a"]
            ahead(pb)
            for m in range(2):
                scaled(pb, m, sg_u[:, m, :], SEQ, META)
            dve.wait_ge(sg_rms, 1)
            link(V.reciprocal(sg_r[:, 1, :], sg_r[:, 0, :]))
            for g in range(4):
                t, c0 = g // 2, 4 * (g % 2)
                dve.wait_ge(vt_tr, g + 1)
                TS(v_tok[:, t, c0 * P:(c0 + 4) * P], bank[5 + g % 3][:, :], sg_r[:, 1, t:t + 1], None, MUL).then_inc(vt_read, 1)
            ahead(pb + 1)
            for m in range(2):
                scaled(pb + 1, m, sg_u[:, 2 + m, :], SEQ, META)
            for c in range(NC8):
                dve.wait_ge(sg_mm, c + 1)
                for t in range(2):
                    i_ = STT(out=sg_s[:, c, t * P:(t + 1) * P], in0=bank[4 + c % 4][:, t * P:(t + 1) * P],
                             scalar=pcol("sg_v_norm", c), in1=bs_all[:, c, :], op0=MUL, op1=ADD)
                i_.then_inc(sg_read, 1)
            def outputs2(cs):
                for c in cs:
                    dve.wait_ge(sg_gelu, NC8 + c + 1)
                    TT(sg_s[:, c, :], sg_s[:, c, :], sg_u[:, c, :], MUL).then_inc(act_new, 1)
                for c in cs:
                    split_x(y_lo, y_hi, c, SEQ, sg_s[:, c, :], SPLITS["y_sg_out"] + c)

            for p in (2, 3):
                ahead(pb + p)
                if p == 3:
                    dve.wait_ge(sg_read, NC8)
                    outputs2(range(4))
                for m in range(2):
                    scaled(pb + p, m, sg_u[:, 2 * p + m, :], SEQ, META)
            outputs2(range(4, 6))
            outputs2(range(6, 8))
            out_phase("sg_out", lambda c: pcol("ffn2_norm", NC8 + c), SPLITS["x_in12"], half=1.0)

            in_phase("in12", 3, 5, SPLITS["y_out12"])
            out_phase("out12", None, 0)
            inverse(6, META)
            dve.wait_ge(cleared, 1)
            for c in range(NC8 + 1):
                if c < NC8:
                    STT(out=h[:, c, META:L], in0=h[:, c, META:L], scalar=pcol("final_norm", c), in1=rstd[:, META:L], op0=MUL,
                        op1=MUL).then_inc(final_new, 1)
                if c:
                    dve.wait_ge(final_new, c)
                    split_x(x_lo, x_hi, c - 1, L, h[:, c - 1, :], SPLITS["x_kv0"] + c - 1, pcol("norm_g_2", c - 1))

            def rsqrt(y, x, t):
                i32 = mybir.dt.int32
                link(TS(y.bitcast(i32), x.bitcast(i32), 1, None, ALU.logical_shift_right))
                link(TS(y.bitcast(i32), y.bitcast(i32), -1, 0x5F3759DF, MUL, ADD))
                for _ in range(3):
                    link(TT(t, y, y, MUL))
                    link(STT(out=t, in0=t, scalar=-0.5, in1=x, op0=MUL, op1=MUL))
                    link(STT(out=y, in0=t, scalar=1.5, in1=y, op0=ADD, op1=MUL))

            for l in range(DEPTH):
                I0 = len(ITEMS) * l
                narrow = l == DEPTH - 1
                T0 = META if narrow else 0

                def tables():
                    gq, gk = pcol("attn_q_norm_g_2", l), pcol("attn_k_norm_g_2", l)
                    sc = DH ** -0.5
                    if l:
                        dve.wait_ge(m_hm, M_H * l)
                    TS(cos_g[:, 0, :], cst("cos"), gq, sc, MUL, MUL)
                    TS(cos_g[:, 1, :], cst("cos"), gk, None, MUL)
                    TS(rot_g[:, 0, :], cst("rot"), gq, sc, MUL, MUL)
                    TS(rot_g[:, 1, :], cst("rot"), gk, None, MUL).then_inc(cos_ready, 1)

                def gates_in(pr):
                    wait_tile(pr, 1)
                    b0 = bank[(2 * pr) % 4]
                    if l:
                        dve.wait_ge(m_hm, M_H * l)
                    TT(g_row[0:4, 3, :], b0[0:4, 0:L], rstd[0:4, :], MUL)
                    link(TT(g_row[0:4, 0, :], b0[32:36, 0:L], rstd[32:36, :], MUL))
                    TS(g_row[0:4, 3, :], g_row[0:4, 3, :], gbias[:, l:l + 1], None, ADD)
                    link(TS(g_row[0:4, 0, :], g_row[0:4, 0, :], gbias[:, DEPTH + l:DEPTH + l + 1], None, ADD))
                    V.tensor_copy(g_row[0:1, 4, 0:1], g_row[0:1, 0, 0:1]).then_inc(tile_read, 2)
                    STT(out=g_row[0:4, 1, :], in0=g_row[0:4, 0, :], scalar=-1.0, in1=g_row[0:4, 0, :], op0=MUL,
                        op1=MIN).then_inc(g_nx, 1)

                def forget_rows(part):
                    if part < 3:
                        if part == 0:
                            dve.wait_ge(g_e, l + 1)
                        log1p(g_row[0:4, 5, :], g_row[0:4, 2, :], g_row[0:4, 1, :], exp_b[0:4, :], m_b[0:4, :], part)
                        return
                    link(STT(out=g_row[0:4, 1, :], in0=g_row[0:4, 0, :], scalar=0.0, in1=g_row[0:4, 5, :], op0=MIN, op1=SUB))
                    link(V.memset(g_row[0:4, 0, :], 1.0))
                    link(V.tensor_tensor_scan(g_row[0:4, 2, :], g_row[0:4, 0, :], g_row[0:4, 1, :], 0.0, MUL, ADD))
                    link(TT(g_row[0:4, 3, :], g_row[0:4, 3, :], g_row[0:4, 2, :], SUB))
                    link(V.tensor_tensor_scan(g_row[0:4, 4, :], g_row[0:4, 3, :], g_row[0:4, 3, :], 0.0, MAX, MAX))
                    link(TT(g_row[0:4, 5, :], g_row[0:4, 2, :], g_row[0:4, 4, :], ADD))
                    TS(g_row[0:4, 5, :], g_row[0:4, 5, :], M_MIN, None, MAX).then_inc(g_cm, 1)

                def rs():
                    dve.wait_ge(turn_mm, 9 * (l + 1))
                    W = 2 * NR
                    TS(norms[:, 0, 0:W], bank[4][:, 0:W], EPS, None, ADD)
                    link(TS(norms[0:TAIL, 0, W:W + NR], bank[4][0:TAIL, W:W + NR], EPS, None, ADD))
                    rsqrt(norms[:, 3, :], norms[:, 0, :], norms[:, 1, :])
                    TS(norms[:, 2, :], norms[:, 3, :], -1.0, None, MUL).then_inc(rs_new, 1)

                def turn(c):
                    n = 9 * l + c
                    dst = k_att if c == 0 else q[:, c - 1, :]
                    dve.wait_ge(turn_mm, n + 1)
                    TT(dst, bank[5 + n % 2][:, 0:L], qc[:, n % 2, :], ADD).then_inc(q_ready, 1)

                def rt():
                    dve.wait_ge(rt_mm, 2 * l + 2)
                    TT(k_att, k_att, bank[6][:, 0:L], MUL).then_inc(k_ready, 1)
                    for g in range(2):
                        for e in range(2):
                            i_ = TT(q_tail[g * DH:(g + 1) * DH, g, e * DH:(e + 1) * DH].rearrange("p (c t) -> p c t", t=TAIL),
                                    q[e * DH:(e + 1) * DH, 4 * g:4 * g + 4, 2 * P:L],
                                    bank[7][e * DH:(e + 1) * DH, 4 * g * TAIL:4 * (g + 1) * TAIL].rearrange(
                                        "p (c t) -> p c t", t=TAIL), MUL)
                        i_.then_inc(tail_new, 1)

                def kx():
                    dve.wait_ge(kx_mm, l + 1)
                    V.tensor_copy(va_t[:, 0:2, :], bank[5][:, 0:2 * P].rearrange("p (t n) -> p t n", n=P))
                    V.tensor_copy(va_t[0:TAIL, 2, :], bank[5][0:TAIL, 2 * P:3 * P])
                    V.tensor_copy(g_tok[:, 0:2, :], bank[5][:, 3 * P:3 * P + 16].rearrange("p (t n) -> p t n", n=8))
                    V.tensor_copy(g_tok[0:TAIL, 2, :], bank[5][0:TAIL, 3 * P + 16:3 * P + 24]).then_inc(kx_read, 1)

                def att(v):
                    if v < len(ITEMS):
                        g, hd = ITEMS[v]
                        n = I0 + v
                        i = v % 2
                        s, mx, nm = score[:, i, :], att_s[:, 3 * i, :], att_s[:, 3 * i + 1, :]
                        dve.wait_ge(s_mm, n + 1)
                        if v >= 2:
                            dve.wait_ge(s_exp, n - 1)
                        if hd is None:
                            link(V.tensor_tensor_reduce(s[:, 0:L], bank[4][:, 0:L], cst("tmask"), 1.0, NEG, ADD, MAX, mx[:, 0:1]))
                            TS(nm[:, 0:1], mx[:, 0:1], -1.0, neg_tail[:, 2 * l + g:2 * l + g + 1], MUL, MIN).then_inc(s_max, 1)
                        else:
                            am = cst("amask")
                            V.tensor_tensor_reduce(s[:, 0:P], bank[4][:, 0:P], am[:, 0:P], 1.0, NEG, ADD, MAX, mx[:, 0:1])
                            link(V.tensor_tensor_reduce(s[:, P:AW], bank[4][:, P:AW], am[:, P:AW], 1.0, NEG, ADD, MAX,
                                                        mx[:, 1:2]))
                            for t in range(2):
                                at = NR * t + 2 + hd
                                i_ = TS(nm[:, t:t + 1], mx[:, t:t + 1], norms[:, 2, at:at + 1],
                                        neg_sinks[:, l * ATT_H + hd:l * ATT_H + hd + 1], MUL, MIN)
                            i_.then_inc(s_max, 1)
                    if v >= 3:
                        g, hd = ITEMS[v - 3]
                        n = I0 + v - 3
                        if hd is None:
                            dve.wait_ge(s_pv, n + 1)
                            V.tensor_copy(q[:, 4 * g:4 * g + 4, 2 * P:L],
                                          bank[7][:, 0:DH].rearrange("p (c t) -> p c t", t=TAIL)).then_inc(s_out, 1)
                        elif hd % 2:
                            dve.wait_ge(s_pv, n + 1)
                            V.tensor_copy(q[:, hd // 2, 0:2 * P], bank[7][:, 0:2 * P]).then_inc(s_out, 1)

                def att_later(v):
                    if v < len(ITEMS):
                        i = v % 2
                        dve.wait_ge(s_exp, I0 + v + 1)
                        link(TT(att_s[:, 10 + i, 0:2], att_s[:, 3 * i + 2, 0:2], att_s[:, 6 + i, 0:2], ADD))
                        V.reciprocal(att_s[:, 8 + i, 0:2], att_s[:, 10 + i, 0:2]).then_inc(s_rec, 1)
                        dve.wait_ge(s_rec, I0 + v + 1)
                        pr = prob[:, i, 0:P]
                        TS(pr, pr, att_s[:, 8 + i, 0:1], None, MUL).then_inc(s_prob0, 1)

                def conv(p):
                    for k in range(1, 4):
                        for m in range(2):
                            c = 2 * p + m
                            w = pcol("mlstm_conv_w_2", (l * 4 + k) * NC8 + c)
                            if k == 1:
                                dve.wait_ge(tap0, NC8 * l + c + 1)
                            i_ = STT(out=qk[:, c, :], in0=pre[:, m, k:k + L], scalar=w, in1=qk[:, c, :], op0=MUL, op1=ADD)
                            if k == 3:
                                i_.then_inc(conv2_new, 1)
                        if k < 3:
                            link(i_)

                def ml(hd, stage):
                    n = M_H * l + hd
                    if stage == 0:
                        dve.wait_ge(m_bc, n + 1)
                        if n:
                            dve.wait_ge(m_pt_new, n)
                        for t, (a, b) in enumerate(LT):
                            i_ = TT(m_arg[0:b - a, MOFF[t]:MOFF[t] + b - a], bank[4][0:b - a, a:b],
                                    con[0:b - a, CONST_AT["mmask"]:CONST_AT["mmask"] + b - a], ADD)
                        i_.then_inc(m_arg_new, 1)

                def ml_later(hd, stage):
                    n = M_H * l + hd
                    small = ((slice(0, P), slice(0, 2)), (slice(0, TAIL), slice(2, 3)))
                    if stage == 0:
                        dve.wait_ge(m_qk, n + 1)
                        dve.wait_ge(m_exp_new, n + 1)
                        if n:
                            dve.wait_ge(m_num, n)
                        W01 = MOFF[2]
                        STT(out=m_pt[:, 0:W01], in0=bank[5][:, 0:W01], scalar=0.25 * QK_D ** -0.5, in1=m_arg[:, 0:W01], op0=MUL,
                            op1=MUL)
                        STT(out=m_pt[0:TAIL, W01:MW], in0=bank[5][0:TAIL, W01:MW], scalar=0.25 * QK_D ** -0.5,
                            in1=m_arg[0:TAIL, W01:MW], op0=MUL, op1=MUL).then_inc(m_pt_new, 1)
                    if stage == 1:
                        dve.wait_ge(m_num, n + 1)
                        for r, c in small:
                            i_ = TS(den_s[r, 0, c], bank[4][r, 400 + c.start:400 + c.stop], -1.0, None, MUL)
                        link(i_)
                        for r, c in small:
                            i_ = TT(den_s[r, 0, c], bank[4][r, 400 + c.start:400 + c.stop], den_s[r, 0, c], MAX)
                        i_.then_inc(m_den, 1)
                        dve.wait_ge(m_den, n + 1)
                        link(TT(den_s[:, 0, 0:3], den_s[:, 0, 0:3], g_tok[:, :, 4 + hd], MAX))
                        link(STT(out=den_s[:, 1, 0:3], in0=den_s[:, 0, 0:3], scalar=EPS, in1=den_s[:, 0, 0:3], op0=MUL, op1=MUL))
                    if stage == 2:
                        dve.wait_ge(m_ms, n + 1)
                        for r, c in small:
                            i_ = STT(out=den_s[r, 2, c], in0=bank[4][r, 408 + c.start:408 + c.stop], scalar=1.0 / 256,
                                     in1=den_s[r, 1, c], op0=MUL, op1=ADD)
                        i_.then_inc(ms_read, 1)
                        dve.wait_ge(ms_read, n + 1)
                        rsqrt(den_s[:, 5, 0:3], den_s[:, 2, 0:3], den_s[:, 4, 0:3])
                        if n:
                            dve.wait_ge(m_bb, n)
                        for j, (a, b) in enumerate(LT):
                            i_ = TS(diag[0:b - a, j, 0:b - a], ident[0:b - a, 0:b - a], den_s[0:b - a, 5, j:j + 1], 0.25,
                                    MUL, MUL)
                        i_.then_inc(m_diag, 1)
                    if stage == 3:
                        dve.wait_ge(m_sb, n + 1)
                        for w in range(2):
                            c = 2 * hd + w
                            t = g_x2[:, w, :]
                            i_ = STT(out=t, in0=bank[6 + w][:, 0:L], scalar=pcol("mlstm_out_norm_g_2", l * NC8 + c),
                                     in1=s_b, op0=MUL, op1=MUL)
                        link(i_)
                        for w in range(2):
                            c = 2 * hd + w
                            dve.wait_ge(gate_act, G0 + c + 1)
                            i_ = STT(out=mv[:, c, T0:L], in0=mv[:, c, T0:L], scalar=1.0, in1=g_x2[:, w, T0:L], op0=ADD,
                                     op1=MUL)
                        i_.then_inc(m_hm, 1)

                G0 = 24 * l

                def gated(ph, p):
                    g = 1 if ph == "ag" else 2
                    for m in range(2):
                        dve.wait_ge(gate_act, G0 + 8 * g + 2 * p + m + 1)
                        i_ = STT(out=gate_x[:, m, T0:L], in0=gate_t[:, m, T0:L], scalar=1.0, in1=gate_x[:, m, T0:L], op0=ADD,
                                 op1=MUL)
                    link(i_)
                    for m in range(2):
                        c = 2 * p + m
                        if ph == "ag":
                            if m == 0:
                                dve.wait_ge(s_out, 10 * (l + 1))
                            i_ = STT(out=q[:, c, T0:L], in0=gate_x[:, m, T0:L], scalar=0.5, in1=q[:, c, T0:L], op0=MUL,
                                     op1=MUL)
                        else:
                            if m == 0:
                                dve.wait_ge(m_hm, M_H * l + p + 1)
                            i_ = TT(mv[:, c, T0:L], mv[:, c, T0:L], gate_x[:, m, T0:L], MUL)
                        i_.then_inc(act_new, 1)

                def gated_lo(ph, p):
                    for m in range(2):
                        c = 2 * p + m
                        k = c if ph == "ag" else NC8 + c
                        dve.wait_ge(act_hi, SPLITS[f"y_proj{l}"] + k + 1)
                        cols = slice(k * L + T0, (k + 1) * L)
                        src = q if ph == "ag" else mv
                        TT(y_lo[:, cols], src[:, c, T0:L], y_hi[:, cols].bitcast(fp32), SUB).then_inc(act_ready, 1)

                def nothing(n):
                    return None

                do = dict(turn=turn, rs=lambda n: rs(), rt=lambda n: rt() if n else None, kx=lambda n: kx(), att=att,
                          silu=nothing, mvt=nothing, ml=lambda hs: ml(*hs))
                do_later = dict(att=att_later, ml=lambda hs: ml_later(*hs))
                def tiles(ph, p, pr):
                    if ph == "kv":
                        scaled(pr, 0, k_att, L, 0)
                        scaled(pr, 1, v_att, L, 0)
                        tables()
                    if ph == "mif":
                        gates_in(pr)
                    if ph == "aq":
                        for m in range(2):
                            scaled(pr, m, q[:, 2 * p + m, T0:L], L - T0, T0)
                        forget_rows(p)
                    if ph == "mqk":
                        for m in range(2):
                            if p:
                                dve.wait_ge(conv2_new, NC8 * l + 2 * p)
                            scaled(pr, m, pre[:, m, 3:3 + L], L, 0)
                    if ph == "mv":
                        for m in range(2):
                            scaled(pr, m, mv[:, 2 * p + m, :], L, 0)
                    if ph == "mo":
                        for m in range(2):
                            dve.wait_ge(mt_tr, NC8 * l + 2 * p + m + 1)
                            scaled(pr, m, mv[:, 2 * p + m, T0:L], L - T0, T0)
                    if ph in ("ag", "mg"):
                        for m in range(2):
                            scaled(pr, m, gate_x[:, m, T0:L], L - T0, T0)

                def attention_unit(U, ph, p, j, pr, steps):
                    if j == 1:
                        tiles(ph, p, pr)
                    split = False
                    for kind, n in steps:
                        do[kind](n)
                        if not split:
                            split_w(U + LEAD)
                            split = True
                        if kind == "att":
                            att_later(n)
                            if j == 1 and ph == "mqk":
                                conv(p)
                    return [s_ for s_ in steps if s_[0] == "ml"]

                u = 0
                later, gate_later = [], None
                for ph in STREAM:
                    pb = PHASES[f"{ph}{l}"][1]
                    for p in range(PHASES[f"{ph}{l}"][2]):
                        pr = pb + p
                        for j, (U, _, _) in enumerate(units_of(pr)):
                            for kind, n in later:
                                do_later[kind](n)
                            later = []
                            steps = VISITS[u]
                            if any(k == "att" for k, _ in steps):
                                later = attention_unit(U, ph, p, j, pr, [s_ for s_ in steps if do[s_[0]] != nothing])
                                u += 1
                                continue
                            if len(steps) == 1 and steps[0][0] == "ml" and steps[0][1][1] == 0:
                                kind, n = steps[0]
                                do[kind](n)
                                later = [steps[0]]
                                steps = steps[1:]
                            if gate_later:
                                gated(*gate_later)
                            split_w(U + LEAD)
                            if gate_later:
                                gated_lo(*gate_later)
                                gate_later = None
                            if u == 1 and l == 0 or u == 0 and l == 1:
                                inverse(7 + l, 0)
                            if j == 1:
                                tiles(ph, p, pr)
                                if ph == "mqk":
                                    conv(p)
                                if ph in ("ag", "mg"):
                                    gate_later = (ph, p)
                            for kind, n in steps:
                                for k_, n_ in later:
                                    do_later[k_](n_)
                                later = [(kind, n)] if kind in do_later else []
                                do[kind](n)
                            u += 1

                def rest():
                    for kind, n in later:
                        do_later[kind](n)
                    gated(*gate_later)
                    gated_lo(*gate_later)

                out_phase(f"proj{l}", (lambda c: pcol("norm_g_2", NC8 + c)) if l == 0 else None,
                          SPLITS.get("x_kv1"), half=1.0, N=L - T0, T0=T0, before=rest)
            for g in (2, 3):
                c0, n, _ = OUT_GROUPS[g]
                dve.wait_ge(ot_tr, g + 1)
                V.tensor_copy(orow[:, :, c0 * P:(c0 + n) * P],
                              bank[4 + g][:, :].rearrange("p (t n) -> p t n", t=2)).then_inc(ot_read[g], 1)


_INS = ['x', 'ffn1_norm', 'ffn1_w_in', 'ffn1_w_out', 'mix_norm', 'ffn2_norm', 'ffn2_w_in', 'ffn2_w_out', 'rec_w_in',
        'rec_conv_w', 'rec_conv_b', 'rec_gate_a_w', 'rec_gate_a_b', 'rec_gate_x_w', 'rec_gate_x_b', 'rec_lambda',
        'rec_w_out', 'sg_w_in', 'sg_v_norm', 'sg_w_s', 'sg_b_s', 'sg_w_out', 'final_norm', 'meta_2', 'norm_g_2',
        'w_in_2', 'attn_q_norm_g_2', 'attn_k_norm_g_2', 'attn_sink_2', 'mlstm_conv_w_2', 'mlstm_conv_b_2',
        'mlstm_b_i_2', 'mlstm_b_f_2', 'mlstm_out_norm_g_2', 'w_out_2']
_OUTS = [((1, SEQ, D), 'float32')]


def kernel(**inputs):
    import numpy as _np
    import concourse.bacc as _bacc
    from concourse import mybir as _mybir
    from concourse.bass_utils import run_bass_kernel_spmd as _run

    nc = _bacc.Bacc("TRN2", target_bir_lowering=False, num_devices=1)
    arrays = {"in_consts_dram": constants()}
    for name in _INS:
        arrays[f"in_{name}_dram"] = _np.ascontiguousarray(inputs[name])
    args = [nc.dram_tensor(n, a.shape, _mybir.dt.from_np(a.dtype), kind="ExternalInput").ap() for n, a in arrays.items()]
    for i, (shape, dtype) in enumerate(_OUTS):
        args.append(nc.dram_tensor(f"out_{i}_dram", shape, _mybir.dt.from_np(_np.dtype(dtype)), kind="ExternalOutput").ap())
    build_stack(nc, *args)
    r = _run(nc, [arrays], core_ids=[0])
    return r.results[0]["out_0_dram"]
```
